# Optimizing a Trainium2 kernel written in Bass

```python
import jax, jax.numpy as jnp
from jax import lax
import numpy as np

D_MODEL = 1024
BATCH = 1
SEQ = 1024
DEPTH = 1

HEAD_DIM = 64
N_Q_HEADS = 8
N_KV_HEADS = 2
Q_PER_KV = N_Q_HEADS // N_KV_HEADS
ATTN_WIDTH = N_Q_HEADS * HEAD_DIM
KV_WIDTH = N_KV_HEADS * HEAD_DIM
WINDOW = 128
ATTN_BLOCK = WINDOW
CONV_WIDTH = D_MODEL // 2
CONV_KERNEL = 31
MIX_WIDTH = ATTN_WIDTH + CONV_WIDTH
IN_WIDTH = ATTN_WIDTH + 2 * KV_WIDTH + 2 * CONV_WIDTH
N_EXPERTS = 32
TOP_K = 4
D_EXPERT = D_MODEL
SWIGLU_LIMIT = 7.0
SWIGLU_ALPHA = 1.702
EXPERT_BLOCK = 128
RMS_EPS = 1e-5
LN_EPS = 1e-5

kernel_name = "hymba_conformer_swa_sink_moe"

def rms_norm(x, g):
    xf = x.astype(jnp.float32)
    y = xf * lax.rsqrt(jnp.mean(xf * xf, axis=-1, keepdims=True) + RMS_EPS)
    return (y * g.astype(jnp.float32)).astype(x.dtype)

def layer_norm(x, g, b):
    xf = x.astype(jnp.float32)
    mu = jnp.mean(xf, axis=-1, keepdims=True)
    xc = xf - mu
    y = xc * lax.rsqrt(jnp.mean(xc * xc, axis=-1, keepdims=True) + LN_EPS)
    return (y * g.astype(jnp.float32) + b.astype(jnp.float32)).astype(x.dtype)

def sliding_window_attention_with_sinks(q, k, v, sinks):
    b, s, _ = q.shape
    L = ATTN_BLOCK
    nb = s // L
    q = q.reshape(b, nb, L, N_KV_HEADS, Q_PER_KV, HEAD_DIM)
    k = k.reshape(b, nb, L, N_KV_HEADS, HEAD_DIM)
    v = v.reshape(b, nb, L, N_KV_HEADS, HEAD_DIM)

    def band(t):
        prev = jnp.concatenate([jnp.zeros_like(t[:, :1]), t[:, :-1]], axis=1)
        return jnp.concatenate([prev, t], axis=2)

    kb, vb = band(k), band(v)
    scores = jnp.einsum('bnqhgd,bnkhd->bnhgqk', q, kb).astype(jnp.float32) * (HEAD_DIM ** -0.5)
    blk = jnp.arange(nb)[:, None, None]
    q_pos = blk * L + jnp.arange(L)[None, :, None]
    k_pos = (blk - 1) * L + jnp.arange(2 * L)[None, None, :]
    valid = (k_pos <= q_pos) & (q_pos - k_pos < WINDOW) & (k_pos >= 0)
    scores = jnp.where(valid[None, :, None, None], scores, -jnp.inf)
    sink = sinks.astype(jnp.float32).reshape(1, 1, N_KV_HEADS, Q_PER_KV, 1, 1)
    sink = jnp.broadcast_to(sink, scores.shape[:-1] + (1,))
    probs = jax.nn.softmax(jnp.concatenate([scores, sink], axis=-1), axis=-1)[..., :-1]
    out = jnp.einsum('bnhgqk,bnkhd->bnqhgd', probs.astype(v.dtype), vb)
    return out.reshape(b, s, ATTN_WIDTH)

def conformer_conv(a, gate, w_dw, b_dw, ln_g, ln_b):
    u = a * jax.nn.sigmoid(gate)
    u = lax.conv_general_dilated(
        u, w_dw[:, None, :].astype(u.dtype), window_strides=(1,),
        padding=[(CONV_KERNEL - 1, 0)],
        dimension_numbers=('NWC', 'WIO', 'NWC'),
        feature_group_count=CONV_WIDTH) + b_dw
    u = layer_norm(u, ln_g, ln_b)
    return jax.nn.silu(u)

def moe_ffn(h, w_router, b_router, w1, b1, w2, b2):
    bsz, s, d = h.shape
    t = bsz * s
    xt = h.reshape(t, d)
    logits = (xt @ w_router + b_router).astype(jnp.float32)
    top_val, top_idx = lax.top_k(logits, TOP_K)
    gates = jax.nn.softmax(top_val, axis=-1)
    n_assign = t * TOP_K
    e_flat = top_idx.reshape(n_assign).astype(jnp.int32)
    tok_flat = jnp.arange(n_assign, dtype=jnp.int32) // TOP_K
    g_flat = gates.reshape(n_assign)
    order = jnp.argsort(e_flat, stable=True)
    e_s, tok_s, g_s = e_flat[order], tok_flat[order], g_flat[order]
    counts = jnp.bincount(e_flat, length=N_EXPERTS).astype(jnp.int32)
    starts = jnp.cumsum(counts) - counts
    padded = (counts + EXPERT_BLOCK - 1) // EXPERT_BLOCK * EXPERT_BLOCK
    pad_end = jnp.cumsum(padded)
    pad_start = pad_end - padded
    dest = pad_start[e_s] + (jnp.arange(n_assign, dtype=jnp.int32) - starts[e_s])
    n_blocks = (n_assign + EXPERT_BLOCK - 1) // EXPERT_BLOCK + N_EXPERTS
    n_rows = n_blocks * EXPERT_BLOCK
    row_tok = jnp.full((n_rows,), t, jnp.int32).at[dest].set(tok_s)
    row_gate = jnp.zeros((n_rows,), jnp.float32).at[dest].set(g_s)
    block_start = jnp.arange(n_blocks, dtype=jnp.int32) * EXPERT_BLOCK
    block_expert = jnp.minimum(jnp.searchsorted(pad_end, block_start, side='right'),
                               N_EXPERTS - 1).astype(jnp.int32)
    x_pad = jnp.concatenate([xt, jnp.zeros((1, d), xt.dtype)], axis=0)
    x_rows = x_pad[row_tok].reshape(n_blocks, EXPERT_BLOCK, d)

    def expert_block(args):
        xb, e = args
        hh = (xb @ w1[e] + b1[e]).reshape(EXPERT_BLOCK, D_EXPERT, 2)
        x_glu = jnp.minimum(hh[..., 0], SWIGLU_LIMIT)
        x_lin = jnp.clip(hh[..., 1], -SWIGLU_LIMIT, SWIGLU_LIMIT)
        act = x_glu * jax.nn.sigmoid(SWIGLU_ALPHA * x_glu) * (x_lin + 1)
        return act @ w2[e] + b2[e]

    y_rows = lax.map(expert_block, (x_rows, block_expert)).reshape(n_rows, d)
    y_rows = y_rows * row_gate[:, None].astype(y_rows.dtype)
    y = jax.ops.segment_sum(y_rows, row_tok, num_segments=t + 1)[:t]
    return y.reshape(bsz, s, d)

def setup_inputs(seed: int = 0) -> dict:
    key = jax.random.key(seed)
    ks = jax.random.split(key, 24)
    f32 = jnp.float32

    def nrm(k, shape, scale):
        return jax.random.normal(k, shape, f32) * scale

    L = DEPTH
    return {
        "x": nrm(ks[0], (BATCH, SEQ, D_MODEL), 1.0),
        "g_mix": 1.0 + nrm(ks[1], (L, D_MODEL), 0.02),
        "w_in": nrm(ks[2], (L, D_MODEL, IN_WIDTH), D_MODEL ** -0.5),
        "b_in": nrm(ks[3], (L, IN_WIDTH), 0.02),
        "sinks": nrm(ks[4], (L, N_Q_HEADS), 0.5),
        "w_dw": nrm(ks[5], (L, CONV_KERNEL, CONV_WIDTH), CONV_KERNEL ** -0.5),
        "b_dw": nrm(ks[6], (L, CONV_WIDTH), 0.02),
        "ln_g": 1.0 + nrm(ks[7], (L, CONV_WIDTH), 0.02),
        "ln_b": nrm(ks[8], (L, CONV_WIDTH), 0.02),
        "g_attn_out": 1.0 + nrm(ks[9], (L, ATTN_WIDTH), 0.02),
        "g_conv_out": 1.0 + nrm(ks[10], (L, CONV_WIDTH), 0.02),
        "w_out": nrm(ks[11], (L, MIX_WIDTH, D_MODEL), MIX_WIDTH ** -0.5),
        "b_out": nrm(ks[12], (L, D_MODEL), 0.02),
        "g_ffn": 1.0 + nrm(ks[13], (L, D_MODEL), 0.02),
        "w_router": nrm(ks[14], (L, D_MODEL, N_EXPERTS), D_MODEL ** -0.5),
        "b_router": nrm(ks[15], (L, N_EXPERTS), 0.01),
        "w1": nrm(ks[16], (L, N_EXPERTS, D_MODEL, 2 * D_EXPERT), D_MODEL ** -0.5),
        "b1": nrm(ks[17], (L, N_EXPERTS, 2 * D_EXPERT), 0.02),
        "w2": nrm(ks[18], (L, N_EXPERTS, D_EXPERT, D_MODEL), D_EXPERT ** -0.5),
        "b2": nrm(ks[19], (L, N_EXPERTS, D_MODEL), 0.02),
        "g_final": 1.0 + nrm(ks[20], (D_MODEL,), 0.02),
    }

def reference(x, g_mix, w_in, b_in, sinks, w_dw, b_dw, ln_g, ln_b, g_attn_out, g_conv_out,
              w_out, b_out, g_ffn, w_router, b_router, w1, b1, w2, b2, g_final):
    split_at = [ATTN_WIDTH, ATTN_WIDTH + KV_WIDTH, ATTN_WIDTH + 2 * KV_WIDTH,
                ATTN_WIDTH + 2 * KV_WIDTH + CONV_WIDTH]
    for l in range(DEPTH):
        u = rms_norm(x, g_mix[l])
        proj = u @ w_in[l] + b_in[l]
        q, k, v, conv_a, conv_gate = jnp.split(proj, split_at, axis=-1)
        attn = sliding_window_attention_with_sinks(q, k, v, sinks[l])
        conv = conformer_conv(conv_a, conv_gate, w_dw[l], b_dw[l], ln_g[l], ln_b[l])
        mixed = jnp.concatenate([rms_norm(attn, g_attn_out[l]),
                                 rms_norm(conv, g_conv_out[l])], axis=-1)
        x = x + (mixed @ w_out[l] + b_out[l])
        x = x + moe_ffn(rms_norm(x, g_ffn[l]), w_router[l], b_router[l],
                        w1[l], b1[l], w2[l], b2[l])
    return rms_norm(x, g_final)


_drawn_inputs = setup_inputs


def setup_inputs(seed=0):
    import zlib

    import numpy as np

    out = dict(_drawn_inputs(seed))
    spreads = {}
    factors = {'sinks': 4.76, 'b_router': 2.713, 'b1': 6.849, 'b2': 7.955, 'g_final': 2.95}
    for name, (base, spread) in spreads.items():
        noise = np.random.default_rng([zlib.crc32(name.encode()), seed]).standard_normal(out[name].shape)
        drawn = base * np.exp(spread * noise) if base else spread * noise
        out[name] = __import__('jax').numpy.asarray(drawn.astype(out[name].dtype))
    for name, factor in factors.items():
        out[name] = (out[name] * factor).astype(out[name].dtype)
    return out
```

```python
import concourse.bass as bass
from concourse import mybir
from contextlib import ExitStack

F32 = mybir.dt.float32
F16 = mybir.dt.float16
BF16 = mybir.dt.bfloat16
U32 = mybir.dt.uint32
I32 = mybir.dt.int32
ALU = mybir.AluOpType
ACT = mybir.ActivationFunctionType
AXX = mybir.AxisListType.X

P = 128
SEQ = 1024
D = 1024
T = SEQ // P
KC = D // P
HEADS, KV, HD = 8, 2, 64
GROUP = HEADS // KV
CW = 512
CT = CW // P
TAPS = 31
NE, TOPK = 32, 4
HALF = 512
UNIT = KC * HALF
KV_UNIT = KC * 256
RING = 3
MIX_UNITS = 6
W1_UNITS, W2_UNITS = 4, 2
ITEM_UNITS = W1_UNITS + W2_UNITS
ITEM_ROWS = 256
WIDTHS = (64, 96, 128, 160, 192, 224, 256)
ITEMS = NE + SEQ * TOPK // ITEM_ROWS
EXTRA = ITEMS - NE
FEW = 16
SPARE = ITEM_ROWS
DVE_SPLIT = 2688
W_SCALE, X_SCALE = 64.0, 16.0
Z_SCALE = W_SCALE * X_SCALE
LIMIT, ALPHA = 7.0, 1.702
EPS = 1e-5
SCORE_SCALE = HD ** -0.5
OUT_SCALE = X_SCALE * D ** 0.5

PARAMS = {}
_at = 0
for _name, _n in (("b_gate", CT), ("b_a", CT), ("b_q", GROUP), ("b_k", 1), ("w_dw", CT * TAPS), ("b_dw", CT),
                  ("ln_g", CT), ("ln_b", CT), ("g_attn", CT), ("g_conv", CT), ("sinks", HEADS)):
    PARAMS[_name] = (_at, _at + _n)
    _at += _n
N_PARAMS = _at
CONSTS = {}
_at = 0
for _name, _n in (("ident", P), ("before", P), ("ones", P), ("iota", NE), ("base", NE),
                  ("token", T), ("item_e", ITEMS), ("item_row", ITEMS), ("eye", NE), ("extra", EXTRA), ("e", 1), ("e_row", 1), ("power", 1),
                  ("band", 2 * P)):
    CONSTS[_name] = (_at, _at + _n)
    _at += _n
N_CONSTS = _at


def hymba_layer_kernel(nc, x, w_units, w_kv, params, rows, b_v, b_router, w_router, b1, b2, consts, table0, zeros, out):
    h_rows = nc.dram_tensor("h_rows", (SEQ + SPARE, D), F32, kind="Internal").ap()
    y_rows = nc.dram_tensor("y_rows", (SEQ + SPARE, D), F32, kind="Internal").ap()
    table = nc.dram_tensor("slot_table", (NE * SEQ, 2), U32, kind="Internal").ap()

    ctx = ExitStack()
    with ctx:
        def sem(name):
            return ctx.enter_context(nc.semaphore(name))

        raw = ctx.enter_context(nc.sbuf_tensor("raw", [P, RING, UNIT], F32))
        whi = ctx.enter_context(nc.sbuf_tensor("whi", [P, RING, UNIT], F16))
        wlo = ctx.enter_context(nc.sbuf_tensor("wlo", [P, RING, UNIT], F16))
        KB = 256
        arena = ctx.enter_context(nc.sbuf_tensor("arena", [P, 111 * KB + 192], F32))
        ps = ctx.enter_context(nc.psum_tensor("ps", [P, 8, HALF], F32))

        def view(word, shape, dt=F32):
            n = 1
            for s in shape:
                n *= s
            words = n * (4 if dt in (F32, U32, I32) else 2) // 4
            v = arena[:, int(word):int(word) + words]
            if dt != F32:
                v = v.bitcast(dt)
            if len(shape) == 2:
                v = v.rearrange("p (a b) -> p a b", a=shape[0])
            if len(shape) == 3:
                v = v.rearrange("p (a b c) -> p a b c", a=shape[0], b=shape[1])
            return v

        A, B, C, DD, G, E, K = 0, 32 * KB, 56 * KB, 65 * KB, 81 * KB, 93 * KB, 101 * KB
        u_hi = view(A, (KC, SEQ), F16)
        u_lo = view(A + 16 * KB, (KC, SEQ), F16)
        q_t = view(B, (GROUP, SEQ))
        k_t = view(B + 16 * KB, (SEQ,))
        v_sb = view(B + 20 * KB, (T, P))
        cu = view(C, (2, TAPS - 1 + SEQ))
        conv = view(DD, (CT, SEQ))
        x_in = view(G, (2, D))
        xn = view(G + 8 * KB, (D,))
        g_mix = view(E, (D,))
        band_f = view(E + 4 * KB, (2 * P,))
        sg = view(E, (2, HALF))
        mix_hi = view(A, (2 * CT, SEQ), F16)
        mix_lo = view(A + 16 * KB, (2 * CT, SEQ), F16)
        prob = view(G, (2, GROUP, 2 * P))
        prob_t = view(G + 8 * KB, (2, HALF))
        sq = view(E, (CT, HALF))
        heads = [view(C, (CT, HALF)), view(DD, (CT, HALF))]
        xr = view(B, (4, D))
        h_sb = view(B + 16 * KB, (2, D))
        b_out = view(G, (D,))
        g_ffn = view(G + 4 * KB, (D,))
        ht_hi = view(G + 8 * KB, (KC, P), F16)
        ht_lo = view(G + 10 * KB, (KC, P), F16)
        b2_sb = view(E, (D,))
        wr = view(E + 4 * KB, (KC * NE,))
        wr_hi = view(E + 5 * KB, (KC, NE), F16)
        wr_lo = view(E + 5.5 * KB, (KC, NE), F16)
        xg = view(A, (2, D))
        xt_hi = view(A + 8 * KB, (KC, ITEM_ROWS), F16)
        xt_lo = view(A + 12 * KB, (KC, ITEM_ROWS), F16)
        act_hi = view(A + 16 * KB, (KC, ITEM_ROWS), F16)
        act_lo = view(A + 20 * KB, (KC, ITEM_ROWS), F16)
        y_sb = view(A + 24 * KB, (2, D))
        b1_sb = view(C, (2 * KC, NE))
        g_top = view(C + 2 * KB, (KC, NE))
        g_add = view(C + 3 * KB, (KC, NE))
        l_top = view(C + 4 * KB, (KC, NE))
        l_low = view(C + 5 * KB, (KC, NE))
        l_add = view(C + 6 * KB, (KC, NE))
        glu = view(DD, (2, ITEM_ROWS))
        lin = view(DD + 2 * KB, (2, ITEM_ROWS))
        sig = view(DD + 4 * KB, (2, ITEM_ROWS))
        gs = view(DD + 6 * KB, (2, ITEM_ROWS))
        act = view(DD + 8 * KB, (2, ITEM_ROWS))
        idx_all = view(DD + 10 * KB, (ITEMS, 2, 2), U32)
        idx_g = view(DD + 11 * KB, (2, 2), U32)
        idx_s = view(DD + 11 * KB + 4, (2, 2), U32)
        fin = view(B, (6, D))
        g_final = view(G, (D,))
        kat = [K]

        def small(shape, dt=F32):
            n = 1
            for s in shape:
                n *= s
            w = kat[0]
            kat[0] += (n * (4 if dt in (F32, U32, I32) else 2) + 7) // 8 * 2
            assert kat[0] <= 111 * KB + 192
            return view(w, shape, dt)

        cs = {}
        cs_all = small((CONSTS["band"][0],))
        for name, (a, b) in CONSTS.items():
            if name != "band":
                cs[name] = cs_all[:, a:b]
        pr = small((N_PARAMS,))
        par = {name: pr[:, a:b] for name, (a, b) in PARAMS.items()}
        ident_b = small((P,), BF16)
        before_b = small((P,), BF16)
        ones_b = small((P,), BF16)
        band_b = small((2 * P,), BF16)
        mean_w = small((P,))
        rs = small((2, HALF))
        neg_sinks = small((HEADS,))
        ss1, rs1, ss2, rs2, ss3, rs3 = (small((T,)) for _ in range(6))
        nm, dsk, rsum, esum, rden, mxs = (small((2, GROUP)) for _ in range(6))
        bv_sb = view(E + 6 * KB, (P,))
        br_sb = small((NE,))
        lg = small((NE,))
        mx8 = small((8,))
        ix8 = small((8,), U32)
        ixf = small((TOPK,))
        nm0 = small((1,))
        ex = small((TOPK,))
        se = small((1,))
        rse = small((1,))
        oh = view(E + 6 * KB, (2, TOPK, NE))
        gk = view(E + 7 * KB, (TOPK, NE))
        gates_g = small((NE,))
        posb = small((NE,))
        slf = small((TOPK,))
        slots = view(DD + 13 * KB, (T, TOPK), U32)
        pay = view(DD + 13 * KB + 32, (T, TOPK * 2), U32)
        mb = view(DD + 13 * KB + 96, (T, NE), BF16)
        gt_sb = view(E + 7.5 * KB, (P,))
        cnt, xe, st, en = (small((1,)) for _ in range(4))
        itm = view(B, (4, ITEMS))
        mt, rr, t1 = (view(B + KB + 64 * i, (EXTRA,)) for i in range(3))
        items = view(DD + 12 * KB, (4, ITEMS), I32)

        W_LAST = 3 * ITEMS

        raw_full = [sem(f"raw_full{s}") for s in range(RING)]
        hi_done, lo_dve, lo_pool, raw_scaled = sem("hi_done"), sem("lo_dve"), sem("lo_pool"), sem("raw_scaled_pool")
        c_in, g_in, xin = sem("consts_loaded"), sem("g_mix_loaded"), [sem("x_loaded0"), sem("x_loaded1")]
        step_pool, step_dve = sem("waits_passed_pool"), sem("waits_passed_dve")
        setup, eps_p = sem("setup_pool"), sem("eps_added")
        setup_d = sem("setup_dve")
        x_sq, x_rs, x_nd, x_tr, u_hd, u_ld = (sem(n) for n in ("x_squared", "x_rstd", "x_normed", "x_transposed", "u_hi_done", "u_lo_done"))
        proj, ev_a, ev_d = sem("proj_done"), sem("proj_read_act"), sem("proj_read_dve")
        tap_d = sem("taps_done")
        mean_pe, sub_d, vsq_a, var_pe, ve_d, root_a, rstd_d = (sem(n) for n in ("mean_done", "centred", "centred_squared", "var_done", "var_copied", "root_done", "rstd_done"))
        y_d, sgm_a, z_p, s_d, csq_a, ms_pe, mse_d, m_d, mhi_a, mlo_p = (sem(n) for n in (
            "ln_scaled", "swish_sigmoid", "ln_affine", "swish_done", "branch_squared", "meansq_done", "meansq_copied", "branch_normed", "mix_hi_done", "mix_lo_done"))
        sc_pe, mx_d, nm_d, dsk_d, exp_a, den_d, rden_d, pn_p, pt_pe, pta, ptd, ot_pe, og_a = (sem(n) for n in (
            "scores_done", "row_max", "neg_max", "sink_shift", "exp_done", "denominator", "rden", "probs_normed", "probs_transposed", "prob_t_act", "prob_t_dve", "heads_done", "heads_read"))
        r_in, xr_in, xb_p, out_pe, x2_d, x2sq, rs2_p, h_d, h_st, tr_pe, hth, htl = (sem(n) for n in (
            "route_consts", "xr_loaded", "xb_done", "out_done", "x2_done", "x2_squared", "x2_rstd", "h_done", "h_stored", "h_transposed", "ht_hi_done", "ht_lo_done"))
        xr_s = [sem(f"xr_loaded{i}") for i in range(4)]
        rt_pe, ra, ea, gt_pe, rc, gb_pe, acc_d, acc_st, scat = (sem(n) for n in (
            "router_done", "route_step", "gate_exp", "gates_transposed", "gates_t_copied", "gate_bias_done", "acc_done", "acc_stored", "slots_stored"))
        rb = sem("slot_step")
        init = sem("tables_initialised")
        cnt_pe, it_d, st_pe, row_pe, items_ready = (sem(n) for n in ("counts_done", "item_step", "starts_done", "item_rows_done", "items_ready"))
        b1_in, b1_t, idx_in, clr = sem("b1_loaded"), sem("b1_tables"), sem("lists_loaded"), sem("expert_cleared")
        zfree, used, xt_ready, xt_hd, t_done, act_done = (sem(n) for n in ("z_banks_free", "units_used", "xt_ready", "xt_hi_done", "rows_transposed", "act_done"))
        ig, is_, xg_in = sem("idx_gather"), sem("idx_scatter"), [sem("rows_gathered0"), sem("rows_gathered1")]
        dch, sig_a, ahi_a, yd, ysc = sem("dve_expert_step"), sem("sigmoid_done"), sem("act_hi_done"), sem("y_done"), [sem("y_scattered0"), sem("y_scattered1")]
        f_in = [sem(f"final_loaded{i}") for i in range(6)]
        gf_in, f_sq, f_rs, f_d, f_st = (sem(n) for n in ("g_final_loaded", "final_squared", "final_rstd", "final_done", "final_stored"))

        block = ctx.enter_context(nc.Block())

        def unit_cols(u):
            return KV_UNIT if u == 3 else UNIT

        def proj_reader(n):
            if n < 16:
                c, r = n // 4, n % 4
                return (ev_a, 2 * c + r + 1) if r < 2 else (ev_d, 2 * c + r - 1)
            return (ev_a, 8 + n - 15) if n < 26 else (ev_d, 8 + n - 25)

        def wait_mix_unit_used(e, u):
            e.wait_ge(*((proj, (8, 16, 24, 28)[u]) if u < 4 else (out_pe, 2 * T)))

        def wait_split(e, u):
            e.wait_ge(lo_dve, u + 1)
            e.wait_ge(lo_pool, u + 1)

        def split_hi(e, u, slot, n):
            e.activation(whi[:, slot, 0:n], raw[:, slot, 0:n], ACT.Copy, scale=W_SCALE).then_inc(hi_done, 1)

        def split_lo_pool(e, k, slot, a, b):
            part = raw[:, slot, a:b]
            e.tensor_scalar(part, part, W_SCALE, 0.0, ALU.mult, ALU.add).then_inc(raw_scaled, 1)
            e.wait_ge(raw_scaled, k)
            if not isinstance(k, int):
                after_waits(e)
            e.tensor_tensor(wlo[:, slot, a:b], part, whi[:, slot, a:b], ALU.subtract).then_inc(lo_pool, 1)

        def split_lo(e, slot, a, b, done):
            e.scalar_tensor_tensor(out=wlo[:, slot, a:b], in0=raw[:, slot, a:b], scalar=W_SCALE,
                                   in1=whi[:, slot, a:b], op0=ALU.mult, op1=ALU.subtract).then_inc(done, 1)

        def mixer_split(e, u):
            slot, n = u % RING, unit_cols(u)
            if u >= RING:
                wait_mix_unit_used(e, u - RING)
            if e is act_engine[0]:
                e.wait_ge(raw_full[slot], 16 * (u // RING + 1))
                split_hi(e, u, slot, n)
            else:
                e.wait_ge(hi_done, u + 1)
                cut = DVE_SPLIT * n // UNIT
                if e is dve_engine[0]:
                    split_lo(e, slot, 0, cut, lo_dve)
                else:
                    split_lo_pool(e, u + 1, slot, cut, n)

        act_engine, dve_engine, pool_engine = [None], [None], [None]

        def after_waits(e):
            e.sem_inc(step_pool if e is pool_engine[0] else step_dve, 1)

        def item_split(e, i, v):
            slot = v % RING
            e.wait_ge(used, i * ITEM_UNITS + (v - 2))
            if v == 2:
                e.wait_ge(out_pe, 2 * T)
            if e is act_engine[0]:
                e.wait_ge(raw_full[slot], i * 32 + 16 * (3 + v // RING))
                split_hi(e, v, slot, UNIT)
            else:
                e.wait_ge(hi_done, i * ITEM_UNITS + (MIX_UNITS + v + 1))
                if e is dve_engine[0]:
                    split_lo(e, slot, 0, DVE_SPLIT, lo_dve)
                else:
                    after_waits(e)
                    split_lo_pool(e, i * ITEM_UNITS + (MIX_UNITS + v + 1), slot, DVE_SPLIT, UNIT)

        items_flat = items.rearrange("p a b -> p (a b)")
        N_CONST_DMAS = 16 * 5

        def taps(e, c, done):
            a, b = 0, SEQ
            dst = conv[:, c, a:b]
            w = par["w_dw"]
            e.tensor_scalar(dst, cu[:, c % 2, a:b], w[:, c * TAPS:c * TAPS + 1], par["b_dw"][:, c:c + 1],
                            ALU.mult, ALU.add).then_inc(done, 1)
            for k in range(1, TAPS):
                e.wait_ge(done, c * TAPS + k)
                e.scalar_tensor_tensor(out=dst, in0=cu[:, c % 2, a + k:b + k], scalar=w[:, c * TAPS + k:c * TAPS + k + 1],
                                       in1=dst, op0=ALU.mult, op1=ALU.add).then_inc(done, 1)

        @block.sync
        def _(e):
            e.dma_start(pr, params).then_inc(c_in, 16)
            e.dma_start(cs_all, consts[:, 0:CONSTS["band"][0]]).then_inc(c_in, 16)
            e.dma_start(band_f, consts[:, slice(*CONSTS["band"])]).then_inc(c_in, 16)
            e.dma_start(bv_sb, b_v).then_inc(c_in, 16)
            e.dma_start(br_sb, b_router).then_inc(c_in, 16)
            e.dma_start(g_mix, rows[0]).then_inc(g_in, 16)

            def load_unit(u):
                slot = u % RING
                if u >= RING:
                    wait_split(e, u - RING)
                if u == 3:
                    e.dma_start(raw[:, slot, 0:KV_UNIT], w_kv).then_inc(raw_full[slot], 16)
                else:
                    e.dma_start(raw[:, slot, :], w_units[u - (u > 3)]).then_inc(raw_full[slot], 16)

            for t in range(T):
                if t >= 2:
                    e.wait_ge(x_nd, t - 1)
                e.dma_start(x_in[:, t % 2, :], x[t * P:(t + 1) * P, :]).then_inc(xin[t % 2], 16)
                if t in (2, 4, 6):
                    load_unit((2, 4, 6).index(t))
            e.dma_start(table, table0).then_inc(init, 16)
            e.dma_start(h_rows[SEQ:SEQ + SPARE, :], zeros).then_inc(init, 16)
            e.dma_start(y_rows[SEQ:SEQ + SPARE, :], zeros).then_inc(init, 16)
            for u in range(3, 8):
                load_unit(u)
            e.wait_ge(ot_pe, 2 * T)
            e.wait_ge(ms_pe, 4)
            e.dma_start(b_out, rows[1]).then_inc(r_in, 16)
            e.dma_start(g_ffn, rows[2]).then_inc(r_in, 16)
            e.dma_start(b2_sb[0:NE, :], b2).then_inc(r_in, 16)
            e.dma_start(wr, w_router).then_inc(r_in, 16)
            e.wait_ge(mhi_a, 4 * CT)
            e.wait_ge(mlo_p, 4 * CT)
            e.dma_start(b1_sb.rearrange("p a b -> p (a b)"), b1).then_inc(b1_in, 16)
            for t in range(T + 3):
                if t < T:
                    if t >= 4:
                        e.wait_ge(acc_st, 16 * (t - 3))
                    e.dma_start(xr[:, t % 4, :], x[t * P:(t + 1) * P, :]).then_inc(xr_s[t % 4], 16)
                if 1 <= t <= T:
                    e.wait_ge(h_d, t)
                    e.dma_start(h_rows[(t - 1) * P:t * P, :], h_sb[:, (t - 1) % 2, :]).then_inc(h_st, 16)
                if t >= 3:
                    e.wait_ge(acc_d, 2 * (t - 2))
                    e.dma_start(y_rows[(t - 3) * P:(t - 2) * P, :], xr[:, (t - 3) % 4, :]).then_inc(acc_st, 16)

            def item_weights(i, expert, first=0):
                for v in range(first, ITEM_UNITS):
                    for s in (hi_done, lo_dve, lo_pool):
                        e.wait_ge(s, i * ITEM_UNITS + (MIX_UNITS + v - 2))
                    src = w_units[bass.ds(expert * ITEM_UNITS + (MIX_UNITS - 1 + v), 1)].rearrange("a p n -> p (a n)")
                    e.dma_start(raw[:, v % RING, :], src).then_inc(raw_full[v % RING], 16)

            e.wait_ge(lo_pool, MIX_UNITS)
            e.wait_ge(lo_dve, MIX_UNITS)
            for v in range(2, ITEM_UNITS):
                for s in (hi_done, lo_dve, lo_pool):
                    e.wait_ge(s, MIX_UNITS + v - 2)
                e.dma_start(raw[:, v % RING, :], w_units[MIX_UNITS - 1 + v]).then_inc(raw_full[v % RING], 16)
            with e.Fori(1, NE) as i:
                item_weights(i, i)
            e.wait_ge(items_ready, 1)
            last_item = e.value_load(items_flat[0:1, W_LAST:W_LAST + 1], min_val=NE - 1, max_val=ITEMS - 1)
            with e.If(last_item > NE - 1):
                with e.Fori(NE, last_item + 1) as i:
                    expert = e.value_load(items_flat[0:1, bass.ds(i, 1)], min_val=0, max_val=NE - 1)
                    item_weights(i, expert)
            e.nop()
            e.dma_start(g_final, rows[3]).then_inc(gf_in, 16)
            e.wait_ge(ysc[0], last_item * 16 + 16)
            e.wait_ge(ysc[1], last_item * 16 + 16)
            for t in range(T):
                if t >= 6:
                    e.wait_ge(f_st, 16 * (t - 5))
                e.dma_start(fin[:, t % 6, :], y_rows[t * P:(t + 1) * P, :]).then_inc(f_in[t % 6], 16)
                if t >= 2:
                    e.wait_ge(f_d, t - 1)
                    e.dma_start(out[(t - 2) * P:(t - 1) * P, :], fin[:, (t - 2) % 6, :]).then_inc(f_st, 16)
            for t in range(T - 2, T):
                e.wait_ge(f_d, t + 1)
                e.dma_start(out[t * P:(t + 1) * P, :], fin[:, t % 6, :]).then_inc(f_st, 16)
            e.wait_ge(f_st, 16 * T)

        @block.tensor
        def _(e):
            def product(out_ap, l_hi, l_lo, r_hi, r_lo, start, stop):
                e.matmul(out_ap, l_hi, r_hi, start=start, stop=False)
                e.matmul(out_ap, l_hi, r_lo, start=False, stop=False)
                return e.matmul(out_ap, l_lo, r_hi, start=False, stop=stop)

            e.wait_ge(c_in, N_CONST_DMAS)
            for t in range(T):
                e.wait_ge(x_nd, t + 1)
                if t >= 2:
                    e.wait_ge(u_ld, t - 1)
                for k in range(KC):
                    last = e.transpose(ps[:, 2 * (t % 2) + k // 4, (k % 4) * P:(k % 4 + 1) * P],
                                       xn[:, k * P:(k + 1) * P], cs["ident"])
                last.then_inc(x_tr, 1)
            n = 0
            for u in range(4):
                slot = u % RING
                wait_split(e, u)
                for tile in range(4 if u < 3 else 1):
                    for half in range(2):
                        e.wait_ge(u_ld, 4 * (half + 1))
                        if n >= 4:
                            e.wait_ge(*proj_reader(n - 4))
                        wide = HALF if u < 3 else 256
                        for k in range(KC):
                            at = k * wide + tile * P
                            toks = slice(half * HALF, (half + 1) * HALF)
                            last = product(ps[:, 4 + n % 4, :], whi[:, slot, at:at + P], wlo[:, slot, at:at + P],
                                           u_hi[:, k, toks], u_lo[:, k, toks], k == 0, k == KC - 1)
                        last.then_inc(proj, 1)
                        n += 1
            for quad in range(2):
                e.wait_ge(*proj_reader(n - 4))
                for tt in range(4):
                    t = quad * 4 + tt
                    for k in range(KC):
                        at = k * 256 + P
                        toks = slice(t * P, (t + 1) * P)
                        last = product(ps[:, 4 + n % 4, tt * P:(tt + 1) * P], u_hi[:, k, toks], u_lo[:, k, toks],
                                       whi[:, 0, at:at + P], wlo[:, 0, at:at + P], k == 0, k == KC - 1)
                last.then_inc(proj, 1)
                n += 1

            def channel_mean(bank, src, done):
                for j in range(CT):
                    last = e.matmul(ps[:, bank, :], mean_w, src[:, j, :], start=(j == 0), stop=(j == CT - 1))
                last.then_inc(done, 1)

            def scores(n):
                b, g = n // KV, n % KV
                if n < 2:
                    e.wait_ge(ev_a, 18)
                else:
                    e.wait_ge(exp_a, 5 * (n - 1))
                lo = 0 if b else P
                part = slice(g * HD, (g + 1) * HD)
                for j in range(GROUP):
                    dst = ps[:, 2 * (n % 2) + j // 2, (j % 2) * 2 * P + lo:(j % 2 + 1) * 2 * P]
                    e.matmul(dst, q_t[part, j, b * P:(b + 1) * P], k_t[part, (b - 1) * P + lo:(b + 1) * P],
                             start=True, stop=False)
                    last = e.matmul(dst, ident_b, band_b[:, lo:2 * P], start=False, stop=True)
                last.then_inc(sc_pe, 1)

            def probs_t(n):
                b = n // KV
                e.wait_ge(pn_p, 4 * (n + 1))
                if n >= 1:
                    e.wait_ge(pta, n)
                    e.wait_ge(ptd, n)
                for kb in range(0 if b else 1, 2):
                    for j in range(GROUP):
                        last = e.transpose(ps[:, 4 + kb, j * P:(j + 1) * P],
                                           prob[:, n % 2, j, kb * P:(kb + 1) * P], cs["ident"])
                last.then_inc(pt_pe, 1)

            def heads_t(n):
                b, g = n // KV, n % KV
                e.wait_ge(pta, n + 1)
                e.wait_ge(ptd, n + 1)
                if n == 0:
                    e.wait_ge(ve_d, 2)
                else:
                    e.wait_ge(og_a, n)
                first = 0 if b else 1
                for kb in range(first, 2):
                    last = e.matmul(ps[g * HD:(g + 1) * HD, 6, :], v_sb[:, b - 1 + kb, g * HD:(g + 1) * HD],
                                    prob_t[:, kb, :], start=(kb == first), stop=(kb == 1))
                last.then_inc(ot_pe, 1)

            e.wait_ge(tap_d, CT * TAPS)
            e.wait_ge(ev_d, 10)
            for h in range(2):
                channel_mean(7 - h, conv[:, :, h * HALF:(h + 1) * HALF], mean_pe)
            scores(0)
            scores(1)
            for h in range(2):
                e.wait_ge(vsq_a, CT * (h + 1))
                channel_mean(7 - h, sq, var_pe)

            def branch_meansq(i):
                e.wait_ge(csq_a, CT * (i + 1))
                e.wait_ge(*((ve_d, 1) if i == 0 else (mse_d, i)))
                channel_mean(7, sq, ms_pe)

            for n in range(2 * T):
                probs_t(n)
                heads_t(n)
                if n + 2 < 2 * T:
                    scores(n + 2)
                if n in (1, 3, 9):
                    branch_meansq((1, 3, 9).index(n))
            branch_meansq(3)

            def out_half(t, half):
                slot = (4 + half) % RING
                if t == 0:
                    wait_split(e, 4 + half)
                    e.wait_ge(mlo_p, 4 * CT)
                    e.wait_ge(exp_a, 5 * 2 * T)
                if t >= 2 and half == 0:
                    e.wait_ge(x2_d, t - 1)
                toks = slice(t * P, (t + 1) * P)
                for c in range(2 * CT):
                    at = c * HALF
                    last = product(ps[:, 2 * (t % 2) + half, :], mix_hi[:, c, toks], mix_lo[:, c, toks],
                                   whi[:, slot, at:at + HALF], wlo[:, slot, at:at + HALF], c == 0, c == 2 * CT - 1)
                last.then_inc(out_pe, 1)

            def h_t(t):
                e.wait_ge(h_d, t + 1)
                if t == 0:
                    e.wait_ge(pta, 2 * T)
                    e.wait_ge(ptd, 2 * T)
                else:
                    e.wait_ge(htl, t)
                for k in range(KC):
                    last = e.transpose(ps[:, 4 + k // 4, (k % 4) * P:(k % 4 + 1) * P],
                                       h_sb[:, t % 2, k * P:(k + 1) * P], cs["ident"])
                last.then_inc(tr_pe, 1)

            def router(t):
                e.wait_ge(htl, t + 1)
                if t == 0:
                    e.wait_ge(og_a, 2 * T)
                    e.wait_ge(b1_t, 1)
                else:
                    e.wait_ge(rc, t)
                for k in range(KC):
                    last = product(ps[:, 6, 0:NE], ht_hi[:, k, :], ht_lo[:, k, :], wr_hi[:, k, :], wr_lo[:, k, :],
                                   k == 0, k == KC - 1)
                last.then_inc(rt_pe, 1)

            def positions(t):
                e.wait_ge(ra, 11 * (t + 1))
                for s in range(t):
                    e.matmul(ps[:, 6, NE:2 * NE], ones_b, mb[:, s, :], start=(s == 0), stop=False)
                e.matmul(ps[:, 6, NE:2 * NE], before_b, mb[:, t, :], start=(t == 0), stop=True)
                e.transpose(ps[0:NE, 6, P:2 * P], gates_g, cs["ident"]).then_inc(gt_pe, 1)

            def gate_bias(t, half):
                e.wait_ge(rc, t + 1)
                if t == 0 and half == 0:
                    e.wait_ge(mse_d, 4)
                elif half or t:
                    e.wait_ge(acc_d, 2 * t + half)
                e.matmul(ps[:, 7, :], gt_sb[0:NE, :], b2_sb[0:NE, half * HALF:(half + 1) * HALF],
                         start=True, stop=True).then_inc(gb_pe, 1)

            e.wait_ge(r_in, 64)
            for t in range(T + 3):
                if t < T:
                    out_half(t, 0)
                if 1 <= t <= T:
                    h_t(t - 1)
                if 2 <= t <= T + 1:
                    positions(t - 2)
                if 3 <= t:
                    gate_bias(t - 3, 0)
                if t < T:
                    out_half(t, 1)
                if 3 <= t:
                    gate_bias(t - 3, 1)
                if 1 <= t <= T:
                    router(t - 1)

            for t in range(T):
                last = e.matmul(ps[0:NE, 6, 2 * P:2 * P + 1], mb[:, t, :], ones_b[:, 0:1], start=(t == 0), stop=(t == T - 1))
            last.then_inc(cnt_pe, 1)
            e.wait_ge(it_d, 4)
            e.matmul(ps[0:NE, 6, 2 * P + 2:2 * P + 3], cs["before"][0:NE, 0:NE], xe[0:NE, :], start=True, stop=True).then_inc(st_pe, 1)
            e.wait_ge(it_d, 18)
            e.matmul(ps[0:1, 7, 0:4 * ITEMS], cs["ones"][0:NE, 0:1], itm[0:NE, :, :].rearrange("p a b -> p (a b)"),
                     start=True, stop=True).then_inc(row_pe, 1)

            def rows_t(block, banks):
                for k in range(KC):
                    last = e.transpose(ps[:, banks + k // 4, (k % 4) * P:(k % 4 + 1) * P],
                                       xg[:, block, k * P:(k + 1) * P], cs["ident"])
                return last

            def transpose_rows(i, n):
                e.wait_ge(xg_in[0], i * 16 + 32)
                e.wait_ge(xg_in[1], i * 16 + 32)
                e.wait_ge(yd, i * 2)
                e.wait_ge(zfree, i * 4 + 5)
                with e.If(n > P):
                    rows_t(1, 0)
                rows_t(0, 6).then_inc(t_done, 1)

            def up(u, width):
                slot, pair = u % RING, 2 * (u % 2)
                for tile in range(4):
                    for k in range(KC):
                        at = k * HALF + tile * P
                        last = product(ps[:, pair + tile // 2, (tile % 2) * ITEM_ROWS:(tile % 2) * ITEM_ROWS + width],
                                       whi[:, slot, at:at + P], wlo[:, slot, at:at + P],
                                       xt_hi[:, k, 0:width], xt_lo[:, k, 0:width], k == 0, k == KC - 1)
                last.then_inc(used, 1)

            def all_up(i, width):
                for u in range(W1_UNITS):
                    e.wait_ge(lo_dve, i * ITEM_UNITS + (MIX_UNITS + u + 1))
                    e.wait_ge(lo_pool, i * ITEM_UNITS + (MIX_UNITS + u + 1))
                    e.wait_ge(zfree, i * 4 + (u + 1))
                    up(u, width)

            def by_width(n, widths, body):
                if len(widths) == 1:
                    body(widths[0])
                    return
                mid = len(widths) // 2
                with e.If(n <= widths[mid - 1]):
                    by_width(n, widths[:mid], body)
                    e.nop()
                with e.Else():
                    by_width(n, widths[mid:], body)
                    e.nop()

            def down(half, blk):
                slot = (W1_UNITS + half) % RING
                for k in range(KC):
                    at = k * HALF
                    toks = slice(blk * P, (blk + 1) * P)
                    last = product(ps[:, 4 + 2 * half + blk, :], act_hi[:, k, toks], act_lo[:, k, toks],
                                   whi[:, slot, at:at + HALF], wlo[:, slot, at:at + HALF], k == 0, k == KC - 1)
                return last

            def item(i, n_last):
                n = e.value_load(items_flat[0:1, bass.ds(i + 2 * ITEMS, 1)], min_val=0, max_val=ITEM_ROWS)
                e.wait_ge(xt_ready, i + 1)
                by_width(n, WIDTHS, lambda w: all_up(i, w))
                if not n_last:
                    n_next = e.value_load(items_flat[0:1, bass.ds(i + (2 * ITEMS + 1), 1)], min_val=0, max_val=ITEM_ROWS)
                    transpose_rows(i, n_next)
                for half in range(W2_UNITS):
                    e.wait_ge(lo_dve, i * ITEM_UNITS + (MIX_UNITS + W1_UNITS + half + 1))
                    e.wait_ge(lo_pool, i * ITEM_UNITS + (MIX_UNITS + W1_UNITS + half + 1))
                    e.wait_ge(act_done, i * 4 + 4)
                    e.wait_ge(yd, i * 2)
                    if half and not n_last:
                        e.wait_ge(xt_ready, i + 2)
                    with e.If(n > P):
                        down(half, 1)
                    down(half, 0).then_inc(used, 1)

            e.wait_ge(items_ready, 1)
            last_item = e.value_load(items_flat[0:1, W_LAST:W_LAST + 1], min_val=NE - 1, max_val=ITEMS - 1)
            e.wait_ge(xg_in[0], 16)
            e.wait_ge(xg_in[1], 16)
            e.wait_ge(zfree, 2)
            rows_t(1, 0)
            rows_t(0, 4).then_inc(t_done, 1)
            with e.Fori(0, last_item) as i:
                item(i, False)
            item(last_item, True)

        @block.scalar
        def _(e):
            act_engine[0] = e
            e.wait_ge(c_in, N_CONST_DMAS)
            for t in range(T + 1):
                if t < T:
                    e.wait_ge(xin[t % 2], 16 * (t // 2 + 1))
                    if t >= 4:
                        e.wait_ge(x_sq, t - 3)
                    e.activation(conv[:, t % 4, :], x_in[:, t % 2, :], ACT.Square,
                                 accum_out=ss1[:, t:t + 1]).then_inc(x_sq, 1)
                if t >= 1:
                    e.wait_ge(x_tr, t)
                    src = ps[:, 2 * ((t - 1) % 2):2 * ((t - 1) % 2) + 2, :].rearrange("p a (k c) -> p (a k) c", c=P)
                    e.activation(u_hi[:, :, (t - 1) * P:t * P], src, ACT.Copy).then_inc(u_hd, 1)
                if t in (3, 5, 7):
                    mixer_split(e, (3, 5, 7).index(t))
            for n in range(26):
                e.wait_ge(proj, n + 1)
                bank = ps[:, 4 + n % 4, :]
                half = n % 2
                if n < 16 and n % 4 < 2:
                    gi = n // 4 * 2 + half
                    if gi >= 2:
                        e.wait_ge(ev_d, gi - 1)
                    e.activation(sg[:, gi % 2, :], bank, ACT.Sigmoid, scale=1.0 / Z_SCALE,
                                 bias=par["b_gate"][:, n // 4:n // 4 + 1]).then_inc(ev_a, 1)
                elif n >= 16:
                    j = n // 2 - 8
                    if n < 24:
                        e.activation(q_t[:, j, half * HALF:(half + 1) * HALF], bank, ACT.Identity, scale=1.0 / Z_SCALE,
                                     bias=par["b_q"][:, j:j + 1]).then_inc(ev_a, 1)
                    else:
                        e.activation(k_t[:, half * HALF:(half + 1) * HALF], bank, ACT.Identity, scale=1.0 / Z_SCALE,
                                     bias=par["b_k"]).then_inc(ev_a, 1)
                if n in (8, 16, 24):
                    mixer_split(e, (8, 16, 24).index(n) + 3)
            mixer_split(e, 6)

            def centred_squares(h):
                for j in range(CT):
                    e.wait_ge(sub_d, CT * h + j + 1)
                    if j == 0:
                        e.wait_ge(*((ev_d, 10) if h == 0 else (var_pe, h)))
                    e.activation(sq[:, j, :], conv[:, j, h * HALF:(h + 1) * HALF], ACT.Square).then_inc(vsq_a, 1)

            def exps(n):
                b = n // KV
                lo = 0 if b else P
                e.wait_ge(nm_d, n + 1)
                if n >= 2:
                    e.wait_ge(pt_pe, n - 1)
                    e.wait_ge(den_d, n - 1)
                for j in range(GROUP):
                    src = ps[:, 2 * (n % 2) + j // 2, (j % 2) * 2 * P + lo:(j % 2 + 1) * 2 * P]
                    e.activation(prob[:, n % 2, j, lo:2 * P], src, ACT.Exp, scale=SCORE_SCALE,
                                 bias=nm[:, n % 2, j:j + 1], accum_out=rsum[:, n % 2, j:j + 1]).then_inc(exp_a, 1)
                e.wait_ge(dsk_d, n + 1)
                e.activation(esum[:, n % 2, :], dsk[:, n % 2, :], ACT.Exp).then_inc(exp_a, 1)

            def root(h, k):
                e.wait_ge(*((ve_d, k) if k <= 2 else (mse_d, k - 2)))
                e.activation(rs[:, h, :], rs[:, h, :], ACT.Sqrt).then_inc(root_a, 1)

            def swish(h):
                for j in range(CT):
                    e.wait_ge(y_d, CT * h + j + 1)
                    if j == 0:
                        e.wait_ge(*((var_pe, 2) if h == 0 else (ms_pe, 1)))
                    e.activation(sq[:, j, :], conv[:, j, h * HALF:(h + 1) * HALF], ACT.Sigmoid,
                                 scale=par["ln_g"][:, j:j + 1], bias=par["ln_b"][:, j:j + 1]).then_inc(sgm_a, 1)
                for j in range(CT):
                    e.wait_ge(s_d, CT * h + j + 1)
                    e.activation(sq[:, j, :], conv[:, j, h * HALF:(h + 1) * HALF], ACT.Square).then_inc(csq_a, 1)

            def head_squares(h):
                e.wait_ge(og_a, 8 * (h + 1))
                e.wait_ge(ms_pe, 2 + h)
                for j in range(CT):
                    e.activation(sq[:, j, :], heads[h][:, j, :], ACT.Square).then_inc(csq_a, 1)

            def mixed_hi(i):
                h = i % 2
                root(h, 3 + i)
                for j in range(CT):
                    src = conv[:, j, h * HALF:(h + 1) * HALF] if i < 2 else heads[h][:, j, :]
                    e.wait_ge(m_d, CT * i + j + 1)
                    e.activation(mix_hi[:, j + (CT if i < 2 else 0), h * HALF:(h + 1) * HALF], src, ACT.Copy).then_inc(mhi_a, 1)

            centred_squares(0)
            exps(0)
            centred_squares(1)
            exps(1)
            root(0, 1)
            root(1, 2)
            for n in range(2 * T):
                b, g = n // KV, n % KV
                e.wait_ge(pt_pe, n + 1)
                if n:
                    e.wait_ge(ot_pe, n)
                e.activation(prob_t[:, 1, :], ps[:, 5, :], ACT.Copy).then_inc(pta, 1)
                e.wait_ge(ot_pe, n + 1)
                if n == 0:
                    e.wait_ge(tap_d, CT * TAPS)
                if n == 8:
                    e.wait_ge(mlo_p, 2 * CT)
                e.activation(heads[b // 4][g * HD:(g + 1) * HD, :, (b % 4) * P:(b % 4 + 1) * P],
                             ps[g * HD:(g + 1) * HD, 6, :].rearrange("p (j c) -> p j c", j=GROUP),
                             ACT.Copy).then_inc(og_a, 1)
                if n + 2 < 2 * T:
                    exps(n + 2)
                if n == 0:
                    swish(0)
                if n == 2:
                    mixed_hi(0)
                    swish(1)
                if n == 4:
                    mixed_hi(1)
                if n == 8:
                    head_squares(0)
                if n == 10:
                    mixed_hi(2)
            head_squares(1)
            mixed_hi(3)

            def h_hi(t):
                e.wait_ge(tr_pe, t + 1)
                if t:
                    e.wait_ge(rt_pe, t)
                e.activation(ht_hi, ps[:, 4:6, :].rearrange("p a (k c) -> p (a k) c", c=P), ACT.Copy, scale=X_SCALE).then_inc(hth, 1)

            for t in range(T + 1):
                if t >= 1:
                    h_hi(t - 1)
                if t < T:
                    e.wait_ge(x2_d, t + 1)
                    if t >= 2:
                        e.wait_ge(tr_pe, t - 1)
                        e.wait_ge(h_st, 16 * (t - 1))
                    e.activation(h_sb[:, t % 2, :], xr[:, t % 4, :], ACT.Square, accum_out=ss2[:, t:t + 1]).then_inc(x2sq, 1)
                if t >= 1:
                    e.wait_ge(ra, 11 * (t - 1) + 5)
                    e.activation(ex, mx8[:, 0:TOPK], ACT.Exp, bias=nm0, accum_out=se).then_inc(ea, 1)
            mixer_split(e, 7)

            def rows_hi(i):
                e.wait_ge(t_done, i + 1)
                e.activation(xt_hi[:, :, 0:P], ps[:, 6:8, :].rearrange("p a (k c) -> p (a k) c", c=P),
                             ACT.Copy, scale=X_SCALE).then_inc(xt_hd, 1)

            def gated(i, u):
                e.wait_ge(dch, i * 32 + (8 * u + 4))
                e.activation(sig, glu, ACT.Sigmoid, scale=ALPHA / Z_SCALE).then_inc(sig_a, 1)
                e.wait_ge(dch, i * 32 + (8 * u + 7))
                e.activation(act_hi[:, 2 * u:2 * u + 2, :], act, ACT.Copy).then_inc(ahi_a, 1)

            def item(i, n_last):
                for u in range(ITEM_UNITS):
                    if u < 4 or not n_last:
                        item_split(e, i, u + 2)
                    if u < W1_UNITS:
                        gated(i, u)
                    if u == 3 and not n_last:
                        rows_hi(i + 1)

            e.wait_ge(items_ready, 1)
            last_item = e.value_load(items_flat[0:1, W_LAST:W_LAST + 1], min_val=NE - 1, max_val=ITEMS - 1)
            e.wait_ge(t_done, 1)
            e.activation(xt_hi[:, :, 0:P], ps[:, 4:6, :].rearrange("p a (k c) -> p (a k) c", c=P), ACT.Copy, scale=X_SCALE).then_inc(xt_hd, 1)
            with e.Fori(0, last_item) as i:
                item(i, False)
            item(last_item, True)

            for t in range(T):
                e.wait_ge(f_in[t % 6], 16 * (t // 6 + 1))
                if t >= 2:
                    e.wait_ge(f_sq, t - 1)
                e.activation(xg[:, t % 2, :], fin[:, t % 6, :], ACT.Square, accum_out=ss3[:, t:t + 1]).then_inc(f_sq, 1)

        @block.vector
        def _(e):
            dve_engine[0] = e
            e.memset(cu[:, 0, 0:TAPS - 1], 0.0).then_inc(setup_d, 1)
            e.memset(cu[:, 1, 0:TAPS - 1], 0.0).then_inc(setup_d, 1)

            def u_lo_part(t):
                e.wait_ge(u_hd, t + 1)
                src = ps[:, 2 * (t % 2):2 * (t % 2) + 2, :].rearrange("p a (k c) -> p (a k) c", c=P)
                e.tensor_tensor(u_lo[:, :, t * P:(t + 1) * P], src, u_hi[:, :, t * P:(t + 1) * P], ALU.subtract).then_inc(u_ld, 1)

            for t in range(T + 1):
                if t < T:
                    e.wait_ge(x_rs, t + 1)
                    if t >= 1:
                        e.wait_ge(x_tr, t)
                    e.scalar_tensor_tensor(out=xn, in0=x_in[:, t % 2, :], scalar=rs1[:, t:t + 1], in1=g_mix,
                                           op0=ALU.mult, op1=ALU.mult).then_inc(x_nd, 1)
                if t >= 1:
                    u_lo_part(t - 1)
                if t in (3, 5, 7):
                    mixer_split(e, (3, 5, 7).index(t))

            e.wait_ge(x_sq, T)
            e.wait_ge(setup, 5)
            for c in range(CT):
                for half in range(2):
                    e.wait_ge(proj, 4 * c + 3 + half)
                    e.wait_ge(ev_a, 2 * c + half + 1)
                    e.scalar_tensor_tensor(out=cu[:, c % 2, TAPS - 1 + half * HALF:TAPS - 1 + (half + 1) * HALF],
                                           in0=ps[:, 4 + (4 * c + 2 + half) % 4, :], scalar=par["b_a"][:, c:c + 1],
                                           in1=sg[:, half, :], op0=ALU.add, op1=ALU.mult).then_inc(ev_d, 1)
                e.wait_ge(ev_d, 2 * c + 2)
                taps(e, c, tap_d)
                if c in (1, 3):
                    mixer_split(e, 3 if c == 1 else 4)
            for quad in range(2):
                e.wait_ge(proj, 27 + quad)
                e.scalar_tensor_tensor(out=v_sb[:, quad * 4:quad * 4 + 4, :],
                                       in0=ps[:, 6 + quad, :].rearrange("p (a b) -> p a b", a=4), scalar=1.0 / Z_SCALE,
                                       in1=bv_sb.unsqueeze(1).to_broadcast([P, 4, P]), op0=ALU.mult, op1=ALU.add).then_inc(ev_d, 1)
            mixer_split(e, 5)

            def centre(h):
                e.wait_ge(mean_pe, h + 1)
                for j in range(CT):
                    c = conv[:, j, h * HALF:(h + 1) * HALF]
                    e.tensor_tensor(c, c, ps[:, 7 - h, :], ALU.subtract).then_inc(sub_d, 1)

            def row_max(n):
                b, g = n // KV, n % KV
                lo = 0 if b else P
                e.wait_ge(sc_pe, n + 1)
                src = ps[:, 2 * (n % 2):2 * (n % 2) + 2, :].rearrange("p a (j c) -> p (a j) c", j=2)
                if n >= 2:
                    e.wait_ge(exp_a, 5 * (n - 1))
                e.tensor_reduce(mxs[:, n % 2, :], src[:, :, lo:2 * P], AXX, ALU.max).then_inc(mx_d, 1)
                e.wait_ge(mx_d, n + 1)
                e.scalar_tensor_tensor(out=nm[:, n % 2, :], in0=mxs[:, n % 2, :], scalar=-SCORE_SCALE,
                                       in1=neg_sinks[:, g * GROUP:(g + 1) * GROUP], op0=ALU.mult, op1=ALU.min).then_inc(nm_d, 1)
                e.wait_ge(nm_d, n + 1)
                e.tensor_tensor(dsk[:, n % 2, :], nm[:, n % 2, :], par["sinks"][:, g * GROUP:(g + 1) * GROUP], ALU.add).then_inc(dsk_d, 1)

            def plus_eps(src_done, k, bank, h, done):
                e.wait_ge(src_done, k)
                e.tensor_scalar(rs[:, h, :], ps[:, bank, :], EPS, None, ALU.add).then_inc(done, 1)

            def inverse(h, k):
                e.wait_ge(root_a, k)
                e.reciprocal(rs[:, h, :], rs[:, h, :]).then_inc(rstd_d, 1)
                e.wait_ge(rstd_d, k)

            def ln_and_swish(h):
                for j in range(CT):
                    c = conv[:, j, h * HALF:(h + 1) * HALF]
                    e.tensor_tensor(c, c, rs[:, h, :], ALU.mult).then_inc(y_d, 1)
                for j in range(CT):
                    c = conv[:, j, h * HALF:(h + 1) * HALF]
                    e.wait_ge(z_p, CT * h + j + 1)
                    e.tensor_tensor(c, c, sq[:, j, :], ALU.mult).then_inc(s_d, 1)

            def branch_norm(i):
                h = i % 2
                plus_eps(ms_pe, i + 1, 7, h, mse_d)
                inverse(h, 3 + i)
                name = "g_conv" if i < 2 else "g_attn"
                for j in range(CT):
                    c = conv[:, j, h * HALF:(h + 1) * HALF] if i < 2 else heads[h][:, j, :]
                    e.scalar_tensor_tensor(out=c, in0=c, scalar=par[name][:, j:j + 1], in1=rs[:, h, :],
                                           op0=ALU.mult, op1=ALU.mult).then_inc(m_d, 1)

            centre(0)
            row_max(0)
            centre(1)
            row_max(1)
            for h in range(2):
                plus_eps(var_pe, h + 1, 7 - h, h, ve_d)
            for h in range(2):
                inverse(h, h + 1)
            for n in range(2 * T):
                e.wait_ge(exp_a, 5 * (n + 1))
                if n >= 2:
                    e.wait_ge(pn_p, 4 * (n - 1))
                e.tensor_tensor(rden[:, n % 2, :], rsum[:, n % 2, :], esum[:, n % 2, :], ALU.add).then_inc(den_d, 1)
                e.wait_ge(den_d, n + 1)
                e.reciprocal(rden[:, n % 2, :], rden[:, n % 2, :]).then_inc(rden_d, 1)
                e.wait_ge(pt_pe, n + 1)
                if n >= 1:
                    e.wait_ge(ot_pe, n)
                if n < 2:
                    e.memset(prob_t[:, 0, 0:2], 0.0).then_inc(ptd, 1)
                    e.wait_ge(ptd, n + 1)
                else:
                    e.tensor_copy(prob_t[:, 0, :], ps[:, 4, :]).then_inc(ptd, 1)
                if n + 2 < 2 * T:
                    row_max(n + 2)
                if n == 0:
                    ln_and_swish(0)
                if n == 2:
                    branch_norm(0)
                    ln_and_swish(1)
                if n == 4:
                    branch_norm(1)
                if n == 10:
                    branch_norm(2)
            branch_norm(3)
            mixer_split(e, 6)

            def residual(t):
                e.wait_ge(out_pe, 2 * (t + 1))
                e.wait_ge(xb_p, t + 1)
                c = xr[:, t % 4, :]
                e.scalar_tensor_tensor(out=c, in0=ps[:, 2 * (t % 2):2 * (t % 2) + 2, :].rearrange("p a b -> p (a b)"),
                                       scalar=1.0 / Z_SCALE, in1=c, op0=ALU.mult, op1=ALU.add).then_inc(x2_d, 1)

            def normed(t):
                e.wait_ge(rs2_p, t + 1)
                e.scalar_tensor_tensor(out=h_sb[:, t % 2, :], in0=xr[:, t % 4, :], scalar=rs2[:, t:t + 1], in1=g_ffn,
                                       op0=ALU.mult, op1=ALU.mult).then_inc(h_d, 1)

            def h_low(t):
                e.wait_ge(hth, t + 1)
                src = ps[:, 4:6, :].rearrange("p a (k c) -> p (a k) c", c=P)
                e.scalar_tensor_tensor(out=ht_lo, in0=src, scalar=X_SCALE, in1=ht_hi, op0=ALU.mult, op1=ALU.subtract).then_inc(htl, 1)

            def route(t):
                k = 11 * t

                def step(ins, n):
                    ins.then_inc(ra, 1)
                    e.wait_ge(ra, k + n)
                e.wait_ge(rt_pe, t + 1)
                step(e.scalar_tensor_tensor(out=lg, in0=ps[:, 6, 0:NE], scalar=1.0 / Z_SCALE, in1=br_sb, op0=ALU.mult, op1=ALU.add), 1)
                step(e.max(mx8, lg), 2)
                step(e.max_index(ix8, mx8, lg), 3)
                step(e.tensor_copy(ixf, ix8[:, 0:TOPK]), 4)
                step(e.tensor_scalar(nm0, mx8[:, 0:1], -1.0, None, ALU.mult), 5)
                step(e.tensor_tensor(oh[:, t % 2, :, :], cs["iota"].unsqueeze(1).to_broadcast([P, TOPK, NE]),
                                     ixf.unsqueeze(2).to_broadcast([P, TOPK, NE]), ALU.is_equal), 6)
                with nc.allow_low_precision(reason="zeros and ones"):
                    step(e.tensor_reduce(mb[:, t, :], oh[:, t % 2, :, :].rearrange("p k e -> p e k"), AXX, ALU.add), 7)
                e.wait_ge(ea, t + 1)
                step(e.reciprocal(rse, se), 8)
                gates = pay[:, t, :].rearrange("p (k w) -> p k w", w=2)[:, :, 1].bitcast(F32)
                step(e.tensor_scalar(gates, ex, rse, None, ALU.mult), 9)
                step(e.tensor_tensor(gk, oh[:, t % 2, :, :], gates.unsqueeze(2).to_broadcast([P, TOPK, NE]), ALU.mult), 10)
                if t:
                    e.wait_ge(gt_pe, t)
                step(e.tensor_reduce(gates_g, gk.rearrange("p k e -> p e k"), AXX, ALU.add), 11)

            def place(t):
                def step(ins, n):
                    ins.then_inc(rb, 1)
                    e.wait_ge(rb, 4 * t + n)
                e.wait_ge(gt_pe, t + 1)
                step(e.tensor_tensor(posb, ps[:, 6, NE:2 * NE], cs["base"], ALU.add), 1)
                step(e.tensor_tensor(gk, oh[:, t % 2, :, :], posb.unsqueeze(1).to_broadcast([P, TOPK, NE]), ALU.mult), 2)
                step(e.tensor_reduce(slf, gk, AXX, ALU.add), 3)
                step(e.tensor_copy(slots[:, t, :], slf), 4)
                if t:
                    e.wait_ge(gb_pe, 2 * t)
                e.tensor_copy(gt_sb[0:NE, :], ps[0:NE, 6, P:2 * P]).then_inc(rc, 1)

            def add_bias(t, half):
                e.wait_ge(gb_pe, 2 * t + half + 1)
                c = xr[:, t % 4, half * HALF:(half + 1) * HALF]
                e.tensor_tensor(c, c, ps[:, 7, :], ALU.add).then_inc(acc_d, 1)

            e.wait_ge(b1_t, 1)
            for t in range(T + 3):
                if 3 <= t:
                    add_bias(t - 3, 0)
                if 1 <= t <= T:
                    h_low(t - 1)
                if 2 <= t <= T + 1:
                    place(t - 2)
                if 3 <= t:
                    add_bias(t - 3, 1)
                if t < T:
                    residual(t)
                if 1 <= t <= T:
                    route(t - 1)
                if t < T:
                    normed(t)

            def step(ins, n):
                ins.then_inc(it_d, 1)
                e.wait_ge(it_d, n)
            q = slice(0, NE)
            e.wait_ge(cnt_pe, 1)
            e.wait_ge(acc_st, 16 * T)
            step(e.tensor_copy(cnt[q], ps[q, 6, 2 * P:2 * P + 1]), 1)
            step(e.tensor_scalar(xe[q], cnt[q], float(ITEM_ROWS), None, ALU.is_gt), 2)
            step(e.scalar_tensor_tensor(out=xe[q], in0=cnt[q], scalar=2.0 * ITEM_ROWS, in1=xe[q], op0=ALU.is_gt, op1=ALU.add), 3)
            step(e.scalar_tensor_tensor(out=xe[q], in0=cnt[q], scalar=3.0 * ITEM_ROWS, in1=xe[q], op0=ALU.is_gt, op1=ALU.add), 4)
            e.wait_ge(st_pe, 1)
            step(e.tensor_copy(st[q], ps[q, 6, 2 * P + 2:2 * P + 3]), 5)
            step(e.tensor_tensor(en[q], st[q], xe[q], ALU.add), 6)
            step(e.tensor_scalar(mt[q], cs["extra"][q], st[q], None, ALU.is_ge), 7)
            step(e.scalar_tensor_tensor(out=mt[q], in0=cs["extra"][q], scalar=en[q], in1=mt[q], op0=ALU.is_lt, op1=ALU.mult), 8)
            step(e.tensor_scalar(rr[q], cs["extra"][q], st[q], 1.0, ALU.subtract, ALU.add), 9)
            step(e.tensor_scalar(itm[q, 0, NE:ITEMS], mt[q], cs["e"][q], None, ALU.mult), 10)
            step(e.tensor_copy(itm[q, 0, 0:NE], cs["item_e"][q, 0:NE]), 11)
            step(e.tensor_scalar(t1[q], rr[q], float(ITEM_ROWS), cs["e_row"][q], ALU.mult, ALU.add), 12)
            step(e.tensor_tensor(itm[q, 1, NE:ITEMS], t1[q], mt[q], ALU.mult), 13)
            step(e.tensor_copy(itm[q, 1, 0:NE], cs["item_row"][q, 0:NE]), 14)
            step(e.tensor_scalar(t1[q], rr[q], -float(ITEM_ROWS), cnt[q], ALU.mult, ALU.add), 15)
            step(e.tensor_tensor(itm[q, 2, NE:ITEMS], t1[q], mt[q], ALU.mult), 16)
            step(e.tensor_scalar(itm[q, 2, 0:NE], cs["eye"][q], cnt[q], None, ALU.mult), 17)
            step(e.tensor_scalar(itm[q, 3, :], cs["item_e"][q], 0.0, xe[q], ALU.mult, ALU.add), 18)
            e.wait_ge(row_pe, 1)
            row = ps[0:1, 7, 0:4 * ITEMS]
            step(e.tensor_copy(items_flat[0:1, 0:2 * ITEMS], row[:, 0:2 * ITEMS]), 19)
            step(e.tensor_scalar(items_flat[0:1, 2 * ITEMS:3 * ITEMS], row[:, 2 * ITEMS:3 * ITEMS], float(ITEM_ROWS), None, ALU.min), 20)
            e.tensor_scalar(items_flat[0:1, 3 * ITEMS:4 * ITEMS], row[:, 3 * ITEMS:4 * ITEMS], float(NE - 1), None, ALU.add).then_inc(items_ready, 1)
            mixer_split(e, 7)

            for a in (glu, lin, act):
                e.memset(a, 0.0).then_inc(clr, 1)
            e.wait_ge(out_pe, 2 * T)
            for a in (xt_hi, xt_lo, act_hi, act_lo, y_sb):
                e.memset(a, 0.0).then_inc(clr, 1)
            e.wait_ge(clr, 8)

            def block1_rows():
                src = ps[:, 0:2, :].rearrange("p a (k c) -> p (a k) c", c=P)
                return src

            def rows_low(i, n, first=False):
                e.wait_ge(t_done, i + 1)
                src = ps[:, 0:2, :].rearrange("p a (k c) -> p (a k) c", c=P)
                if first:
                    e.tensor_scalar(xt_hi[:, :, P:2 * P], src, X_SCALE, None, ALU.mult).then_inc(clr, 1)
                    e.wait_ge(clr, 9)
                    e.scalar_tensor_tensor(out=xt_lo[:, :, P:2 * P], in0=src, scalar=X_SCALE, in1=xt_hi[:, :, P:2 * P],
                                           op0=ALU.mult, op1=ALU.subtract)
                else:
                    after_waits(e)
                    with e.If(n > P):
                        e.tensor_scalar(xt_hi[:, :, P:2 * P], src, X_SCALE, None, ALU.mult)
                        e.drain()
                        e.scalar_tensor_tensor(out=xt_lo[:, :, P:2 * P], in0=src, scalar=X_SCALE, in1=xt_hi[:, :, P:2 * P],
                                               op0=ALU.mult, op1=ALU.subtract)
                e.wait_ge(xt_hd, i + 1)
                src = ps[:, 4:6, :] if first else ps[:, 6:8, :]
                e.scalar_tensor_tensor(out=xt_lo[:, :, 0:P], in0=src.rearrange("p a (k c) -> p (a k) c", c=P), scalar=X_SCALE,
                                       in1=xt_hi[:, :, 0:P], op0=ALU.mult, op1=ALU.subtract).then_inc(xt_ready, 1)

            def swiglu(i, u, expert, w):
                base = 8 * u
                for p in range(2):
                    bank = 2 * (u % 2) + p
                    j = 2 * u + p
                    e.tensor_scalar(glu[:, p, 0:w], ps[:, bank, 0:w], g_top[:, j, bass.ds(expert, 1)],
                                    g_add[:, j, bass.ds(expert, 1)], ALU.min, ALU.add).then_inc(dch, 1)
                    last = e.tensor_scalar(lin[:, p, 0:w], ps[:, bank, ITEM_ROWS:ITEM_ROWS + w], l_top[:, j, bass.ds(expert, 1)],
                                           l_low[:, j, bass.ds(expert, 1)], ALU.min, ALU.max).then_inc(dch, 1)
                e.wait_ge(sig_a, i * 4 + (u + 1))
                e.scalar_tensor_tensor(out=gs[:, :, 0:w], in0=glu[:, :, 0:w], scalar=X_SCALE / Z_SCALE ** 2, in1=sig[:, :, 0:w],
                                       op0=ALU.mult, op1=ALU.mult).then_inc(dch, 1)
                e.wait_ge(dch, i * 32 + (base + 5))
                for p in range(2):
                    e.scalar_tensor_tensor(out=act[:, p, 0:w], in0=lin[:, p, 0:w], scalar=l_add[:, 2 * u + p, bass.ds(expert, 1)],
                                           in1=gs[:, p, 0:w], op0=ALU.add, op1=ALU.mult).then_inc(dch, 1)
                e.wait_ge(ahi_a, i * 4 + (u + 1))
                e.tensor_tensor(act_lo[:, 2 * u:2 * u + 2, 0:w], act[:, :, 0:w], act_hi[:, 2 * u:2 * u + 2, 0:w],
                                ALU.subtract).then_inc(dch, 1)

            def item(i, n_last):
                n = e.value_load(items_flat[0:1, bass.ds(i + 2 * ITEMS, 1)], min_val=0, max_val=ITEM_ROWS)
                expert = e.value_load(items_flat[0:1, bass.ds(i, 1)], min_val=0, max_val=NE - 1)
                for u in range(ITEM_UNITS):
                    if u < 4 or not n_last:
                        item_split(e, i, u + 2)
                    e.wait_ge(used, i * ITEM_UNITS + (u + 1))
                    if u < W1_UNITS:
                        e.wait_ge(dch, i * 32 + 8 * u)
                        after_waits(e)
                        with e.If(n > P):
                            swiglu(i, u, expert, ITEM_ROWS)
                        with e.Else():
                            swiglu(i, u, expert, P)
                        e.engine_nop().then_inc(zfree, 1)
                        e.engine_nop().then_inc(act_done, 1)
                        if u == 3 and not n_last:
                            n_next = e.value_load(items_flat[0:1, bass.ds(i + (2 * ITEMS + 1), 1)], min_val=0, max_val=ITEM_ROWS)
                            rows_low(i + 1, n_next)
                    else:
                        half = u - W1_UNITS
                        if half == 0:
                            e.wait_ge(ysc[0], i * 16)
                            e.wait_ge(ysc[1], i * 16)
                        after_waits(e)
                        gate = [idx_all[:, bass.ds(i, 1), blk, 1].bitcast(F32) for blk in range(2)]
                        with e.If(n > P):
                            e.tensor_scalar(y_sb[:, 1, half * HALF:(half + 1) * HALF], ps[:, 5 + 2 * half, :], gate[1], 1.0 / Z_SCALE, ALU.mult, ALU.mult)
                        e.tensor_scalar(y_sb[:, 0, half * HALF:(half + 1) * HALF], ps[:, 4 + 2 * half, :], gate[0], 1.0 / Z_SCALE,
                                        ALU.mult, ALU.mult).then_inc(yd, 1)

            e.wait_ge(items_ready, 1)
            last_item = e.value_load(items_flat[0:1, W_LAST:W_LAST + 1], min_val=NE - 1, max_val=ITEMS - 1)
            e.engine_nop().then_inc(zfree, 2)
            rows_low(0, None, first=True)
            e.wait_ge(idx_in, 32)
            with e.Fori(0, last_item) as i:
                item(i, False)
            item(last_item, True)

            e.wait_ge(gf_in, 16)
            for t in range(T):
                e.wait_ge(f_rs, t + 2)
                e.scalar_tensor_tensor(out=fin[:, t % 6, :], in0=fin[:, t % 6, :], scalar=rs3[:, t:t + 1], in1=g_final,
                                       op0=ALU.mult, op1=ALU.mult).then_inc(f_d, 1)

        @block.gpsimd
        def _(e):
            pool_engine[0] = e
            e.wait_ge(c_in, N_CONST_DMAS)
            e.wait_ge(g_in, 16)
            e.tensor_scalar(g_mix, g_mix, OUT_SCALE, 0.0, ALU.mult, ALU.add).then_inc(setup, 1)
            e.tensor_scalar(par["b_a"], par["b_a"], Z_SCALE, 0.0, ALU.mult, ALU.add).then_inc(setup, 1)
            e.tensor_scalar(par["w_dw"], par["w_dw"], 1.0 / Z_SCALE, 0.0, ALU.mult, ALU.add).then_inc(setup, 1)
            gains = pr[:, PARAMS["g_attn"][0]:PARAMS["g_conv"][1]]
            e.tensor_scalar(gains, gains, X_SCALE, 0.0, ALU.mult, ALU.add).then_inc(setup, 1)
            e.tensor_scalar(neg_sinks, par["sinks"], -1.0, 0.0, ALU.mult, ALU.add).then_inc(setup, 1)

            def rstd(dst, src, k):
                e.tensor_scalar(dst, src, D * EPS, 0.0, ALU.add, ALU.add).then_inc(eps_p, 1)
                e.wait_ge(eps_p, k)
                return e.tensor_tensor(dst, dst, cs["power"], ALU.pow)

            for t in range(T):
                e.wait_ge(x_sq, t + 1)
                if t == 0:
                    e.wait_ge(setup, 1)
                rstd(rs1[:, t:t + 1], ss1[:, t:t + 1], t + 1).then_inc(x_rs, 1)
                if t in (3, 5, 7):
                    mixer_split(e, (3, 5, 7).index(t))
            e.tensor_copy(ident_b, cs["ident"]).then_inc(setup, 1)
            e.tensor_copy(before_b, cs["before"]).then_inc(setup, 1)
            e.tensor_copy(ones_b, cs["ones"]).then_inc(setup, 1)
            e.tensor_copy(band_b, band_f).then_inc(setup, 1)
            e.tensor_scalar(mean_w, cs["ones"], 1.0 / CW, 0.0, ALU.mult, ALU.add).then_inc(setup, 1)
            for u in range(3, MIX_UNITS):
                mixer_split(e, u)

            def affine(h):
                for j in range(CT):
                    c = conv[:, j, h * HALF:(h + 1) * HALF]
                    e.wait_ge(sgm_a, CT * h + j + 1)
                    e.tensor_scalar(c, c, par["ln_g"][:, j:j + 1], par["ln_b"][:, j:j + 1], ALU.mult, ALU.add).then_inc(z_p, 1)

            def mixed_lo(i):
                h = i % 2
                for j in range(CT):
                    src = conv[:, j, h * HALF:(h + 1) * HALF] if i < 2 else heads[h][:, j, :]
                    at = j + (CT if i < 2 else 0)
                    e.wait_ge(mhi_a, CT * i + j + 1)
                    e.tensor_tensor(mix_lo[:, at, h * HALF:(h + 1) * HALF], src, mix_hi[:, at, h * HALF:(h + 1) * HALF],
                                    ALU.subtract).then_inc(mlo_p, 1)

            for n in range(2 * T):
                lo = 0 if n // KV else P
                e.wait_ge(rden_d, n + 1)
                for j in range(GROUP):
                    pj = prob[:, n % 2, j, lo:2 * P]
                    e.tensor_scalar(pj, pj, rden[:, n % 2, j:j + 1], 0.0, ALU.mult, ALU.add).then_inc(pn_p, 1)
                if n == 0:
                    affine(0)
                if n == 2:
                    mixed_lo(0)
                    affine(1)
                if n == 4:
                    mixed_lo(1)
                if n == 10:
                    mixed_lo(2)
            mixed_lo(3)
            mixer_split(e, 6)

            e.wait_ge(r_in, 64)
            e.tensor_scalar(g_ffn, g_ffn, D ** 0.5, 0.0, ALU.mult, ALU.add).then_inc(setup, 1)
            e.tensor_scalar(wr_hi.rearrange("p a b -> p (a b)"), wr, W_SCALE, 0.0, ALU.mult, ALU.add).then_inc(setup, 1)
            e.wait_ge(setup, 12)
            token = pay.rearrange("p t (k w) -> p t k w", w=2)
            e.tensor_copy(token[:, :, :, 0], cs["token"].unsqueeze(2).to_broadcast([P, T, TOPK])).then_inc(setup, 1)
            e.tensor_scalar(wr, wr, W_SCALE, 0.0, ALU.mult, ALU.add).then_inc(setup, 1)
            e.wait_ge(setup, 14)
            e.tensor_tensor(wr_lo.rearrange("p a b -> p (a b)"), wr, wr_hi.rearrange("p a b -> p (a b)"), ALU.subtract).then_inc(b1_t, 1)

            def residual_bias(t):
                e.wait_ge(xr_s[t % 4], 16 * (t // 4 + 1))
                c = xr[:, t % 4, :]
                e.tensor_tensor(c, c, b_out, ALU.add).then_inc(xb_p, 1)

            def store_slots(t):
                e.wait_ge(rb, 4 * (t + 1))
                if t == 0:
                    e.wait_ge(init, 48)
                for k in range(TOPK):
                    e.indirect_dma_start(table, bass.IndirectOffsetOnAxis(ap=slots[:, t, k:k + 1], axis=0),
                                         pay[:, t, 2 * k:2 * k + 2], None).then_inc(scat, 16)
                    e.wait_ge(scat, 16 * (4 * t + k + 1))

            residual_bias(0)
            for t in range(T + 2):
                if t + 1 < T:
                    residual_bias(t + 1)
                if t < T:
                    e.wait_ge(x2sq, t + 1)
                    rstd(rs2[:, t:t + 1], ss2[:, t:t + 1], T + t + 1).then_inc(rs2_p, 1)
                if t == 1:
                    e.wait_ge(b1_in, 16)
                    bg, bl = b1_sb[:, 0:KC, :], b1_sb[:, KC:2 * KC, :]
                    e.tensor_scalar(g_top, bg, -Z_SCALE, LIMIT * Z_SCALE, ALU.mult, ALU.add).then_inc(b1_t, 1)
                    e.tensor_scalar(g_add, bg, Z_SCALE, 0.0, ALU.mult, ALU.add).then_inc(b1_t, 1)
                    e.tensor_scalar(l_top, bl, -Z_SCALE, LIMIT * Z_SCALE, ALU.mult, ALU.add).then_inc(b1_t, 1)
                    e.tensor_scalar(l_low, bl, -Z_SCALE, -LIMIT * Z_SCALE, ALU.mult, ALU.add).then_inc(b1_t, 1)
                    e.tensor_scalar(l_add, bl, Z_SCALE, Z_SCALE, ALU.mult, ALU.add).then_inc(b1_t, 1)
                if t >= 2:
                    store_slots(t - 2)

            def list_of(k, row, done):
                src = table[bass.ds(row, ITEM_ROWS), :].rearrange("(b p) w -> p b w", p=P)
                e.dma_start(idx_all[:, bass.ds(k, 1), :, :].rearrange("p a b w -> p (a b) w"), src).then_inc(done, 16)

            src = table.rearrange("(x s p) w -> p x s w", p=P, s=SEQ // P)
            for blk in range(2):
                e.dma_start(idx_all[:, 0:NE, blk, :], src[:, :, blk, :]).then_inc(idx_in, 16)
            e.wait_ge(items_ready, 1)
            last_item = e.value_load(items_flat[0:1, W_LAST:W_LAST + 1], min_val=NE - 1, max_val=ITEMS - 1)
            e.wait_ge(idx_in, 32)
            with e.If(last_item > NE - 1):
                with e.Fori(NE, last_item + 1) as k:
                    row = e.value_load(items_flat[0:1, bass.ds(k + ITEMS, 1)], min_val=0, max_val=(NE - 1) * SEQ + 3 * ITEM_ROWS)
                    list_of(k, row, idx_in)
                    e.wait_ge(idx_in, (k - NE) * 16 + 48)
            e.nop()

            def gather(blk, rows=P):
                e.indirect_dma_start(xg[0:rows, blk, :], None, h_rows, bass.IndirectOffsetOnAxis(ap=idx_g[0:rows, blk, 0:1], axis=0)).then_inc(xg_in[blk], 16)

            def scatter(blk, rows=P):
                e.indirect_dma_start(y_rows, bass.IndirectOffsetOnAxis(ap=idx_s[0:rows, blk, 0:1], axis=0), y_sb[0:rows, blk, :], None,
                                     compute_op=ALU.add).then_inc(ysc[blk], 16)

            def fetch_rows(k, n=None):
                e.tensor_copy(idx_g.rearrange("p a b -> p (a b)"), idx_all[:, bass.ds(k, 1), :, :].rearrange("p a b w -> p (a b w)")).then_inc(ig, 1)
                e.wait_ge(ig, k + 1)
                after_waits(e)
                gather(0)
                if n is None:
                    gather(1)
                else:
                    with e.If(n > P):
                        gather(1)
                    with e.Else():
                        gather(1, FEW)

            def item(i, n_last):
                n = e.value_load(items_flat[0:1, bass.ds(i + 2 * ITEMS, 1)], min_val=0, max_val=ITEM_ROWS)
                if not n_last:
                    n_next = e.value_load(items_flat[0:1, bass.ds(i + (2 * ITEMS + 1), 1)], min_val=0, max_val=ITEM_ROWS)
                    e.wait_ge(t_done, i + 1)
                    after_waits(e)
                    fetch_rows(i + 1, n_next)
                for u in range(ITEM_UNITS):
                    if u < 4 or not n_last:
                        item_split(e, i, u + 2)
                e.wait_ge(ysc[0], i * 16)
                e.wait_ge(ysc[1], i * 16)
                after_waits(e)
                e.tensor_copy(idx_s.rearrange("p a b -> p (a b)"), idx_all[:, bass.ds(i, 1), :, :].rearrange("p a b w -> p (a b w)")).then_inc(is_, 1)
                e.wait_ge(is_, i + 1)
                e.wait_ge(yd, i * 2 + 2)
                after_waits(e)
                scatter(0)
                with e.If(n > P):
                    scatter(1)
                with e.Else():
                    scatter(1, FEW)

            e.wait_ge(h_st, 16 * T)
            e.wait_ge(out_pe, 2 * T)
            fetch_rows(0)
            mixer_split(e, 7)
            with e.Fori(0, last_item) as i:
                item(i, False)
            item(last_item, True)

            e.wait_ge(gf_in, 16)
            e.tensor_scalar(g_final, g_final, D ** 0.5, 0.0, ALU.mult, ALU.add).then_inc(f_rs, 1)
            for t in range(T):
                e.wait_ge(f_sq, t + 1)
                rstd(rs3[:, t:t + 1], ss3[:, t:t + 1], 2 * T + t + 1).then_inc(f_rs, 1)


def _constants(np):
    c = np.zeros((P, N_CONSTS), np.float32)

    def put(name, a):
        lo, hi = CONSTS[name]
        c[:a.shape[0], lo:hi] = a
    r = np.arange(P)
    put("ident", np.eye(P))
    put("before", r[:, None] < r[None, :])
    put("ones", np.ones((P, P)))
    ahead = np.arange(2 * P)[None, :] - r[:, None]
    put("band", np.where((ahead >= 1) & (ahead <= P), 0.0, -1e30))
    put("iota", np.tile(np.arange(NE), (P, 1)))
    put("base", np.tile(np.arange(NE) * SEQ, (P, 1)))
    put("token", r[:, None] + P * np.arange(T)[None, :])
    ne = np.arange(NE)
    e_of = np.zeros((NE, ITEMS))
    e_of[ne, ne] = ne
    put("item_e", e_of)
    put("item_row", e_of * SEQ)
    put("eye", np.eye(NE))
    put("extra", np.tile(np.arange(EXTRA), (P, 1)))
    put("power", np.full((P, 1), -0.5))
    put("e", ne[:, None])
    put("e_row", ne[:, None] * SEQ)
    slot = np.arange(NE * SEQ)
    table = np.stack([SEQ + slot % SPARE, 0 * slot], axis=1).astype(np.uint32)
    return c, table


def kernel(**inputs):
    import numpy as np
    import concourse.bacc as bacc
    from concourse.bass_utils import run_bass_kernel_spmd as run

    a = {k: np.asarray(v) for k, v in inputs.items()}
    w_in, w_out, w1, w2 = a["w_in"][0], a["w_out"][0], a["w1"][0], a["w2"][0]
    att, kvw = HEADS * HD, KV * HD

    def chunks(w):
        return w.reshape(w.shape[0] // P, P, w.shape[1]).transpose(1, 0, 2)

    order = np.arange(att).reshape(KV, GROUP, HD).transpose(1, 0, 2).reshape(-1)
    conv_a, gate = w_in[:, att + 2 * kvw:att + 2 * kvw + CW], w_in[:, att + 2 * kvw + CW:]
    glu_cols = [np.concatenate([m[:, c * P:(c + 1) * P] for c in (2 * i, 2 * i + 1) for m in (gate, conv_a)], axis=1) for i in range(2)]
    q_cols = w_in[:, :att][:, order]
    wo = np.concatenate([w_out[:att][order], w_out[att:]], axis=0)
    units = [chunks(m) for m in (glu_cols[0], glu_cols[1], q_cols, wo[:, :HALF], wo[:, HALF:])]
    up = w1.reshape(NE, KC, P, W1_UNITS, 2, P, 2).transpose(0, 3, 2, 1, 4, 6, 5).reshape(NE, W1_UNITS, P, UNIT)
    down = w2.reshape(NE, KC, P, W2_UNITS, HALF).transpose(0, 3, 2, 1, 4).reshape(NE, W2_UNITS, P, UNIT)
    experts = np.concatenate([up, down], axis=1).reshape(NE * ITEM_UNITS, P, UNIT)
    w_units = np.concatenate([np.stack([u.reshape(P, UNIT) for u in units]), experts], axis=0)
    w_kv = np.ascontiguousarray(chunks(w_in[:, att:att + 2 * kvw]).reshape(P, KV_UNIT))

    def cols(v):
        return v.reshape(-1, P).T
    b_in = a["b_in"][0]
    b_conv, b_gate = b_in[att + 2 * kvw:att + 2 * kvw + CW], b_in[att + 2 * kvw + CW:]
    params = np.concatenate([
        cols(b_gate), cols(b_conv), cols(b_in[:att][order]), cols(b_in[att:att + kvw]),
        a["w_dw"][0].reshape(TAPS, CT, P).transpose(2, 1, 0).reshape(P, CT * TAPS), cols(a["b_dw"][0]),
        cols(a["ln_g"][0]), cols(a["ln_b"][0]), cols(a["g_attn_out"][0][order]), cols(a["g_conv_out"][0]),
        np.broadcast_to(a["sinks"][0], (P, HEADS))], axis=1)
    rows = np.stack([np.broadcast_to(v, (P, D)) for v in (a["g_mix"][0], a["b_out"][0], a["g_ffn"][0], a["g_final"])])
    b1 = a["b1"][0].reshape(NE, KC, P, 2).transpose(2, 3, 1, 0).reshape(P, 2 * KC * NE)
    w_router = chunks(a["w_router"][0]).reshape(P, KC * NE)
    consts, table0 = _constants(np)
    arrays = {
        "x": a["x"][0], "w_units": w_units, "w_kv": w_kv, "params": params, "rows": rows,
        "b_v": np.broadcast_to(b_in[att + kvw:att + 2 * kvw], (P, P)), "b_router": np.broadcast_to(a["b_router"][0], (P, NE)),
        "w_router": w_router, "b1": b1, "b2": a["b2"][0], "consts": consts, "table0": table0,
        "zeros": np.zeros((SPARE, D), np.float32),
    }
    arrays = {f"in_{k}": np.ascontiguousarray(v) for k, v in arrays.items()}
    nc = bacc.Bacc("TRN2", target_bir_lowering=False, num_devices=1)
    args = [nc.dram_tensor(k, v.shape, mybir.dt.from_np(v.dtype), kind="ExternalInput").ap() for k, v in arrays.items()]
    out = nc.dram_tensor("out", (SEQ, D), F32, kind="ExternalOutput").ap()
    hymba_layer_kernel(nc, *args, out)
    r = run(nc, [arrays], core_ids=[0])
    return r.results[0]["out"].reshape(1, SEQ, D)
```

```python
import concourse.bass as bass
from concourse import mybir
from contextlib import ExitStack

F32 = mybir.dt.float32
F16 = mybir.dt.float16
BF16 = mybir.dt.bfloat16
U32 = mybir.dt.uint32
I32 = mybir.dt.int32
ALU = mybir.AluOpType
ACT = mybir.ActivationFunctionType
AXX = mybir.AxisListType.X

P = 128
SEQ = 1024
D = 1024
T = SEQ // P
KC = D // P
HEADS, KV, HD = 8, 2, 64
GROUP = HEADS // KV
CW = 512
CT = CW // P
TAPS = 31
NE, TOPK = 32, 4
HALF = 512
UNIT = KC * HALF
KV_UNIT = KC * 256
RING = 3
MIX_UNITS = 6
W1_UNITS, W2_UNITS = 4, 2
ITEM_UNITS = W1_UNITS + W2_UNITS
ITEM_ROWS = 256
WIDTHS = (64, 96, 128, 160, 192, 224, 256)
ITEMS = NE + SEQ * TOPK // ITEM_ROWS
EXTRA = ITEMS - NE
DVE_TOKENS = 832
GLU_EVERY = 18
XR = 6
FEW = 16
SPARE = ITEM_ROWS
DVE_SPLIT = 2304
W_SCALE, X_SCALE = 64.0, 16.0
Z_SCALE = W_SCALE * X_SCALE
LIMIT, ALPHA = 7.0, 1.702
EPS = 1e-5
SCORE_SCALE = HD ** -0.5
OUT_SCALE = X_SCALE * D ** 0.5

PARAMS = {}
_at = 0
for _name, _n in (("b_gate", CT), ("b_a", CT), ("b_q", GROUP), ("b_k", 1), ("w_dw", CT * TAPS), ("b_dw", CT),
                  ("ln_g", CT), ("ln_b", CT), ("g_attn", CT), ("g_conv", CT), ("sinks", HEADS)):
    PARAMS[_name] = (_at, _at + _n)
    _at += _n
N_PARAMS = _at
CONSTS = {}
_at = 0
for _name, _n in (("ident", P), ("before", P), ("ones", P), ("iota", NE), ("base", NE),
                  ("token", T), ("item_e", ITEMS), ("item_row", ITEMS), ("eye", NE), ("extra", EXTRA), ("e", 1), ("e_row", 1), ("power", 1),
                  ("band", 2 * P)):
    CONSTS[_name] = (_at, _at + _n)
    _at += _n
N_CONSTS = _at


def hymba_layer_kernel(nc, x, w_units, w_kv, params, rows, b_v, b_router, w_router, b1, b2, consts, table0, zeros, out):
    h_rows = nc.dram_tensor("h_rows", (SEQ + SPARE, D), F32, kind="Internal").ap()
    y_rows = nc.dram_tensor("y_rows", (SEQ + SPARE, D), F32, kind="Internal").ap()
    table = nc.dram_tensor("slot_table", (NE * SEQ, 2), U32, kind="Internal").ap()

    ctx = ExitStack()
    with ctx:
        def sem(name):
            return ctx.enter_context(nc.semaphore(name))

        raw = ctx.enter_context(nc.sbuf_tensor("raw", [P, RING, UNIT], F32))
        whi = ctx.enter_context(nc.sbuf_tensor("whi", [P, RING, UNIT], F16))
        wlo = ctx.enter_context(nc.sbuf_tensor("wlo", [P, RING, UNIT], F16))
        KB = 256
        arena = ctx.enter_context(nc.sbuf_tensor("arena", [P, 111 * KB + 192], F32))
        ps = ctx.enter_context(nc.psum_tensor("ps", [P, 8, HALF], F32))

        def view(word, shape, dt=F32):
            n = 1
            for s in shape:
                n *= s
            words = n * (4 if dt in (F32, U32, I32) else 2) // 4
            v = arena[:, int(word):int(word) + words]
            if dt != F32:
                v = v.bitcast(dt)
            if len(shape) == 2:
                v = v.rearrange("p (a b) -> p a b", a=shape[0])
            if len(shape) == 3:
                v = v.rearrange("p (a b c) -> p a b c", a=shape[0], b=shape[1])
            return v

        A, B, C, DD, G, E, K = 0, 32 * KB, 56 * KB, 65 * KB, 81 * KB, 93 * KB, 101 * KB
        u_hi = view(A, (KC, SEQ), F16)
        u_lo = view(A + 16 * KB, (KC, SEQ), F16)
        q_t = view(B, (GROUP, SEQ))
        k_t = view(B + 16 * KB, (SEQ,))
        v_sb = view(B + 20 * KB, (T, P))
        cu = [view(C, (TAPS - 1 + SEQ,)), view(C + TAPS - 1 + SEQ, (TAPS - 1 + SEQ,)),
              view(G, (TAPS - 1 + SEQ,)), view(G + TAPS - 1 + SEQ, (TAPS - 1 + SEQ,))]
        conv = view(DD, (CT, SEQ))
        tap_part = view(G + 2 * (TAPS - 1 + SEQ), (2, SEQ - DVE_TOKENS))
        x_in = view(G, (2, D))
        xn = view(G + 8 * KB, (D,))
        g_mix = view(E, (D,))
        band_f = view(E + 4 * KB, (2 * P,))
        sg = view(E, (2, HALF))
        mix_hi = view(A, (2 * CT, SEQ), F16)
        mix_lo = view(A + 16 * KB, (2 * CT, SEQ), F16)
        prob = view(G, (2, GROUP, 2 * P))
        prob_t = view(G + 8 * KB, (2, HALF))
        sq = view(E, (CT, HALF))
        heads = [view(C, (CT, HALF)), view(DD, (CT, HALF))]
        xr = view(B, (XR, D))
        h_sb = view(DD, (2, D))
        b_out = view(G, (D,))
        g_ffn = view(G + 4 * KB, (D,))
        ht_hi = view(G + 8 * KB, (KC, P), F16)
        ht_lo = view(G + 10 * KB, (KC, P), F16)
        b2_sb = view(E, (D,))
        wr = view(E + 4 * KB, (KC * NE,))
        wr_hi = view(E + 5 * KB, (KC, NE), F16)
        wr_lo = view(E + 5.5 * KB, (KC, NE), F16)
        xg = view(A, (2, D))
        xt_hi = view(A + 8 * KB, (KC, ITEM_ROWS), F16)
        xt_lo = view(A + 12 * KB, (KC, ITEM_ROWS), F16)
        act_hi = view(A + 16 * KB, (KC, ITEM_ROWS), F16)
        act_lo = view(A + 20 * KB, (KC, ITEM_ROWS), F16)
        y_sb = view(A + 24 * KB, (2, D))
        b1_sb = view(C, (2 * KC, NE))
        g_top = view(C + 2 * KB, (KC, NE))
        g_add = view(C + 3 * KB, (KC, NE))
        l_top = view(C + 4 * KB, (KC, NE))
        l_low = view(C + 5 * KB, (KC, NE))
        l_add = view(C + 6 * KB, (KC, NE))
        glu = view(DD, (2, ITEM_ROWS))
        lin = view(DD + 2 * KB, (2, ITEM_ROWS))
        sig = view(DD + 4 * KB, (2, ITEM_ROWS))
        gs = view(DD + 6 * KB, (2, ITEM_ROWS))
        act = view(DD + 8 * KB, (2, ITEM_ROWS))
        idx_all = view(DD + 10 * KB, (ITEMS, 2, 2), U32)
        idx_g = view(DD + 11 * KB, (2, 2), U32)
        idx_s = view(DD + 11 * KB + 4, (2, 2), U32)
        fin = view(B, (6, D))
        g_final = view(G, (D,))
        kat = [K]

        def small(shape, dt=F32):
            n = 1
            for s in shape:
                n *= s
            w = kat[0]
            kat[0] += (n * (4 if dt in (F32, U32, I32) else 2) + 7) // 8 * 2
            assert kat[0] <= 111 * KB + 192
            return view(w, shape, dt)

        cs = {}
        cs_all = small((CONSTS["band"][0],))
        for name, (a, b) in CONSTS.items():
            if name != "band":
                cs[name] = cs_all[:, a:b]
        pr = small((N_PARAMS,))
        par = {name: pr[:, a:b] for name, (a, b) in PARAMS.items()}
        ident_b = small((P,), BF16)
        before_b = small((P,), BF16)
        ones_b = small((P,), BF16)
        band_b = small((2 * P,), BF16)
        mean_w = small((P,))
        rs = small((2, HALF))
        neg_sinks = small((HEADS,))
        ss1, rs1, ss2, rs2, ss3, rs3 = (small((T,)) for _ in range(6))
        nm, dsk, rsum, esum, rden, mxs = (small((2, GROUP)) for _ in range(6))
        bv_sb = view(E + 6 * KB, (P,))
        br_sb = small((NE,))
        lg = small((NE,))
        mx8 = small((8,))
        ix8 = small((8,), U32)
        ixf = small((TOPK,))
        nm0 = small((1,))
        ex = small((TOPK,))
        se = small((1,))
        rse = small((1,))
        oh = view(E + 6 * KB, (2, TOPK, NE))
        gk = view(E + 7 * KB, (TOPK, NE))
        gates_g = small((NE,))
        posb = small((NE,))
        slf = small((TOPK,))
        slots = view(DD + 13 * KB, (T, TOPK), U32)
        pay = view(DD + 13 * KB + 32, (T, TOPK * 2), U32)
        mb = view(DD + 13 * KB + 96, (T, NE), BF16)
        gt_sb = view(E + 7.5 * KB, (P,))
        cnt, xe, st, en = (small((1,)) for _ in range(4))
        itm = view(DD + 14 * KB, (4, ITEMS))
        mt, rr, t1 = (view(DD + 15 * KB + 64 * i, (EXTRA,)) for i in range(3))
        items = view(DD + 12 * KB, (4, ITEMS), I32)

        W_LAST = 3 * ITEMS

        raw_full = [sem(f"raw_full{s}") for s in range(RING)]
        hi_done, lo_dve, lo_pool, raw_scaled = sem("hi_done"), sem("lo_dve"), sem("lo_pool"), sem("raw_scaled_pool")
        c_in, g_in, xin = sem("consts_loaded"), sem("g_mix_loaded"), [sem("x_loaded0"), sem("x_loaded1")]
        step_pool, step_dve = sem("waits_passed_pool"), sem("waits_passed_dve")
        setup, eps_p = sem("setup_pool"), sem("eps_added")
        setup_d = sem("setup_dve")
        x_sq, x_rs, x_nd, x_tr, u_hd, u_ld = (sem(n) for n in ("x_squared", "x_rstd", "x_normed", "x_transposed", "u_hi_done", "u_lo_done"))
        proj, ev_a, ev_d = sem("proj_done"), sem("proj_read_act"), sem("proj_read_dve")
        tap_d, tap_p, tap_m = sem("taps_dve"), sem("taps_pool"), sem("tap_products_pool")
        mean_pe, sub_d, vsq_a, var_pe, ve_d, root_a, rstd_d = (sem(n) for n in ("mean_done", "centred", "centred_squared", "var_done", "var_copied", "root_done", "rstd_done"))
        y_d, sgm_a, z_p, s_d, csq_a, ms_pe, mse_d, m_d, mhi_a, mlo_p = (sem(n) for n in (
            "ln_scaled", "swish_sigmoid", "ln_affine", "swish_done", "branch_squared", "meansq_done", "meansq_copied", "branch_normed", "mix_hi_done", "mix_lo_done"))
        sc_pe, mx_d, nm_d, dsk_d, exp_a, den_d, rden_d, pn_p, pt_pe, pta, ptd, ot_pe, og_a = (sem(n) for n in (
            "scores_done", "row_max", "neg_max", "sink_shift", "exp_done", "denominator", "rden", "probs_normed", "probs_transposed", "prob_t_act", "prob_t_dve", "heads_done", "heads_read"))
        r_in, xr_in, xb_p, out_pe, x2_d, x2sq, rs2_p, h_d, tr_pe, hth, htl = (sem(n) for n in (
            "route_consts", "xr_loaded", "xb_done", "out_done", "x2_done", "x2_squared", "x2_rstd", "h_done", "h_transposed", "ht_hi_done", "ht_lo_done"))
        h_st, acc_st = [sem(f"h_stored{i}") for i in range(2)], [sem(f"acc_stored{i}") for i in range(XR)]
        xr_s = [sem(f"xr_loaded{i}") for i in range(XR)]
        rt_pe, ra, ea, gt_pe, rc, gb_pe, acc_d, scat = (sem(n) for n in (
            "router_done", "route_step", "gate_exp", "gates_transposed", "gates_t_copied", "gate_bias_done", "acc_done", "slots_stored"))
        rb = sem("slot_step")
        init = sem("tables_initialised")
        cnt_pe, it_d, st_pe, row_pe, items_ready = (sem(n) for n in ("counts_done", "item_step", "starts_done", "item_rows_done", "items_ready"))
        b1_in, b1_t, idx_in, lists_ready, clr = sem("b1_loaded"), sem("b1_tables"), sem("lists_loaded"), sem("lists_ready"), sem("expert_cleared")
        used, xt_ready, xt_hd, t_done = (sem(n) for n in ("units_used", "xt_ready", "xt_hi_done", "rows_transposed"))
        ig, is_, xg_in = sem("idx_gather"), sem("idx_scatter"), [sem("rows_gathered0"), sem("rows_gathered1")]
        dch, sig_a, ahi_a, yd, ysc = sem("dve_expert_step"), sem("sigmoid_done"), sem("act_hi_done"), sem("y_done"), [sem("y_scattered0"), sem("y_scattered1")]
        f_in = [sem(f"final_loaded{i}") for i in range(6)]
        gf_in, f_sq, f_rs, f_d, f_st = (sem(n) for n in ("g_final_loaded", "final_squared", "final_rstd", "final_done", "final_stored"))

        block = ctx.enter_context(nc.Block())

        def unit_cols(u):
            return KV_UNIT if u == 3 else UNIT

        def proj_reader(n):
            if n < 16:
                c, r = n // 4, n % 4
                return (ev_a, 2 * c + r + 1) if r < 2 else (ev_d, 2 * c + r - 1)
            return (ev_a, 8 + n - 15) if n < 26 else (ev_d, 8 + n - 25)

        def wait_mix_unit_used(e, u):
            e.wait_ge(*((proj, (8, 16, 24, 28)[u]) if u < 4 else (out_pe, 2 * T)))

        def wait_split(e, u):
            e.wait_ge(lo_dve, u + 1)
            e.wait_ge(lo_pool, u + 1)

        def split_hi(e, u, slot, n):
            e.activation(whi[:, slot, 0:n], raw[:, slot, 0:n], ACT.Copy, scale=W_SCALE).then_inc(hi_done, 1)

        def split_lo_pool(e, k, slot, a, b):
            part = raw[:, slot, a:b]
            e.tensor_scalar(part, part, W_SCALE, 0.0, ALU.mult, ALU.add).then_inc(raw_scaled, 1)
            e.wait_ge(raw_scaled, k)
            if not isinstance(k, int):
                after_waits(e)
            e.tensor_tensor(wlo[:, slot, a:b], part, whi[:, slot, a:b], ALU.subtract).then_inc(lo_pool, 1)

        def split_lo(e, slot, a, b, done):
            e.scalar_tensor_tensor(out=wlo[:, slot, a:b], in0=raw[:, slot, a:b], scalar=W_SCALE,
                                   in1=whi[:, slot, a:b], op0=ALU.mult, op1=ALU.subtract).then_inc(done, 1)

        def mixer_split(e, u):
            slot, n = u % RING, unit_cols(u)
            if u >= RING:
                wait_mix_unit_used(e, u - RING)
            if e is act_engine[0]:
                e.wait_ge(raw_full[slot], 16 * (u // RING + 1))
                split_hi(e, u, slot, n)
            else:
                e.wait_ge(hi_done, u + 1)
                cut = DVE_SPLIT * n // UNIT
                if e is dve_engine[0]:
                    split_lo(e, slot, 0, cut, lo_dve)
                else:
                    split_lo_pool(e, u + 1, slot, cut, n)

        act_engine, dve_engine, pool_engine = [None], [None], [None]

        def all_stored(e, slots):
            for s, done in enumerate(slots):
                e.wait_ge(done, 16 * len(range(s, T, len(slots))))

        def after_waits(e):
            e.sem_inc(step_pool if e is pool_engine[0] else step_dve, 1)

        def item_hi(e, i, v):
            e.wait_ge(used, i * ITEM_UNITS + (v - 2))
            e.wait_ge(raw_full[v % RING], i * 32 + 16 * (3 + v // RING))
            split_hi(e, v, v % RING, UNIT)

        def item_lo_dve(e, i, v):
            e.wait_ge(hi_done, i * ITEM_UNITS + (MIX_UNITS + v + 1))
            split_lo(e, v % RING, 0, DVE_SPLIT, lo_dve)

        def item_lo_pool(e, i, v):
            e.wait_ge(hi_done, i * ITEM_UNITS + (MIX_UNITS + v + 1))
            after_waits(e)
            split_lo_pool(e, i * ITEM_UNITS + (MIX_UNITS + v + 1), v % RING, DVE_SPLIT, UNIT)

        DCH0 = 8
        CLIPPED, MADE, SPLIT = (4, 11, 19, 27), (7, 15, 23, 31), (12, 20, 28, 32)

        items_flat = items.rearrange("p a b -> p (a b)")
        N_CONST_DMAS = 16 * 5


        @block.sync
        def _(e):
            e.dma_start(pr, params).then_inc(c_in, 16)
            e.dma_start(cs_all, consts[:, 0:CONSTS["band"][0]]).then_inc(c_in, 16)
            e.dma_start(band_f, consts[:, slice(*CONSTS["band"])]).then_inc(c_in, 16)
            e.dma_start(bv_sb, b_v).then_inc(c_in, 16)
            e.dma_start(br_sb, b_router).then_inc(c_in, 16)
            e.dma_start(g_mix, rows[0]).then_inc(g_in, 16)

            def load_unit(u):
                slot = u % RING
                if u >= RING:
                    wait_split(e, u - RING)
                if u == 3:
                    e.dma_start(raw[:, slot, 0:KV_UNIT], w_kv).then_inc(raw_full[slot], 16)
                else:
                    e.dma_start(raw[:, slot, :], w_units[u - (u > 3)]).then_inc(raw_full[slot], 16)

            for t in range(T):
                if t >= 2:
                    e.wait_ge(x_nd, t - 1)
                e.dma_start(x_in[:, t % 2, :], x[t * P:(t + 1) * P, :]).then_inc(xin[t % 2], 16)
                if t in (2, 4, 6):
                    load_unit((2, 4, 6).index(t))
            e.dma_start(table, table0).then_inc(init, 16)
            e.dma_start(h_rows[SEQ:SEQ + SPARE, :], zeros).then_inc(init, 16)
            e.dma_start(y_rows[SEQ:SEQ + SPARE, :], zeros).then_inc(init, 16)
            for u in range(3, 8):
                load_unit(u)
            e.wait_ge(ot_pe, 2 * T)
            e.wait_ge(ms_pe, 4)
            e.dma_start(b_out, rows[1]).then_inc(r_in, 16)
            e.dma_start(g_ffn, rows[2]).then_inc(r_in, 16)
            e.dma_start(b2_sb[0:NE, :], b2).then_inc(r_in, 16)
            e.dma_start(wr, w_router).then_inc(r_in, 16)
            e.wait_ge(mhi_a, 4 * CT)
            e.wait_ge(mlo_p, 4 * CT)
            e.dma_start(b1_sb.rearrange("p a b -> p (a b)"), b1).then_inc(b1_in, 16)
            def first_item(v):
                for s in (hi_done, lo_dve, lo_pool):
                    e.wait_ge(s, MIX_UNITS + v - 2)
                e.dma_start(raw[:, v % RING, :], w_units[MIX_UNITS - 1 + v]).then_inc(raw_full[v % RING], 16)

            def load_residual(t):
                if t >= XR:
                    e.wait_ge(acc_st[t % XR], 16 * (t // XR))
                e.dma_start(xr[:, t % XR, :], x[t * P:(t + 1) * P, :]).then_inc(xr_s[t % XR], 16)

            load_residual(0)
            load_residual(1)
            for t in range(T + 3):
                if t + 2 < T:
                    load_residual(t + 2)
                if 1 <= t <= T:
                    e.wait_ge(h_d, t)
                    e.dma_start(h_rows[(t - 1) * P:t * P, :], h_sb[:, (t - 1) % 2, :]).then_inc(h_st[(t - 1) % 2], 16)
                if t == T:
                    first_item(2)
                    first_item(3)
                if t >= 3:
                    e.wait_ge(acc_d, 2 * (t - 2))
                    e.dma_start(y_rows[(t - 3) * P:(t - 2) * P, :], xr[:, (t - 3) % XR, :]).then_inc(acc_st[(t - 3) % XR], 16)

            def item_weights(i, expert, first=0):
                for v in range(first, ITEM_UNITS):
                    for s in (hi_done, lo_dve, lo_pool):
                        e.wait_ge(s, i * ITEM_UNITS + (MIX_UNITS + v - 2))
                    src = w_units[bass.ds(expert * ITEM_UNITS + (MIX_UNITS - 1 + v), 1)].rearrange("a p n -> p (a n)")
                    e.dma_start(raw[:, v % RING, :], src).then_inc(raw_full[v % RING], 16)

            e.wait_ge(scat, 16 * TOPK * T)
            src = table.rearrange("(x s p) w -> p x s w", p=P, s=SEQ // P)
            for blk in range(2):
                e.dma_start(idx_all[:, 0:NE, blk, :], src[:, :, blk, :]).then_inc(idx_in, 16)
            e.wait_ge(items_ready, 1)
            last_item = e.value_load(items_flat[0:1, W_LAST:W_LAST + 1], min_val=NE - 1, max_val=ITEMS - 1)
            with e.If(last_item > NE - 1):
                for k in range(NE, ITEMS):
                    row = e.value_load(items_flat[0:1, ITEMS + k:ITEMS + k + 1], min_val=0, max_val=(NE - 1) * SEQ + 3 * ITEM_ROWS)
                    src = table[bass.ds(row, ITEM_ROWS), :].rearrange("(b p) w -> p b w", p=P)
                    e.dma_start(idx_all[:, k, :, :], src).then_inc(idx_in, 16)
                e.wait_ge(idx_in, 32 + 16 * EXTRA)
                e.sem_inc(lists_ready, 1)
            with e.Else():
                e.wait_ge(idx_in, 32)
                e.sem_inc(lists_ready, 1)
            for v in range(4, ITEM_UNITS):
                first_item(v)
            with e.Fori(1, NE) as i:
                item_weights(i, i)
            e.wait_ge(items_ready, 1)
            last_item = e.value_load(items_flat[0:1, W_LAST:W_LAST + 1], min_val=NE - 1, max_val=ITEMS - 1)
            with e.If(last_item > NE - 1):
                with e.Fori(NE, last_item + 1) as i:
                    expert = e.value_load(items_flat[0:1, bass.ds(i, 1)], min_val=0, max_val=NE - 1)
                    item_weights(i, expert)
            e.nop()
            e.dma_start(g_final, rows[3]).then_inc(gf_in, 16)
            e.wait_ge(ysc[0], last_item * 16 + 32)
            e.wait_ge(ysc[1], last_item * 16 + 32)
            for t in range(T):
                if t >= 6:
                    e.wait_ge(f_st, 16 * (t - 5))
                e.dma_start(fin[:, t % 6, :], y_rows[t * P:(t + 1) * P, :]).then_inc(f_in[t % 6], 16)
                if t >= 2:
                    e.wait_ge(f_d, t - 1)
                    e.dma_start(out[(t - 2) * P:(t - 1) * P, :], fin[:, (t - 2) % 6, :]).then_inc(f_st, 16)
            for t in range(T - 2, T):
                e.wait_ge(f_d, t + 1)
                e.dma_start(out[t * P:(t + 1) * P, :], fin[:, t % 6, :]).then_inc(f_st, 16)
            e.wait_ge(f_st, 16 * T)

        @block.tensor
        def _(e):
            def product(out_ap, l_hi, l_lo, r_hi, r_lo, start, stop):
                e.matmul(out_ap, l_hi, r_hi, start=start, stop=False)
                e.matmul(out_ap, l_hi, r_lo, start=False, stop=False)
                return e.matmul(out_ap, l_lo, r_hi, start=False, stop=stop)

            e.wait_ge(c_in, N_CONST_DMAS)
            for t in range(T):
                e.wait_ge(x_nd, t + 1)
                if t >= 2:
                    e.wait_ge(u_ld, t - 1)
                for k in range(KC):
                    last = e.transpose(ps[:, 2 * (t % 2) + k // 4, (k % 4) * P:(k % 4 + 1) * P],
                                       xn[:, k * P:(k + 1) * P], cs["ident"])
                last.then_inc(x_tr, 1)
            n = 0
            for u in range(4):
                slot = u % RING
                wait_split(e, u)
                for tile in range(4 if u < 3 else 1):
                    for half in range(2):
                        e.wait_ge(u_ld, 4 * (half + 1))
                        if n >= 4:
                            e.wait_ge(*proj_reader(n - 4))
                        wide = HALF if u < 3 else 256
                        for k in range(KC):
                            at = k * wide + tile * P
                            toks = slice(half * HALF, (half + 1) * HALF)
                            last = product(ps[:, 4 + n % 4, :], whi[:, slot, at:at + P], wlo[:, slot, at:at + P],
                                           u_hi[:, k, toks], u_lo[:, k, toks], k == 0, k == KC - 1)
                        last.then_inc(proj, 1)
                        n += 1
            for quad in range(2):
                e.wait_ge(*proj_reader(n - 4))
                for tt in range(4):
                    t = quad * 4 + tt
                    for k in range(KC):
                        at = k * 256 + P
                        toks = slice(t * P, (t + 1) * P)
                        last = product(ps[:, 4 + n % 4, tt * P:(tt + 1) * P], u_hi[:, k, toks], u_lo[:, k, toks],
                                       whi[:, 0, at:at + P], wlo[:, 0, at:at + P], k == 0, k == KC - 1)
                last.then_inc(proj, 1)
                n += 1

            def channel_mean(bank, src, done):
                for j in range(CT):
                    last = e.matmul(ps[:, bank, :], mean_w, src[:, j, :], start=(j == 0), stop=(j == CT - 1))
                last.then_inc(done, 1)

            def scores(n):
                b, g = n // KV, n % KV
                if n < 2:
                    e.wait_ge(ev_a, 18)
                else:
                    e.wait_ge(exp_a, 5 * (n - 1))
                lo = 0 if b else P
                part = slice(g * HD, (g + 1) * HD)
                for j in range(GROUP):
                    dst = ps[:, 2 * (n % 2) + j // 2, (j % 2) * 2 * P + lo:(j % 2 + 1) * 2 * P]
                    e.matmul(dst, q_t[part, j, b * P:(b + 1) * P], k_t[part, (b - 1) * P + lo:(b + 1) * P],
                             start=True, stop=False)
                    last = e.matmul(dst, ident_b, band_b[:, lo:2 * P], start=False, stop=True)
                last.then_inc(sc_pe, 1)

            def probs_t(n):
                b = n // KV
                e.wait_ge(pn_p, 4 * (n + 1))
                if n >= 1:
                    e.wait_ge(pta, n)
                    e.wait_ge(ptd, n)
                for kb in range(0 if b else 1, 2):
                    for j in range(GROUP):
                        last = e.transpose(ps[:, 4 + kb, j * P:(j + 1) * P],
                                           prob[:, n % 2, j, kb * P:(kb + 1) * P], cs["ident"])
                last.then_inc(pt_pe, 1)

            def heads_t(n):
                b, g = n // KV, n % KV
                e.wait_ge(pta, n + 1)
                e.wait_ge(ptd, n + 1)
                if n == 0:
                    e.wait_ge(ve_d, 2)
                else:
                    e.wait_ge(og_a, n)
                first = 0 if b else 1
                for kb in range(first, 2):
                    last = e.matmul(ps[g * HD:(g + 1) * HD, 6, :], v_sb[:, b - 1 + kb, g * HD:(g + 1) * HD],
                                    prob_t[:, kb, :], start=(kb == first), stop=(kb == 1))
                last.then_inc(ot_pe, 1)

            e.wait_ge(tap_d, CT * TAPS)
            e.wait_ge(tap_p, CT * TAPS)
            e.wait_ge(ev_d, 10)
            for h in range(2):
                channel_mean(7 - h, conv[:, :, h * HALF:(h + 1) * HALF], mean_pe)
            scores(0)
            scores(1)
            for h in range(2):
                e.wait_ge(vsq_a, CT * (h + 1))
                channel_mean(7 - h, sq, var_pe)

            def branch_meansq(i):
                e.wait_ge(csq_a, CT * (i + 1))
                e.wait_ge(*((ve_d, 1) if i == 0 else (mse_d, i)))
                channel_mean(7, sq, ms_pe)

            for n in range(2 * T):
                probs_t(n)
                if n + 2 < 2 * T:
                    scores(n + 2)
                heads_t(n)
                if n in (1, 3, 9):
                    branch_meansq((1, 3, 9).index(n))
            branch_meansq(3)

            def out_half(t, half):
                slot = (4 + half) % RING
                if t == 0:
                    wait_split(e, 4 + half)
                    e.wait_ge(mlo_p, 4 * CT)
                    e.wait_ge(exp_a, 5 * 2 * T)
                if t >= 2 and half == 0:
                    e.wait_ge(x2_d, t - 1)
                toks = slice(t * P, (t + 1) * P)
                for c in range(2 * CT):
                    at = c * HALF
                    last = product(ps[:, 2 * (t % 2) + half, :], mix_hi[:, c, toks], mix_lo[:, c, toks],
                                   whi[:, slot, at:at + HALF], wlo[:, slot, at:at + HALF], c == 0, c == 2 * CT - 1)
                last.then_inc(out_pe, 1)

            def h_t(t):
                e.wait_ge(h_d, t + 1)
                if t == 0:
                    e.wait_ge(pta, 2 * T)
                    e.wait_ge(ptd, 2 * T)
                else:
                    e.wait_ge(htl, t)
                for k in range(KC):
                    last = e.transpose(ps[:, 4 + k // 4, (k % 4) * P:(k % 4 + 1) * P],
                                       h_sb[:, t % 2, k * P:(k + 1) * P], cs["ident"])
                last.then_inc(tr_pe, 1)

            def router(t):
                e.wait_ge(htl, t + 1)
                if t == 0:
                    e.wait_ge(og_a, 2 * T)
                    e.wait_ge(b1_t, 1)
                else:
                    e.wait_ge(rc, t)
                for k in range(KC):
                    last = product(ps[:, 6, 0:NE], ht_hi[:, k, :], ht_lo[:, k, :], wr_hi[:, k, :], wr_lo[:, k, :],
                                   k == 0, k == KC - 1)
                last.then_inc(rt_pe, 1)

            def positions(t):
                e.wait_ge(ra, 11 * (t + 1))
                for s in range(t):
                    e.matmul(ps[:, 6, NE:2 * NE], ones_b, mb[:, s, :], start=(s == 0), stop=False)
                e.matmul(ps[:, 6, NE:2 * NE], before_b, mb[:, t, :], start=(t == 0), stop=True)
                e.transpose(ps[0:NE, 6, P:2 * P], gates_g, cs["ident"]).then_inc(gt_pe, 1)

            def gate_bias(t, half):
                e.wait_ge(rc, t + 1)
                if t == 0 and half == 0:
                    e.wait_ge(mse_d, 4)
                elif half or t:
                    e.wait_ge(acc_d, 2 * t + half)
                e.matmul(ps[:, 7, :], gt_sb[0:NE, :], b2_sb[0:NE, half * HALF:(half + 1) * HALF],
                         start=True, stop=True).then_inc(gb_pe, 1)

            e.wait_ge(r_in, 64)
            for t in range(T + 3):
                if t < T:
                    out_half(t, 0)
                if 1 <= t <= T:
                    h_t(t - 1)
                if 2 <= t <= T + 1:
                    positions(t - 2)
                if 3 <= t:
                    gate_bias(t - 3, 0)
                if t < T:
                    out_half(t, 1)
                if 3 <= t:
                    gate_bias(t - 3, 1)
                if 1 <= t <= T:
                    router(t - 1)

            for t in range(T):
                last = e.matmul(ps[0:NE, 6, 2 * P:2 * P + 1], mb[:, t, :], ones_b[:, 0:1], start=(t == 0), stop=(t == T - 1))
            last.then_inc(cnt_pe, 1)
            e.wait_ge(it_d, 4)
            e.matmul(ps[0:NE, 6, 2 * P + 2:2 * P + 3], cs["before"][0:NE, 0:NE], xe[0:NE, :], start=True, stop=True).then_inc(st_pe, 1)
            e.wait_ge(it_d, 18)
            e.matmul(ps[0:1, 7, 0:4 * ITEMS], cs["ones"][0:NE, 0:1], itm[0:NE, :, :].rearrange("p a b -> p (a b)"),
                     start=True, stop=True).then_inc(row_pe, 1)

            def rows_t(block, banks):
                for k in range(KC):
                    last = e.transpose(ps[:, banks + k // 4, (k % 4) * P:(k % 4 + 1) * P],
                                       xg[:, block, k * P:(k + 1) * P], cs["ident"])
                return last

            def transpose_rows(i, n):
                e.wait_ge(xg_in[0], i * 16 + 32)
                e.wait_ge(xg_in[1], i * 16 + 32)
                e.wait_ge(dch, i * 32 + (DCH0 + CLIPPED[2]))
                with e.If(n > P):
                    rows_t(1, 0)
                rows_t(0, 6).then_inc(t_done, 1)

            def up(u, width):
                slot, pair = u % RING, 2 * (u % 2)
                for tile in range(4):
                    for k in range(KC):
                        at = k * HALF + tile * P
                        last = product(ps[:, pair + tile // 2, (tile % 2) * ITEM_ROWS:(tile % 2) * ITEM_ROWS + width],
                                       whi[:, slot, at:at + P], wlo[:, slot, at:at + P],
                                       xt_hi[:, k, 0:width], xt_lo[:, k, 0:width], k == 0, k == KC - 1)
                last.then_inc(used, 1)

            def all_up(i, width):
                for u in range(W1_UNITS):
                    e.wait_ge(lo_dve, i * ITEM_UNITS + (MIX_UNITS + u + 1))
                    e.wait_ge(lo_pool, i * ITEM_UNITS + (MIX_UNITS + u + 1))
                    if u >= 2:
                        e.wait_ge(dch, i * 32 + (DCH0 + CLIPPED[u - 2]))
                    up(u, width)

            def by_width(n, widths, body):
                if len(widths) == 1:
                    body(widths[0])
                    return
                mid = len(widths) // 2
                with e.If(n <= widths[mid - 1]):
                    by_width(n, widths[:mid], body)
                    e.nop()
                with e.Else():
                    by_width(n, widths[mid:], body)
                    e.nop()

            def down(half, blk, first, last_k):
                slot = (W1_UNITS + half) % RING
                for k in range(first, last_k):
                    at = k * HALF
                    toks = slice(blk * P, (blk + 1) * P)
                    last = product(ps[:, 4 + 2 * half + blk, :], act_hi[:, k, toks], act_lo[:, k, toks],
                                   whi[:, slot, at:at + HALF], wlo[:, slot, at:at + HALF], k == 0, k == KC - 1)
                return last

            def item(i, n_last):
                n = e.value_load(items_flat[0:1, bass.ds(i + 2 * ITEMS, 1)], min_val=0, max_val=ITEM_ROWS)
                e.wait_ge(xt_ready, i + 1)
                by_width(n, WIDTHS, lambda w: all_up(i, w))
                if not n_last:
                    n_next = e.value_load(items_flat[0:1, bass.ds(i + (2 * ITEMS + 1), 1)], min_val=0, max_val=ITEM_ROWS)
                    transpose_rows(i, n_next)
                for half in range(W2_UNITS):
                    e.wait_ge(lo_dve, i * ITEM_UNITS + (MIX_UNITS + W1_UNITS + half + 1))
                    e.wait_ge(lo_pool, i * ITEM_UNITS + (MIX_UNITS + W1_UNITS + half + 1))
                    if half == 0:
                        e.wait_ge(dch, i * 32 + (DCH0 + SPLIT[2]))
                    elif not n_last:
                        e.wait_ge(xt_ready, i + 2)
                    with e.If(n > P):
                        down(half, 1, 0, KC - 2)
                    down(half, 0, 0, KC - 2)
                    if half == 0:
                        e.wait_ge(dch, i * 32 + (DCH0 + SPLIT[3]))
                    with e.If(n > P):
                        down(half, 1, KC - 2, KC)
                    down(half, 0, KC - 2, KC).then_inc(used, 1)

            e.wait_ge(items_ready, 1)
            last_item = e.value_load(items_flat[0:1, W_LAST:W_LAST + 1], min_val=NE - 1, max_val=ITEMS - 1)
            e.wait_ge(xg_in[0], 16)
            e.wait_ge(xg_in[1], 16)
            e.wait_ge(dch, DCH0)
            rows_t(1, 0)
            rows_t(0, 4).then_inc(t_done, 1)
            with e.Fori(0, last_item) as i:
                item(i, False)
            item(last_item, True)

        @block.scalar
        def _(e):
            act_engine[0] = e
            e.wait_ge(c_in, N_CONST_DMAS)
            for t in range(T + 1):
                if t < T:
                    e.wait_ge(xin[t % 2], 16 * (t // 2 + 1))
                    if t >= 4:
                        e.wait_ge(x_sq, t - 3)
                    e.activation(conv[:, t % 4, :], x_in[:, t % 2, :], ACT.Square,
                                 accum_out=ss1[:, t:t + 1]).then_inc(x_sq, 1)
                if t >= 1:
                    e.wait_ge(x_tr, t)
                    src = ps[:, 2 * ((t - 1) % 2):2 * ((t - 1) % 2) + 2, :].rearrange("p a (k c) -> p (a k) c", c=P)
                    e.activation(u_hi[:, :, (t - 1) * P:t * P], src, ACT.Copy).then_inc(u_hd, 1)
                if t in (3, 5, 7):
                    mixer_split(e, (3, 5, 7).index(t))
            for n in range(26):
                e.wait_ge(proj, n + 1)
                bank = ps[:, 4 + n % 4, :]
                half = n % 2
                if n < 16 and n % 4 < 2:
                    gi = n // 4 * 2 + half
                    if gi >= 2:
                        e.wait_ge(ev_d, gi - 1)
                    e.activation(sg[:, gi % 2, :], bank, ACT.Sigmoid, scale=1.0 / Z_SCALE,
                                 bias=par["b_gate"][:, n // 4:n // 4 + 1]).then_inc(ev_a, 1)
                elif n >= 16:
                    j = n // 2 - 8
                    if n < 24:
                        e.activation(q_t[:, j, half * HALF:(half + 1) * HALF], bank, ACT.Identity, scale=1.0 / Z_SCALE,
                                     bias=par["b_q"][:, j:j + 1]).then_inc(ev_a, 1)
                    else:
                        e.activation(k_t[:, half * HALF:(half + 1) * HALF], bank, ACT.Identity, scale=1.0 / Z_SCALE,
                                     bias=par["b_k"]).then_inc(ev_a, 1)
                if n in (8, 16, 24):
                    mixer_split(e, (8, 16, 24).index(n) + 3)
            mixer_split(e, 6)

            def centred_squares(h):
                for j in range(CT):
                    e.wait_ge(sub_d, CT * h + j + 1)
                    if j == 0:
                        e.wait_ge(*((ev_d, 10) if h == 0 else (var_pe, h)))
                    e.activation(sq[:, j, :], conv[:, j, h * HALF:(h + 1) * HALF], ACT.Square).then_inc(vsq_a, 1)

            def exps(n):
                b = n // KV
                lo = 0 if b else P
                e.wait_ge(nm_d, n + 1)
                if n >= 2:
                    e.wait_ge(pt_pe, n - 1)
                    e.wait_ge(den_d, n - 1)
                for j in range(GROUP):
                    src = ps[:, 2 * (n % 2) + j // 2, (j % 2) * 2 * P + lo:(j % 2 + 1) * 2 * P]
                    e.activation(prob[:, n % 2, j, lo:2 * P], src, ACT.Exp, scale=SCORE_SCALE,
                                 bias=nm[:, n % 2, j:j + 1], accum_out=rsum[:, n % 2, j:j + 1]).then_inc(exp_a, 1)
                e.wait_ge(dsk_d, n + 1)
                e.activation(esum[:, n % 2, :], dsk[:, n % 2, :], ACT.Exp).then_inc(exp_a, 1)

            def root(h, k):
                e.wait_ge(*((ve_d, k) if k <= 2 else (mse_d, k - 2)))
                e.activation(rs[:, h, :], rs[:, h, :], ACT.Sqrt).then_inc(root_a, 1)

            def swish(h):
                for j in range(CT):
                    e.wait_ge(y_d, CT * h + j + 1)
                    if j == 0:
                        e.wait_ge(*((var_pe, 2) if h == 0 else (ms_pe, 1)))
                    e.activation(sq[:, j, :], conv[:, j, h * HALF:(h + 1) * HALF], ACT.Sigmoid,
                                 scale=par["ln_g"][:, j:j + 1], bias=par["ln_b"][:, j:j + 1]).then_inc(sgm_a, 1)
                for j in range(CT):
                    e.wait_ge(s_d, CT * h + j + 1)
                    e.activation(sq[:, j, :], conv[:, j, h * HALF:(h + 1) * HALF], ACT.Square).then_inc(csq_a, 1)

            def head_squares(h):
                e.wait_ge(og_a, 8 * (h + 1))
                e.wait_ge(ms_pe, 2 + h)
                for j in range(CT):
                    e.activation(sq[:, j, :], heads[h][:, j, :], ACT.Square).then_inc(csq_a, 1)

            def mixed_hi(i):
                h = i % 2
                root(h, 3 + i)
                for j in range(CT):
                    src = conv[:, j, h * HALF:(h + 1) * HALF] if i < 2 else heads[h][:, j, :]
                    e.wait_ge(m_d, CT * i + j + 1)
                    e.activation(mix_hi[:, j + (CT if i < 2 else 0), h * HALF:(h + 1) * HALF], src, ACT.Copy).then_inc(mhi_a, 1)

            centred_squares(0)
            exps(0)
            centred_squares(1)
            exps(1)
            root(0, 1)
            root(1, 2)
            for n in range(2 * T):
                b, g = n // KV, n % KV
                e.wait_ge(pt_pe, n + 1)
                if n:
                    e.wait_ge(ot_pe, n)
                e.activation(prob_t[:, 1, :], ps[:, 5, :], ACT.Copy).then_inc(pta, 1)
                if n + 2 < 2 * T:
                    exps(n + 2)
                e.wait_ge(ot_pe, n + 1)
                if n == 0:
                    e.wait_ge(tap_d, CT * TAPS)
                    e.wait_ge(tap_p, CT * TAPS)
                if n == 8:
                    e.wait_ge(mlo_p, 2 * CT)
                e.activation(heads[b // 4][g * HD:(g + 1) * HD, :, (b % 4) * P:(b % 4 + 1) * P],
                             ps[g * HD:(g + 1) * HD, 6, :].rearrange("p (j c) -> p j c", j=GROUP),
                             ACT.Copy).then_inc(og_a, 1)
                if n == 0:
                    swish(0)
                if n == 2:
                    mixed_hi(0)
                    swish(1)
                if n == 4:
                    mixed_hi(1)
                if n == 8:
                    head_squares(0)
                if n == 10:
                    mixed_hi(2)
            head_squares(1)
            mixed_hi(3)

            def h_hi(t):
                e.wait_ge(tr_pe, t + 1)
                if t:
                    e.wait_ge(rt_pe, t)
                e.activation(ht_hi, ps[:, 4:6, :].rearrange("p a (k c) -> p (a k) c", c=P), ACT.Copy, scale=X_SCALE).then_inc(hth, 1)

            for t in range(T + 1):
                if t >= 1:
                    h_hi(t - 1)
                if t < T:
                    e.wait_ge(x2_d, t + 1)
                    if t >= 2:
                        e.wait_ge(tr_pe, t - 1)
                        e.wait_ge(h_st[t % 2], 16 * (t // 2))
                    e.activation(h_sb[:, t % 2, :], xr[:, t % XR, :], ACT.Square, accum_out=ss2[:, t:t + 1]).then_inc(x2sq, 1)
                if t >= 1:
                    e.wait_ge(ra, 11 * (t - 1) + 5)
                    e.activation(ex, mx8[:, 0:TOPK], ACT.Exp, bias=nm0, accum_out=se).then_inc(ea, 1)
            mixer_split(e, 7)
            mixer_split(e, 8)

            def rows_hi(i):
                e.wait_ge(t_done, i + 1)
                e.activation(xt_hi[:, :, 0:P], ps[:, 6:8, :].rearrange("p a (k c) -> p (a k) c", c=P),
                             ACT.Copy, scale=X_SCALE).then_inc(xt_hd, 1)

            def sigmoid(i, u):
                e.wait_ge(dch, i * 32 + (DCH0 + CLIPPED[u]))
                e.activation(sig, glu, ACT.Sigmoid, scale=ALPHA / Z_SCALE).then_inc(sig_a, 1)

            def act_high(i, u):
                e.wait_ge(dch, i * 32 + (DCH0 + MADE[u]))
                e.activation(act_hi[:, 2 * u:2 * u + 2, :], act, ACT.Copy).then_inc(ahi_a, 1)

            def item(i, n_last):
                for u in range(3):
                    sigmoid(i, u)
                    item_hi(e, i, u + 3)
                    act_high(i, u)
                sigmoid(i, 3)
                act_high(i, 3)
                if not n_last:
                    rows_hi(i + 1)
                    for v in (6, 7, 8):
                        item_hi(e, i, v)

            e.wait_ge(items_ready, 1)
            last_item = e.value_load(items_flat[0:1, W_LAST:W_LAST + 1], min_val=NE - 1, max_val=ITEMS - 1)
            e.wait_ge(t_done, 1)
            e.activation(xt_hi[:, :, 0:P], ps[:, 4:6, :].rearrange("p a (k c) -> p (a k) c", c=P), ACT.Copy, scale=X_SCALE).then_inc(xt_hd, 1)
            with e.Fori(0, last_item) as i:
                item(i, False)
            item(last_item, True)

            for t in range(T):
                e.wait_ge(f_in[t % 6], 16 * (t // 6 + 1))
                if t >= 2:
                    e.wait_ge(f_sq, t - 1)
                e.activation(xg[:, t % 2, :], fin[:, t % 6, :], ACT.Square, accum_out=ss3[:, t:t + 1]).then_inc(f_sq, 1)

        @block.vector
        def _(e):
            dve_engine[0] = e
            for c in (0, 1):
                e.memset(cu[c][:, 0:TAPS - 1], 0.0).then_inc(setup_d, 1)

            def u_lo_part(t):
                e.wait_ge(u_hd, t + 1)
                src = ps[:, 2 * (t % 2):2 * (t % 2) + 2, :].rearrange("p a (k c) -> p (a k) c", c=P)
                e.tensor_tensor(u_lo[:, :, t * P:(t + 1) * P], src, u_hi[:, :, t * P:(t + 1) * P], ALU.subtract).then_inc(u_ld, 1)

            for t in range(T + 1):
                if t < T:
                    e.wait_ge(x_rs, t + 1)
                    if t >= 1:
                        e.wait_ge(x_tr, t)
                    e.scalar_tensor_tensor(out=xn, in0=x_in[:, t % 2, :], scalar=rs1[:, t:t + 1], in1=g_mix,
                                           op0=ALU.mult, op1=ALU.mult).then_inc(x_nd, 1)
                if t >= 1:
                    u_lo_part(t - 1)
                if t in (3, 5, 7):
                    mixer_split(e, (3, 5, 7).index(t))

            e.wait_ge(x_sq, T)
            e.wait_ge(setup, 5)
            for c in (2, 3):
                e.memset(cu[c][:, 0:TAPS - 1], 0.0).then_inc(setup_d, 1)
            e.wait_ge(setup_d, 4)

            def glu_tile(c):
                for half in range(2):
                    e.wait_ge(proj, 4 * c + 3 + half)
                    e.wait_ge(ev_a, 2 * c + half + 1)
                    e.scalar_tensor_tensor(out=cu[c][:, TAPS - 1 + half * HALF:TAPS - 1 + (half + 1) * HALF],
                                           in0=ps[:, 4 + (4 * c + 2 + half) % 4, :], scalar=par["b_a"][:, c:c + 1],
                                           in1=sg[:, half, :], op0=ALU.add, op1=ALU.mult).then_inc(ev_d, 1)
                e.wait_ge(ev_d, 2 * c + 2)

            def tap(c, k):
                dst, w = conv[:, c, 0:DVE_TOKENS], par["w_dw"][:, c * TAPS + k:c * TAPS + k + 1]
                src = cu[c][:, k:k + DVE_TOKENS]
                if k == 0:
                    ins = e.tensor_scalar(dst, src, w, par["b_dw"][:, c:c + 1], ALU.mult, ALU.add)
                else:
                    e.wait_ge(tap_d, c * TAPS + k)
                    ins = e.scalar_tensor_tensor(out=dst, in0=src, scalar=w, in1=dst, op0=ALU.mult, op1=ALU.add)
                ins.then_inc(tap_d, 1)

            for s in range(CT * TAPS):
                if s % GLU_EVERY == 0 and s // GLU_EVERY < CT:
                    glu_tile(s // GLU_EVERY)
                if s in (2 * GLU_EVERY + 8, 4 * GLU_EVERY):
                    mixer_split(e, 3 if s < 3 * GLU_EVERY else 4)
                tap(s // TAPS, s % TAPS)
            for quad in range(2):
                e.wait_ge(proj, 27 + quad)
                e.scalar_tensor_tensor(out=v_sb[:, quad * 4:quad * 4 + 4, :],
                                       in0=ps[:, 6 + quad, :].rearrange("p (a b) -> p a b", a=4), scalar=1.0 / Z_SCALE,
                                       in1=bv_sb.unsqueeze(1).to_broadcast([P, 4, P]), op0=ALU.mult, op1=ALU.add).then_inc(ev_d, 1)
            mixer_split(e, 5)

            def centre(h):
                e.wait_ge(mean_pe, h + 1)
                for j in range(CT):
                    c = conv[:, j, h * HALF:(h + 1) * HALF]
                    e.tensor_tensor(c, c, ps[:, 7 - h, :], ALU.subtract).then_inc(sub_d, 1)

            def row_max(n):
                b, g = n // KV, n % KV
                lo = 0 if b else P
                e.wait_ge(sc_pe, n + 1)
                src = ps[:, 2 * (n % 2):2 * (n % 2) + 2, :].rearrange("p a (j c) -> p (a j) c", j=2)
                if n >= 2:
                    e.wait_ge(exp_a, 5 * (n - 1))
                e.tensor_reduce(mxs[:, n % 2, :], src[:, :, lo:2 * P], AXX, ALU.max).then_inc(mx_d, 1)
                e.wait_ge(mx_d, n + 1)
                e.scalar_tensor_tensor(out=nm[:, n % 2, :], in0=mxs[:, n % 2, :], scalar=-SCORE_SCALE,
                                       in1=neg_sinks[:, g * GROUP:(g + 1) * GROUP], op0=ALU.mult, op1=ALU.min).then_inc(nm_d, 1)
                e.wait_ge(nm_d, n + 1)
                e.tensor_tensor(dsk[:, n % 2, :], nm[:, n % 2, :], par["sinks"][:, g * GROUP:(g + 1) * GROUP], ALU.add).then_inc(dsk_d, 1)

            def plus_eps(src_done, k, bank, h, done):
                e.wait_ge(src_done, k)
                e.tensor_scalar(rs[:, h, :], ps[:, bank, :], EPS, None, ALU.add).then_inc(done, 1)

            def inverse(h, k):
                e.wait_ge(root_a, k)
                e.reciprocal(rs[:, h, :], rs[:, h, :]).then_inc(rstd_d, 1)
                e.wait_ge(rstd_d, k)

            def ln_and_swish(h):
                for j in range(CT):
                    c = conv[:, j, h * HALF:(h + 1) * HALF]
                    e.tensor_tensor(c, c, rs[:, h, :], ALU.mult).then_inc(y_d, 1)
                for j in range(CT):
                    c = conv[:, j, h * HALF:(h + 1) * HALF]
                    e.wait_ge(z_p, CT * h + j + 1)
                    e.tensor_tensor(c, c, sq[:, j, :], ALU.mult).then_inc(s_d, 1)

            def branch_norm(i):
                h = i % 2
                plus_eps(ms_pe, i + 1, 7, h, mse_d)
                inverse(h, 3 + i)
                name = "g_conv" if i < 2 else "g_attn"
                for j in range(CT):
                    c = conv[:, j, h * HALF:(h + 1) * HALF] if i < 2 else heads[h][:, j, :]
                    e.scalar_tensor_tensor(out=c, in0=c, scalar=par[name][:, j:j + 1], in1=rs[:, h, :],
                                           op0=ALU.mult, op1=ALU.mult).then_inc(m_d, 1)

            centre(0)
            row_max(0)
            centre(1)
            row_max(1)
            for h in range(2):
                plus_eps(var_pe, h + 1, 7 - h, h, ve_d)
            for h in range(2):
                inverse(h, h + 1)
            def denominators(n):
                e.wait_ge(exp_a, 5 * (n + 1))
                if n >= 2:
                    e.wait_ge(pn_p, 4 * (n - 1))
                e.tensor_tensor(rden[:, n % 2, :], rsum[:, n % 2, :], esum[:, n % 2, :], ALU.add).then_inc(den_d, 1)
                e.wait_ge(den_d, n + 1)
                e.reciprocal(rden[:, n % 2, :], rden[:, n % 2, :]).then_inc(rden_d, 1)

            denominators(0)
            for n in range(2 * T):
                if n + 1 < 2 * T:
                    denominators(n + 1)
                e.wait_ge(pt_pe, n + 1)
                if n >= 1:
                    e.wait_ge(ot_pe, n)
                if n < 2:
                    e.memset(prob_t[:, 0, 0:2], 0.0).then_inc(ptd, 1)
                    e.wait_ge(ptd, n + 1)
                else:
                    e.tensor_copy(prob_t[:, 0, :], ps[:, 4, :]).then_inc(ptd, 1)
                if n + 2 < 2 * T:
                    row_max(n + 2)
                if n == 0:
                    ln_and_swish(0)
                if n == 2:
                    branch_norm(0)
                    ln_and_swish(1)
                if n == 4:
                    branch_norm(1)
                if n == 10:
                    branch_norm(2)
            branch_norm(3)
            mixer_split(e, 6)

            def residual(t):
                e.wait_ge(out_pe, 2 * (t + 1))
                e.wait_ge(xb_p, t + 1)
                c = xr[:, t % XR, :]
                e.scalar_tensor_tensor(out=c, in0=ps[:, 2 * (t % 2):2 * (t % 2) + 2, :].rearrange("p a b -> p (a b)"),
                                       scalar=1.0 / Z_SCALE, in1=c, op0=ALU.mult, op1=ALU.add).then_inc(x2_d, 1)

            def normed(t):
                e.wait_ge(rs2_p, t + 1)
                e.scalar_tensor_tensor(out=h_sb[:, t % 2, :], in0=xr[:, t % XR, :], scalar=rs2[:, t:t + 1], in1=g_ffn,
                                       op0=ALU.mult, op1=ALU.mult).then_inc(h_d, 1)

            def h_low(t):
                e.wait_ge(hth, t + 1)
                src = ps[:, 4:6, :].rearrange("p a (k c) -> p (a k) c", c=P)
                e.scalar_tensor_tensor(out=ht_lo, in0=src, scalar=X_SCALE, in1=ht_hi, op0=ALU.mult, op1=ALU.subtract).then_inc(htl, 1)

            def route(t):
                k = 11 * t

                def step(ins, n):
                    ins.then_inc(ra, 1)
                    e.wait_ge(ra, k + n)
                e.wait_ge(rt_pe, t + 1)
                step(e.scalar_tensor_tensor(out=lg, in0=ps[:, 6, 0:NE], scalar=1.0 / Z_SCALE, in1=br_sb, op0=ALU.mult, op1=ALU.add), 1)
                step(e.max(mx8, lg), 2)
                step(e.max_index(ix8, mx8, lg), 3)
                step(e.tensor_copy(ixf, ix8[:, 0:TOPK]), 4)
                step(e.tensor_scalar(nm0, mx8[:, 0:1], -1.0, None, ALU.mult), 5)
                step(e.tensor_tensor(oh[:, t % 2, :, :], cs["iota"].unsqueeze(1).to_broadcast([P, TOPK, NE]),
                                     ixf.unsqueeze(2).to_broadcast([P, TOPK, NE]), ALU.is_equal), 6)
                with nc.allow_low_precision(reason="zeros and ones"):
                    step(e.tensor_reduce(mb[:, t, :], oh[:, t % 2, :, :].rearrange("p k e -> p e k"), AXX, ALU.add), 7)

            def route_gates(t):
                k = 11 * t

                def step(ins, n):
                    ins.then_inc(ra, 1)
                    e.wait_ge(ra, k + n)
                e.wait_ge(ea, t + 1)
                step(e.reciprocal(rse, se), 8)
                gates = pay[:, t, :].rearrange("p (k w) -> p k w", w=2)[:, :, 1].bitcast(F32)
                step(e.tensor_scalar(gates, ex, rse, None, ALU.mult), 9)
                step(e.tensor_tensor(gk, oh[:, t % 2, :, :], gates.unsqueeze(2).to_broadcast([P, TOPK, NE]), ALU.mult), 10)
                if t:
                    e.wait_ge(gt_pe, t)
                step(e.tensor_reduce(gates_g, gk.rearrange("p k e -> p e k"), AXX, ALU.add), 11)

            def place(t):
                def step(ins, n):
                    ins.then_inc(rb, 1)
                    e.wait_ge(rb, 4 * t + n)
                e.wait_ge(gt_pe, t + 1)
                step(e.tensor_tensor(posb, ps[:, 6, NE:2 * NE], cs["base"], ALU.add), 1)
                step(e.tensor_tensor(gk, oh[:, t % 2, :, :], posb.unsqueeze(1).to_broadcast([P, TOPK, NE]), ALU.mult), 2)
                step(e.tensor_reduce(slf, gk, AXX, ALU.add), 3)
                step(e.tensor_copy(slots[:, t, :], slf), 4)
                if t:
                    e.wait_ge(gb_pe, 2 * t)
                e.tensor_copy(gt_sb[0:NE, :], ps[0:NE, 6, P:2 * P]).then_inc(rc, 1)

            def add_bias(t, half):
                e.wait_ge(gb_pe, 2 * t + half + 1)
                c = xr[:, t % XR, half * HALF:(half + 1) * HALF]
                e.tensor_tensor(c, c, ps[:, 7, :], ALU.add).then_inc(acc_d, 1)

            e.wait_ge(b1_t, 1)
            for t in range(T + 3):
                if 3 <= t:
                    add_bias(t - 3, 0)
                if 1 <= t <= T:
                    h_low(t - 1)
                if 2 <= t <= T + 1:
                    place(t - 2)
                if 3 <= t:
                    add_bias(t - 3, 1)
                if t == T:
                    for a in (xt_hi, xt_lo, act_hi):
                        e.memset(a, 0.0).then_inc(dch, 1)
                if t == T + 1:
                    e.wait_ge(tr_pe, T)
                    all_stored(e, h_st)
                    for a in (act_lo, y_sb, glu, lin, act):
                        e.memset(a, 0.0).then_inc(dch, 1)
                if t < T:
                    residual(t)
                if 1 <= t <= T:
                    route(t - 1)
                if t < T:
                    normed(t)
                if 1 <= t <= T:
                    route_gates(t - 1)

            def step(ins, n):
                ins.then_inc(it_d, 1)
                e.wait_ge(it_d, n)
            q = slice(0, NE)
            e.wait_ge(cnt_pe, 1)
            step(e.tensor_copy(cnt[q], ps[q, 6, 2 * P:2 * P + 1]), 1)
            step(e.tensor_scalar(xe[q], cnt[q], float(ITEM_ROWS), None, ALU.is_gt), 2)
            step(e.scalar_tensor_tensor(out=xe[q], in0=cnt[q], scalar=2.0 * ITEM_ROWS, in1=xe[q], op0=ALU.is_gt, op1=ALU.add), 3)
            step(e.scalar_tensor_tensor(out=xe[q], in0=cnt[q], scalar=3.0 * ITEM_ROWS, in1=xe[q], op0=ALU.is_gt, op1=ALU.add), 4)
            e.wait_ge(st_pe, 1)
            step(e.tensor_copy(st[q], ps[q, 6, 2 * P + 2:2 * P + 3]), 5)
            step(e.tensor_tensor(en[q], st[q], xe[q], ALU.add), 6)
            step(e.tensor_scalar(mt[q], cs["extra"][q], st[q], None, ALU.is_ge), 7)
            step(e.scalar_tensor_tensor(out=mt[q], in0=cs["extra"][q], scalar=en[q], in1=mt[q], op0=ALU.is_lt, op1=ALU.mult), 8)
            step(e.tensor_scalar(rr[q], cs["extra"][q], st[q], 1.0, ALU.subtract, ALU.add), 9)
            step(e.tensor_scalar(itm[q, 0, NE:ITEMS], mt[q], cs["e"][q], None, ALU.mult), 10)
            step(e.tensor_copy(itm[q, 0, 0:NE], cs["item_e"][q, 0:NE]), 11)
            step(e.tensor_scalar(t1[q], rr[q], float(ITEM_ROWS), cs["e_row"][q], ALU.mult, ALU.add), 12)
            step(e.tensor_tensor(itm[q, 1, NE:ITEMS], t1[q], mt[q], ALU.mult), 13)
            step(e.tensor_copy(itm[q, 1, 0:NE], cs["item_row"][q, 0:NE]), 14)
            step(e.tensor_scalar(t1[q], rr[q], -float(ITEM_ROWS), cnt[q], ALU.mult, ALU.add), 15)
            step(e.tensor_tensor(itm[q, 2, NE:ITEMS], t1[q], mt[q], ALU.mult), 16)
            step(e.tensor_scalar(itm[q, 2, 0:NE], cs["eye"][q], cnt[q], None, ALU.mult), 17)
            step(e.tensor_scalar(itm[q, 3, :], cs["item_e"][q], 0.0, xe[q], ALU.mult, ALU.add), 18)
            e.wait_ge(row_pe, 1)
            row = ps[0:1, 7, 0:4 * ITEMS]
            step(e.tensor_copy(items_flat[0:1, 0:2 * ITEMS], row[:, 0:2 * ITEMS]), 19)
            step(e.tensor_scalar(items_flat[0:1, 2 * ITEMS:3 * ITEMS], row[:, 2 * ITEMS:3 * ITEMS], float(ITEM_ROWS), None, ALU.min), 20)
            e.tensor_scalar(items_flat[0:1, 3 * ITEMS:4 * ITEMS], row[:, 3 * ITEMS:4 * ITEMS], float(NE - 1), None, ALU.add).then_inc(items_ready, 1)
            mixer_split(e, 7)

            e.wait_ge(dch, DCH0)

            def rows_low(i, n, first=False):
                e.wait_ge(t_done, i + 1)
                src = ps[:, 0:2, :].rearrange("p a (k c) -> p (a k) c", c=P)
                if first:
                    e.tensor_scalar(xt_hi[:, :, P:2 * P], src, X_SCALE, None, ALU.mult).then_inc(clr, 1)
                    e.wait_ge(clr, 1)
                    e.scalar_tensor_tensor(out=xt_lo[:, :, P:2 * P], in0=src, scalar=X_SCALE, in1=xt_hi[:, :, P:2 * P],
                                           op0=ALU.mult, op1=ALU.subtract)
                else:
                    after_waits(e)
                    with e.If(n > P):
                        e.tensor_scalar(xt_hi[:, :, P:2 * P], src, X_SCALE, None, ALU.mult)
                        e.drain()
                        e.scalar_tensor_tensor(out=xt_lo[:, :, P:2 * P], in0=src, scalar=X_SCALE, in1=xt_hi[:, :, P:2 * P],
                                               op0=ALU.mult, op1=ALU.subtract)
                e.wait_ge(xt_hd, i + 1)
                src = ps[:, 4:6, :] if first else ps[:, 6:8, :]
                e.scalar_tensor_tensor(out=xt_lo[:, :, 0:P], in0=src.rearrange("p a (k c) -> p (a k) c", c=P), scalar=X_SCALE,
                                       in1=xt_hi[:, :, 0:P], op0=ALU.mult, op1=ALU.subtract).then_inc(xt_ready, 1)

            def clip(i, u, expert, w):
                e.wait_ge(used, i * ITEM_UNITS + (u + 1))
                e.wait_ge(dch, i * 32 + (DCH0 + (MADE[u - 1] if u else 0)))
                for p in range(2):
                    bank, j = 2 * (u % 2) + p, 2 * u + p
                    e.tensor_scalar(glu[:, p, 0:w], ps[:, bank, 0:w], g_top[:, j, bass.ds(expert, 1)],
                                    g_add[:, j, bass.ds(expert, 1)], ALU.min, ALU.add).then_inc(dch, 1)
                    e.tensor_scalar(lin[:, p, 0:w], ps[:, bank, ITEM_ROWS:ITEM_ROWS + w], l_top[:, j, bass.ds(expert, 1)],
                                    l_low[:, j, bass.ds(expert, 1)], ALU.min, ALU.max).then_inc(dch, 1)

            def make(i, u, expert, w):
                e.wait_ge(sig_a, i * 4 + (u + 1))
                e.scalar_tensor_tensor(out=gs[:, :, 0:w], in0=glu[:, :, 0:w], scalar=X_SCALE / Z_SCALE ** 2, in1=sig[:, :, 0:w],
                                       op0=ALU.mult, op1=ALU.mult).then_inc(dch, 1)
                e.wait_ge(dch, i * 32 + (DCH0 + MADE[u] - 2))
                for p in range(2):
                    e.scalar_tensor_tensor(out=act[:, p, 0:w], in0=lin[:, p, 0:w], scalar=l_add[:, 2 * u + p, bass.ds(expert, 1)],
                                           in1=gs[:, p, 0:w], op0=ALU.add, op1=ALU.mult).then_inc(dch, 1)

            def act_low(i, u, w):
                e.wait_ge(ahi_a, i * 4 + (u + 1))
                e.tensor_tensor(act_lo[:, 2 * u:2 * u + 2, 0:w], act[:, :, 0:w], act_hi[:, 2 * u:2 * u + 2, 0:w],
                                ALU.subtract).then_inc(dch, 1)

            def output(i, half, w):
                e.wait_ge(used, i * ITEM_UNITS + (W1_UNITS + half + 1))
                if half == 0:
                    e.wait_ge(ysc[0], i * 16 + 16)
                    e.wait_ge(ysc[1], i * 16 + 16)
                gate = [idx_all[:, bass.ds(i, 1), blk, 1].bitcast(F32) for blk in range(2)]
                for blk in reversed(range(w // P)):
                    last = e.tensor_scalar(y_sb[:, blk, half * HALF:(half + 1) * HALF], ps[:, 4 + 2 * half + blk, :], gate[blk],
                                           1.0 / Z_SCALE, ALU.mult, ALU.mult)
                last.then_inc(yd, 1)

            def item_of_width(i, expert, w, n_next):
                clip(i, 0, expert, w)
                item_lo_dve(e, i, 2)
                make(i, 0, expert, w)
                for u in (1, 2):
                    clip(i, u, expert, w)
                    act_low(i, u - 1, w)
                    item_lo_dve(e, i, u + 2)
                    make(i, u, expert, w)
                clip(i, 3, expert, w)
                act_low(i, 2, w)
                make(i, 3, expert, w)
                act_low(i, 3, w)
                if n_next is not None:
                    rows_low(i + 1, n_next)
                item_lo_dve(e, i, 5)
                for half in range(W2_UNITS):
                    output(i, half, w)
                    if n_next is not None:
                        item_lo_dve(e, i, 6 + half)

            def item(i, n_last):
                n = e.value_load(items_flat[0:1, bass.ds(i + 2 * ITEMS, 1)], min_val=0, max_val=ITEM_ROWS)
                expert = e.value_load(items_flat[0:1, bass.ds(i, 1)], min_val=0, max_val=NE - 1)
                n_next = None
                if not n_last:
                    n_next = e.value_load(items_flat[0:1, bass.ds(i + (2 * ITEMS + 1), 1)], min_val=0, max_val=ITEM_ROWS)
                with e.If(n > P):
                    item_of_width(i, expert, ITEM_ROWS, n_next)
                with e.Else():
                    item_of_width(i, expert, P, n_next)

            e.wait_ge(items_ready, 1)
            last_item = e.value_load(items_flat[0:1, W_LAST:W_LAST + 1], min_val=NE - 1, max_val=ITEMS - 1)
            rows_low(0, None, first=True)
            e.wait_ge(lists_ready, 1)
            with e.Fori(0, last_item) as i:
                item(i, False)
            item(last_item, True)

            e.wait_ge(gf_in, 16)
            for t in range(T):
                e.wait_ge(f_rs, t + 2)
                e.scalar_tensor_tensor(out=fin[:, t % 6, :], in0=fin[:, t % 6, :], scalar=rs3[:, t:t + 1], in1=g_final,
                                       op0=ALU.mult, op1=ALU.mult).then_inc(f_d, 1)

        @block.gpsimd
        def _(e):
            pool_engine[0] = e
            e.wait_ge(c_in, N_CONST_DMAS)
            e.wait_ge(g_in, 16)
            e.tensor_scalar(g_mix, g_mix, OUT_SCALE, 0.0, ALU.mult, ALU.add).then_inc(setup, 1)
            e.tensor_scalar(par["b_a"], par["b_a"], Z_SCALE, 0.0, ALU.mult, ALU.add).then_inc(setup, 1)
            e.tensor_scalar(par["w_dw"], par["w_dw"], 1.0 / Z_SCALE, 0.0, ALU.mult, ALU.add).then_inc(setup, 1)
            gains = pr[:, PARAMS["g_attn"][0]:PARAMS["g_conv"][1]]
            e.tensor_scalar(gains, gains, X_SCALE, 0.0, ALU.mult, ALU.add).then_inc(setup, 1)
            e.tensor_scalar(neg_sinks, par["sinks"], -1.0, 0.0, ALU.mult, ALU.add).then_inc(setup, 1)

            def rstd(dst, src, k):
                e.tensor_scalar(dst, src, D * EPS, 0.0, ALU.add, ALU.add).then_inc(eps_p, 1)
                e.wait_ge(eps_p, k)
                return e.tensor_tensor(dst, dst, cs["power"], ALU.pow)

            for t in range(T):
                e.wait_ge(x_sq, t + 1)
                if t == 0:
                    e.wait_ge(setup, 1)
                rstd(rs1[:, t:t + 1], ss1[:, t:t + 1], t + 1).then_inc(x_rs, 1)
                if t in (3, 5, 7):
                    mixer_split(e, (3, 5, 7).index(t))
            e.tensor_copy(ident_b, cs["ident"]).then_inc(setup, 1)
            e.tensor_copy(before_b, cs["before"]).then_inc(setup, 1)
            e.tensor_copy(ones_b, cs["ones"]).then_inc(setup, 1)
            e.tensor_copy(band_b, band_f).then_inc(setup, 1)
            e.tensor_scalar(mean_w, cs["ones"], 1.0 / CW, 0.0, ALU.mult, ALU.add).then_inc(setup, 1)
            tap_sums = conv[:, :, DVE_TOKENS:SEQ]
            n = 0
            for c in range(CT):
                e.wait_ge(ev_d, 2 * c + 2)
                if c == 0:
                    e.wait_ge(x_sq, T)
                    e.wait_ge(setup, 5)
                for k in range(TAPS):
                    src, w = cu[c][:, DVE_TOKENS + k:SEQ + k], par["w_dw"][:, c * TAPS + k:c * TAPS + k + 1]
                    if k == 0:
                        e.tensor_scalar(tap_sums[:, c, :], src, w, par["b_dw"][:, c:c + 1], ALU.mult, ALU.add).then_inc(tap_p, 1)
                        continue
                    if n >= 2:
                        e.wait_ge(tap_p, c * TAPS + k - 1)
                    e.tensor_scalar(tap_part[:, n % 2, :], src, w, 0.0, ALU.mult, ALU.add).then_inc(tap_m, 1)
                    n += 1
                    e.wait_ge(tap_m, n)
                    e.wait_ge(tap_p, c * TAPS + k)
                    e.tensor_tensor(tap_sums[:, c, :], tap_sums[:, c, :], tap_part[:, (n - 1) % 2, :], ALU.add).then_inc(tap_p, 1)
                if c in (1, 2):
                    mixer_split(e, 2 + c)
            mixer_split(e, 5)

            def affine(h):
                for j in range(CT):
                    c = conv[:, j, h * HALF:(h + 1) * HALF]
                    e.wait_ge(sgm_a, CT * h + j + 1)
                    e.tensor_scalar(c, c, par["ln_g"][:, j:j + 1], par["ln_b"][:, j:j + 1], ALU.mult, ALU.add).then_inc(z_p, 1)

            def mixed_lo(i):
                h = i % 2
                for j in range(CT):
                    src = conv[:, j, h * HALF:(h + 1) * HALF] if i < 2 else heads[h][:, j, :]
                    at = j + (CT if i < 2 else 0)
                    e.wait_ge(mhi_a, CT * i + j + 1)
                    e.tensor_tensor(mix_lo[:, at, h * HALF:(h + 1) * HALF], src, mix_hi[:, at, h * HALF:(h + 1) * HALF],
                                    ALU.subtract).then_inc(mlo_p, 1)

            for n in range(2 * T):
                lo = 0 if n // KV else P
                e.wait_ge(rden_d, n + 1)
                for j in range(GROUP):
                    pj = prob[:, n % 2, j, lo:2 * P]
                    e.tensor_scalar(pj, pj, rden[:, n % 2, j:j + 1], 0.0, ALU.mult, ALU.add).then_inc(pn_p, 1)
                if n == 0:
                    affine(0)
                if n == 2:
                    mixed_lo(0)
                    affine(1)
                if n == 4:
                    mixed_lo(1)
                if n == 10:
                    mixed_lo(2)
            mixed_lo(3)
            mixer_split(e, 6)

            e.wait_ge(r_in, 64)
            e.tensor_scalar(g_ffn, g_ffn, D ** 0.5, 0.0, ALU.mult, ALU.add).then_inc(setup, 1)
            e.tensor_scalar(wr_hi.rearrange("p a b -> p (a b)"), wr, W_SCALE, 0.0, ALU.mult, ALU.add).then_inc(setup, 1)
            e.wait_ge(setup, 12)
            token = pay.rearrange("p t (k w) -> p t k w", w=2)
            e.tensor_copy(token[:, :, :, 0], cs["token"].unsqueeze(2).to_broadcast([P, T, TOPK])).then_inc(setup, 1)
            e.tensor_scalar(wr, wr, W_SCALE, 0.0, ALU.mult, ALU.add).then_inc(setup, 1)
            e.wait_ge(setup, 14)
            e.tensor_tensor(wr_lo.rearrange("p a b -> p (a b)"), wr, wr_hi.rearrange("p a b -> p (a b)"), ALU.subtract).then_inc(b1_t, 1)

            def residual_bias(t):
                e.wait_ge(xr_s[t % XR], 16 * (t // XR + 1))
                c = xr[:, t % XR, :]
                e.tensor_tensor(c, c, b_out, ALU.add).then_inc(xb_p, 1)

            def store_slots(t):
                e.wait_ge(rb, 4 * (t + 1))
                if t == 0:
                    e.wait_ge(init, 48)
                for k in range(TOPK):
                    e.indirect_dma_start(table, bass.IndirectOffsetOnAxis(ap=slots[:, t, k:k + 1], axis=0),
                                         pay[:, t, 2 * k:2 * k + 2], None).then_inc(scat, 16)

            residual_bias(0)
            for t in range(T + 2):
                if t < T:
                    e.wait_ge(x2sq, t + 1)
                    rstd(rs2[:, t:t + 1], ss2[:, t:t + 1], T + t + 1).then_inc(rs2_p, 1)
                if t + 1 < T:
                    residual_bias(t + 1)
                if t == 1:
                    e.wait_ge(b1_in, 16)
                    bg, bl = b1_sb[:, 0:KC, :], b1_sb[:, KC:2 * KC, :]
                    e.tensor_scalar(g_top, bg, -Z_SCALE, LIMIT * Z_SCALE, ALU.mult, ALU.add).then_inc(b1_t, 1)
                    e.tensor_scalar(g_add, bg, Z_SCALE, 0.0, ALU.mult, ALU.add).then_inc(b1_t, 1)
                    e.tensor_scalar(l_top, bl, -Z_SCALE, LIMIT * Z_SCALE, ALU.mult, ALU.add).then_inc(b1_t, 1)
                    e.tensor_scalar(l_low, bl, -Z_SCALE, -LIMIT * Z_SCALE, ALU.mult, ALU.add).then_inc(b1_t, 1)
                    e.tensor_scalar(l_add, bl, Z_SCALE, Z_SCALE, ALU.mult, ALU.add).then_inc(b1_t, 1)
                if t >= 2:
                    store_slots(t - 2)

            mixer_split(e, 7)
            e.wait_ge(items_ready, 1)
            last_item = e.value_load(items_flat[0:1, W_LAST:W_LAST + 1], min_val=NE - 1, max_val=ITEMS - 1)
            e.wait_ge(lists_ready, 1)

            def gather(blk, rows=P):
                e.indirect_dma_start(xg[0:rows, blk, :], None, h_rows, bass.IndirectOffsetOnAxis(ap=idx_g[0:rows, blk, 0:1], axis=0)).then_inc(xg_in[blk], 16)

            def scatter(blk, rows=P):
                e.indirect_dma_start(y_rows, bass.IndirectOffsetOnAxis(ap=idx_s[0:rows, blk, 0:1], axis=0), y_sb[0:rows, blk, :], None,
                                     compute_op=ALU.add).then_inc(ysc[blk], 16)

            def fetch_rows(k, n=None):
                e.tensor_copy(idx_g.rearrange("p a b -> p (a b)"), idx_all[:, bass.ds(k, 1), :, :].rearrange("p a b w -> p (a b w)")).then_inc(ig, 1)
                e.wait_ge(ig, k + 1)
                after_waits(e)
                gather(0)
                if n is None:
                    gather(1)
                else:
                    with e.If(n > P):
                        gather(1)
                    with e.Else():
                        gather(1, FEW)

            def scatter_rows(i, n, k):
                e.wait_ge(ysc[0], k)
                e.wait_ge(ysc[1], k)
                after_waits(e)
                e.tensor_copy(idx_s.rearrange("p a b -> p (a b)"), idx_all[:, bass.ds(i, 1), :, :].rearrange("p a b w -> p (a b w)")).then_inc(is_, 1)
                e.wait_ge(is_, i + 2)
                e.wait_ge(yd, i * 2 + 2)
                after_waits(e)
                scatter(0)
                with e.If(n > P):
                    scatter(1)
                with e.Else():
                    scatter(1, FEW)

            def item(i, n_last):
                n = e.value_load(items_flat[0:1, bass.ds(i + 2 * ITEMS, 1)], min_val=0, max_val=ITEM_ROWS)
                if not n_last:
                    n_next = e.value_load(items_flat[0:1, bass.ds(i + (2 * ITEMS + 1), 1)], min_val=0, max_val=ITEM_ROWS)
                    e.wait_ge(t_done, i + 1)
                    after_waits(e)
                    fetch_rows(i + 1, n_next)
                for v in range(2, 6 if n_last else 8):
                    item_lo_pool(e, i, v)
                scatter_rows(i, n, i * 16 + 16)

            all_stored(e, h_st)
            e.wait_ge(out_pe, 2 * T)
            fetch_rows(0)
            all_stored(e, acc_st)
            e.tensor_copy(idx_s.rearrange("p a b -> p (a b)"), idx_all[:, 0, :, :].rearrange("p b w -> p (b w)")).then_inc(is_, 1)
            e.wait_ge(is_, 1)
            e.wait_ge(dch, DCH0)
            scatter(0, FEW)
            scatter(1, FEW)
            with e.Fori(0, last_item) as i:
                item(i, False)
            item(last_item, True)

            e.wait_ge(gf_in, 16)
            e.tensor_scalar(g_final, g_final, D ** 0.5, 0.0, ALU.mult, ALU.add).then_inc(f_rs, 1)
            for t in range(T):
                e.wait_ge(f_sq, t + 1)
                rstd(rs3[:, t:t + 1], ss3[:, t:t + 1], 2 * T + t + 1).then_inc(f_rs, 1)


def _constants(np):
    c = np.zeros((P, N_CONSTS), np.float32)

    def put(name, a):
        lo, hi = CONSTS[name]
        c[:a.shape[0], lo:hi] = a
    r = np.arange(P)
    put("ident", np.eye(P))
    put("before", r[:, None] < r[None, :])
    put("ones", np.ones((P, P)))
    ahead = np.arange(2 * P)[None, :] - r[:, None]
    put("band", np.where((ahead >= 1) & (ahead <= P), 0.0, -1e30))
    put("iota", np.tile(np.arange(NE), (P, 1)))
    put("base", np.tile(np.arange(NE) * SEQ, (P, 1)))
    put("token", r[:, None] + P * np.arange(T)[None, :])
    ne = np.arange(NE)
    e_of = np.zeros((NE, ITEMS))
    e_of[ne, ne] = ne
    put("item_e", e_of)
    put("item_row", e_of * SEQ)
    put("eye", np.eye(NE))
    put("extra", np.tile(np.arange(EXTRA), (P, 1)))
    put("power", np.full((P, 1), -0.5))
    put("e", ne[:, None])
    put("e_row", ne[:, None] * SEQ)
    slot = np.arange(NE * SEQ)
    table = np.stack([SEQ + slot % SPARE, 0 * slot], axis=1).astype(np.uint32)
    return c, table


def kernel(**inputs):
    import numpy as np
    import concourse.bacc as bacc
    from concourse.bass_utils import run_bass_kernel_spmd as run

    a = {k: np.asarray(v) for k, v in inputs.items()}
    w_in, w_out, w1, w2 = a["w_in"][0], a["w_out"][0], a["w1"][0], a["w2"][0]
    att, kvw = HEADS * HD, KV * HD

    def chunks(w):
        return w.reshape(w.shape[0] // P, P, w.shape[1]).transpose(1, 0, 2)

    order = np.arange(att).reshape(KV, GROUP, HD).transpose(1, 0, 2).reshape(-1)
    conv_a, gate = w_in[:, att + 2 * kvw:att + 2 * kvw + CW], w_in[:, att + 2 * kvw + CW:]
    glu_cols = [np.concatenate([m[:, c * P:(c + 1) * P] for c in (2 * i, 2 * i + 1) for m in (gate, conv_a)], axis=1) for i in range(2)]
    q_cols = w_in[:, :att][:, order]
    wo = np.concatenate([w_out[:att][order], w_out[att:]], axis=0)
    units = [chunks(m) for m in (glu_cols[0], glu_cols[1], q_cols, wo[:, :HALF], wo[:, HALF:])]
    up = w1.reshape(NE, KC, P, W1_UNITS, 2, P, 2).transpose(0, 3, 2, 1, 4, 6, 5).reshape(NE, W1_UNITS, P, UNIT)
    down = w2.reshape(NE, KC, P, W2_UNITS, HALF).transpose(0, 3, 2, 1, 4).reshape(NE, W2_UNITS, P, UNIT)
    experts = np.concatenate([up, down], axis=1).reshape(NE * ITEM_UNITS, P, UNIT)
    w_units = np.concatenate([np.stack([u.reshape(P, UNIT) for u in units]), experts], axis=0)
    w_kv = np.ascontiguousarray(chunks(w_in[:, att:att + 2 * kvw]).reshape(P, KV_UNIT))

    def cols(v):
        return v.reshape(-1, P).T
    b_in = a["b_in"][0]
    b_conv, b_gate = b_in[att + 2 * kvw:att + 2 * kvw + CW], b_in[att + 2 * kvw + CW:]
    params = np.concatenate([
        cols(b_gate), cols(b_conv), cols(b_in[:att][order]), cols(b_in[att:att + kvw]),
        a["w_dw"][0].reshape(TAPS, CT, P).transpose(2, 1, 0).reshape(P, CT * TAPS), cols(a["b_dw"][0]),
        cols(a["ln_g"][0]), cols(a["ln_b"][0]), cols(a["g_attn_out"][0][order]), cols(a["g_conv_out"][0]),
        np.broadcast_to(a["sinks"][0], (P, HEADS))], axis=1)
    rows = np.stack([np.broadcast_to(v, (P, D)) for v in (a["g_mix"][0], a["b_out"][0], a["g_ffn"][0], a["g_final"])])
    b1 = a["b1"][0].reshape(NE, KC, P, 2).transpose(2, 3, 1, 0).reshape(P, 2 * KC * NE)
    w_router = chunks(a["w_router"][0]).reshape(P, KC * NE)
    consts, table0 = _constants(np)
    arrays = {
        "x": a["x"][0], "w_units": w_units, "w_kv": w_kv, "params": params, "rows": rows,
        "b_v": np.broadcast_to(b_in[att + kvw:att + 2 * kvw], (P, P)), "b_router": np.broadcast_to(a["b_router"][0], (P, NE)),
        "w_router": w_router, "b1": b1, "b2": a["b2"][0], "consts": consts, "table0": table0,
        "zeros": np.zeros((SPARE, D), np.float32),
    }
    arrays = {f"in_{k}": np.ascontiguousarray(v) for k, v in arrays.items()}
    nc = bacc.Bacc("TRN2", target_bir_lowering=False, num_devices=1)
    args = [nc.dram_tensor(k, v.shape, mybir.dt.from_np(v.dtype), kind="ExternalInput").ap() for k, v in arrays.items()]
    out = nc.dram_tensor("out", (SEQ, D), F32, kind="ExternalOutput").ap()
    hymba_layer_kernel(nc, *args, out)
    r = run(nc, [arrays], core_ids=[0])
    return r.results[0]["out"].reshape(1, SEQ, D)
```

```python
import concourse.bass as bass
from concourse import mybir
from contextlib import ExitStack

F32 = mybir.dt.float32
F16 = mybir.dt.float16
BF16 = mybir.dt.bfloat16
U32 = mybir.dt.uint32
I32 = mybir.dt.int32
ALU = mybir.AluOpType
ACT = mybir.ActivationFunctionType
AXX = mybir.AxisListType.X

P = 128
SEQ = 1024
D = 1024
T = SEQ // P
KC = D // P
HEADS, KV, HD = 8, 2, 64
GROUP = HEADS // KV
CW = 512
CT = CW // P
TAPS = 31
NE, TOPK = 32, 4
HALF = 512
UNIT = KC * HALF
KV_UNIT = KC * 256
RING = 3
RAW_SLOT, RAW_BACK = (0, 1, 2, 3, 4, 2), (6, 6, 3, 6, 6, 3)
MIX_UNITS = 6
W1_UNITS, W2_UNITS = 4, 2
ITEM_UNITS = W1_UNITS + W2_UNITS
ITEM_ROWS = 256
WIDTHS = (64, 96, 128, 144, 160, 176, 192, 208, 224, 240, 256)
ITEMS = NE + SEQ * TOPK // ITEM_ROWS
EXTRA = ITEMS - NE
DVE_TOKENS = 704
PARTS = 3
GLU_EVERY = 22
XR = 6
FEW = 16
SPARE = ITEM_ROWS
DVE_SPLIT = 2560
W_SCALE, X_SCALE = 64.0, 16.0
Z_SCALE = W_SCALE * X_SCALE
LIMIT, ALPHA = 7.0, 1.702
EPS = 1e-5
SCORE_SCALE = HD ** -0.5
OUT_SCALE = X_SCALE * D ** 0.5

PARAMS = {}
_at = 0
for _name, _n in (("b_gate", CT), ("b_a", CT), ("b_q", GROUP), ("b_k", 1), ("w_dw", CT * TAPS), ("b_dw", CT),
                  ("ln_g", CT), ("ln_b", CT), ("g_attn", CT), ("g_conv", CT), ("sinks", HEADS)):
    PARAMS[_name] = (_at, _at + _n)
    _at += _n
N_PARAMS = _at
CONSTS = {}
_at = 0
for _name, _n in (("ident", P), ("before", P), ("ones", P), ("iota", NE), ("base", NE),
                  ("token", T), ("item_e", ITEMS), ("item_row", ITEMS), ("eye", NE), ("extra", EXTRA), ("e", 1), ("e_row", 1), ("power", 1),
                  ("band", 2 * P)):
    CONSTS[_name] = (_at, _at + _n)
    _at += _n
N_CONSTS = _at


def hymba_layer_kernel(nc, x, w_units, w_kv, params, rows, b_v, b_router, w_router, b1, b2, consts, table0, zeros, out):
    h_rows = nc.dram_tensor("h_rows", (SEQ + SPARE, D), F32, kind="Internal").ap()
    y_rows = nc.dram_tensor("y_rows", (SEQ + SPARE, D), F32, kind="Internal").ap()
    table = nc.dram_tensor("slot_table", (NE * SEQ, 2), U32, kind="Internal").ap()

    ctx = ExitStack()
    with ctx:
        def sem(name):
            return ctx.enter_context(nc.semaphore(name))

        raw = ctx.enter_context(nc.sbuf_tensor("raw", [P, RING, UNIT], F32))
        whi = ctx.enter_context(nc.sbuf_tensor("whi", [P, RING, UNIT], F16))
        wlo = ctx.enter_context(nc.sbuf_tensor("wlo", [P, RING, UNIT], F16))
        KB = 256
        arena = ctx.enter_context(nc.sbuf_tensor("arena", [P, 111 * KB + 192], F32))
        ps = ctx.enter_context(nc.psum_tensor("ps", [P, 8, HALF], F32))

        def view(word, shape, dt=F32):
            n = 1
            for s in shape:
                n *= s
            words = n * (4 if dt in (F32, U32, I32) else 2) // 4
            v = arena[:, int(word):int(word) + words]
            if dt != F32:
                v = v.bitcast(dt)
            if len(shape) == 2:
                v = v.rearrange("p (a b) -> p a b", a=shape[0])
            if len(shape) == 3:
                v = v.rearrange("p (a b c) -> p a b c", a=shape[0], b=shape[1])
            return v

        A, B, C, DD, G, E, K = 0, 32 * KB, 56 * KB, 65 * KB, 81 * KB, 93 * KB, 101 * KB
        u_hi = view(A, (KC, SEQ), F16)
        u_lo = view(A + 16 * KB, (KC, SEQ), F16)
        q_t = view(B, (GROUP, SEQ))
        k_t = view(B + 16 * KB, (SEQ,))
        v_sb = view(B + 20 * KB, (T, P))
        cu = [view(C, (TAPS - 1 + SEQ,)), view(C + TAPS - 1 + SEQ, (TAPS - 1 + SEQ,)),
              view(G, (TAPS - 1 + SEQ,)), view(G + TAPS - 1 + SEQ, (TAPS - 1 + SEQ,))]
        conv = view(DD, (CT, SEQ))
        tap_part = view(G + 2 * (TAPS - 1 + SEQ), (PARTS, SEQ - DVE_TOKENS))
        x_in = view(B, (XR, D))
        xn = view(G, (2, D))
        g_mix = view(E, (D,))
        band_f = view(E + 4 * KB, (2 * P,))
        sg = view(E, (2, HALF))
        mix_hi = view(A, (2 * CT, SEQ), F16)
        mix_lo = view(A + 16 * KB, (2 * CT, SEQ), F16)
        prob = view(G, (2, GROUP, 2 * P))
        prob_t = view(G + 8 * KB, (2, HALF))
        sq = view(E, (CT, HALF))
        heads = [view(C, (CT, HALF)), view(DD, (CT, HALF))]
        xr = view(B, (XR, D))
        h_sb = view(DD, (D,))
        h_pair = view(DD + 4 * KB, (2, 2 * D), F16)
        h_pair_f = view(DD + 4 * KB, (2, D))
        b_out = view(G, (D,))
        g_ffn = view(G + 4 * KB, (D,))
        ht_hi = view(G + 8 * KB, (KC, P), F16)
        ht_lo = view(G + 10 * KB, (KC, P), F16)
        b2_sb = view(E, (D,))
        wr = view(E + 4 * KB, (KC * NE,))
        wr_hi = view(E + 5 * KB, (KC, NE), F16)
        wr_lo = view(E + 5.5 * KB, (KC, NE), F16)
        xg = view(A, (2, D))
        xg_pair = view(A, (2, 2 * D), F16)
        xt_hi = view(A + 8 * KB, (KC, ITEM_ROWS), F16)
        xt_lo = view(A + 12 * KB, (KC, ITEM_ROWS), F16)
        act_hi = view(A + 16 * KB, (KC, ITEM_ROWS), F16)
        act_lo = view(A + 20 * KB, (KC, ITEM_ROWS), F16)
        y_sb = view(A + 24 * KB, (2, D))
        b1_sb = view(C, (2 * KC, NE))
        g_top = view(C + 2 * KB, (KC, NE))
        g_add = view(C + 3 * KB, (KC, NE))
        l_top = view(C + 4 * KB, (KC, NE))
        l_low = view(C + 5 * KB, (KC, NE))
        l_add = view(C + 6 * KB, (KC, NE))
        glu = view(DD, (2, ITEM_ROWS))
        lin = view(DD + 2 * KB, (2, ITEM_ROWS))
        sig = view(DD + 4 * KB, (2, ITEM_ROWS))
        gs = view(DD + 6 * KB, (2, ITEM_ROWS))
        act = view(DD + 8 * KB, (2, ITEM_ROWS))
        idx_all = view(DD + 10 * KB, (ITEMS, 2, 2), U32)
        idx_g = view(DD + 11 * KB, (2, 2), U32)
        idx_s = view(DD + 11 * KB + 4, (2, 2), U32)
        raw_slots = [raw[:, s, :] for s in range(RING)] + [view(B + 8 * KB, (UNIT,)), view(G, (UNIT,))]
        fin = view(B, (T, D))
        g_final = view(G, (D,))
        kat = [K]

        def small(shape, dt=F32):
            n = 1
            for s in shape:
                n *= s
            w = kat[0]
            kat[0] += (n * (4 if dt in (F32, U32, I32) else 2) + 7) // 8 * 2
            assert kat[0] <= 111 * KB + 192
            return view(w, shape, dt)

        cs = {}
        cs_all = small((CONSTS["band"][0],))
        for name, (a, b) in CONSTS.items():
            if name != "band":
                cs[name] = cs_all[:, a:b]
        pr = small((N_PARAMS,))
        par = {name: pr[:, a:b] for name, (a, b) in PARAMS.items()}
        ident_h = small((P,), F16)
        ident_b = small((P,), BF16)
        before_b = small((P,), BF16)
        ones_b = small((P,), BF16)
        band_b = small((2 * P,), BF16)
        mean_w = small((P,))
        rs = small((2, HALF))
        neg_sinks = small((HEADS,))
        ss1, rs1, ss2, rs2, ss3, rs3 = (small((T,)) for _ in range(6))
        nm, dsk, rsum, esum, rden, mxs = (small((2, GROUP)) for _ in range(6))
        bv_sb = view(E + 6 * KB, (P,))
        br_sb = small((NE,))
        lg = small((NE,))
        mx8 = small((8,))
        ix8 = small((8,), U32)
        ixf = small((TOPK,))
        nm0 = small((1,))
        ex = small((TOPK,))
        se = small((1,))
        rse = small((1,))
        oh = view(E + 6 * KB, (2, TOPK, NE))
        gk = view(E + 7 * KB, (TOPK, NE))
        gates_g = small((NE,))
        posb = small((NE,))
        slf = small((TOPK,))
        slots = view(DD + 13 * KB, (T, TOPK), U32)
        pay = view(DD + 13 * KB + 32, (T, TOPK * 2), U32)
        mb = view(DD + 13 * KB + 96, (T, NE), BF16)
        gt_sb = view(E + 7.5 * KB, (P,))
        cnt, xe, st, en = (small((1,)) for _ in range(4))
        itm = view(DD + 14 * KB, (4, ITEMS))
        mt, rr, t1 = (view(DD + 15 * KB + 64 * i, (EXTRA,)) for i in range(3))
        items = view(DD + 12 * KB, (4, ITEMS), I32)

        W_LAST = 3 * ITEMS

        raw_full = [sem(f"raw_full{s}") for s in range(max(RAW_SLOT) + 1)]
        hi_done, lo_dve, lo_pool, raw_scaled = sem("hi_done"), sem("lo_dve"), sem("lo_pool"), sem("raw_scaled_pool")
        c_in, id_in, g_in, xin = sem("consts_loaded"), sem("shape_consts_loaded"), sem("g_mix_loaded"), [sem(f"x_loaded{i}") for i in range(XR)]
        step_pool, step_dve = sem("waits_passed_pool"), sem("waits_passed_dve")
        setup, eps_p = sem("setup_pool"), sem("eps_added")
        setup_d = sem("setup_dve")
        x_sq, x_rs, x_nd, x_tr, u_hd, u_ld = (sem(n) for n in ("x_squared", "x_rstd", "x_normed", "x_transposed", "u_hi_done", "u_lo_done"))
        proj, ev_a, ev_d = sem("proj_done"), sem("proj_read_act"), sem("proj_read_dve")
        tap_d, tap_p, tap_m = sem("taps_dve"), sem("taps_pool"), sem("tap_products_pool")
        mean_pe, sub_d, vsq_a, var_pe, ve_d, root_a, rstd_d = (sem(n) for n in ("mean_done", "centred", "centred_squared", "var_done", "var_copied", "root_done", "rstd_done"))
        y_d, sgm_a, z_p, s_d, csq_a, ms_pe, mse_d, m_d, mhi_a, mlo_p = (sem(n) for n in (
            "ln_scaled", "swish_sigmoid", "ln_affine", "swish_done", "branch_squared", "meansq_done", "meansq_copied", "branch_normed", "mix_hi_done", "mix_lo_done"))
        sc_pe, mx_d, nm_d, dsk_d, exp_a, den_d, rden_d, pn_p, pt_pe, pta, ptd, ot_pe, og_a = (sem(n) for n in (
            "scores_done", "row_max", "neg_max", "sink_shift", "exp_done", "denominator", "rden", "probs_normed", "probs_transposed", "prob_t_act", "prob_t_dve", "heads_done", "heads_read"))
        rows_in = sem("residual_consts")
        r_in, xb_p, out_pe, x2_d, x2sq, rs2_p, h_d, hh_a, hl_d, tr_pe, hth, htl = (sem(n) for n in (
            "route_consts", "xb_done", "out_done", "x2_done", "x2_squared", "x2_rstd", "h_done", "h_hi_done", "h_lo_done", "h_transposed", "ht_hi_done", "ht_lo_done"))
        h_st, acc_st = [sem(f"h_stored{i}") for i in range(2)], [sem(f"acc_stored{i}") for i in range(XR)]
        xr_s = [sem(f"xr_loaded{i}") for i in range(XR)]
        rt_pe, ra, ea, gt_pe, rc, gb_pe, acc_d, scat = (sem(n) for n in (
            "router_done", "route_step", "gate_exp", "gates_transposed", "gates_t_copied", "gate_bias_done", "acc_done", "slots_stored"))
        rb = sem("slot_step")
        init = sem("tables_initialised")
        cnt_pe, it_d, st_pe, row_pe, items_ready = (sem(n) for n in ("counts_done", "item_step", "starts_done", "item_rows_done", "items_ready"))
        b1_in, b1_t, idx_in, lists_ready = sem("b1_loaded"), sem("b1_tables"), sem("lists_loaded"), sem("lists_ready")
        used, xt_ready, xt_hd, t_done = (sem(n) for n in ("units_used", "xt_ready", "xt_hi_done", "rows_transposed"))
        ig, is_, xg_in = sem("idx_gather"), sem("idx_scatter"), [sem("rows_gathered0"), sem("rows_gathered1")]
        dch, sig_a, ahi_a, yd, ysc = sem("dve_expert_step"), sem("sigmoid_done"), sem("act_hi_done"), sem("y_done"), [sem("y_scattered0"), sem("y_scattered1")]
        f_in = [sem(f"final_loaded{i}") for i in range(T)]
        gf_in, f_sq, f_rs, f_d, f_st = (sem(n) for n in ("g_final_loaded", "final_squared", "final_rstd", "final_done", "final_stored"))

        block = ctx.enter_context(nc.Block())

        def unit_cols(u):
            return KV_UNIT if u == 3 else UNIT

        def proj_reader(n):
            if n < 16:
                c, r = n // 4, n % 4
                return (ev_a, 2 * c + r + 1) if r < 2 else (ev_d, 2 * c + r - 1)
            return (ev_a, 8 + n - 15) if n < 26 else (ev_d, 8 + n - 25)

        def wait_mix_unit_used(e, u):
            e.wait_ge(*((proj, (8, 16, 24, 28)[u]) if u < 4 else (out_pe, 2 * T)))

        def wait_split(e, u):
            e.wait_ge(lo_dve, u + 1)
            e.wait_ge(lo_pool, u + 1)

        def chunks_of(bank):
            return ps[:, bank, :].bitcast(F16).rearrange("p (k c) -> p k c", c=P)

        def split_hi(e, src, slot, n):
            e.activation(whi[:, slot, 0:n], src[:, 0:n], ACT.Copy, scale=W_SCALE).then_inc(hi_done, 1)

        def split_lo_pool(e, k, src, slot, a, b):
            part = src[:, a:b]
            e.tensor_scalar(part, part, W_SCALE, 0.0, ALU.mult, ALU.add).then_inc(raw_scaled, 1)
            e.wait_ge(raw_scaled, k)
            if not isinstance(k, int):
                after_waits(e)
            e.tensor_tensor(wlo[:, slot, a:b], part, whi[:, slot, a:b], ALU.subtract).then_inc(lo_pool, 1)

        def split_lo(e, src, slot, a, b, done):
            e.scalar_tensor_tensor(out=wlo[:, slot, a:b], in0=src[:, a:b], scalar=W_SCALE,
                                   in1=whi[:, slot, a:b], op0=ALU.mult, op1=ALU.subtract).then_inc(done, 1)

        def mixer_split(e, u):
            slot, n = u % RING, unit_cols(u)
            if u >= RING:
                wait_mix_unit_used(e, u - RING)
            if e is act_engine[0]:
                e.wait_ge(raw_full[slot], 16 * (u // RING + 1))
                split_hi(e, raw_slots[slot], slot, n)
            else:
                e.wait_ge(hi_done, u + 1)
                cut = DVE_SPLIT * n // UNIT
                if e is dve_engine[0]:
                    split_lo(e, raw_slots[slot], slot, 0, cut, lo_dve)
                else:
                    split_lo_pool(e, u + 1, raw_slots[slot], slot, cut, n)

        act_engine, dve_engine, pool_engine = [None], [None], [None]

        def all_stored(e, slots):
            for s, done in enumerate(slots):
                e.wait_ge(done, 16 * len(range(s, T, len(slots))))

        def after_waits(e):
            e.sem_inc(step_pool if e is pool_engine[0] else step_dve, 1)

        def item_hi(e, i, v):
            e.wait_ge(used, i * ITEM_UNITS + (v - 2))
            local = v % ITEM_UNITS
            slot = RAW_SLOT[local]
            before, each = (0 if slot >= RING else MIX_UNITS // RING), RAW_SLOT.count(slot)
            nth = before + v // ITEM_UNITS * each + RAW_SLOT[:local + 1].count(slot)
            e.wait_ge(raw_full[slot], i * (16 * each) + 16 * nth)
            split_hi(e, raw_slots[slot], v % RING, UNIT)

        def item_lo_dve(e, i, v):
            e.wait_ge(hi_done, i * ITEM_UNITS + (MIX_UNITS + v + 1))
            split_lo(e, raw_slots[RAW_SLOT[v % ITEM_UNITS]], v % RING, 0, DVE_SPLIT, lo_dve)

        def item_lo_pool(e, i, v):
            e.wait_ge(hi_done, i * ITEM_UNITS + (MIX_UNITS + v + 1))
            after_waits(e)
            split_lo_pool(e, i * ITEM_UNITS + (MIX_UNITS + v + 1), raw_slots[RAW_SLOT[v % ITEM_UNITS]], v % RING, DVE_SPLIT, UNIT)

        DCH0 = 8
        CLIPPED, MADE, SPLIT = (4, 11, 19, 27), (7, 15, 23, 31), (12, 20, 28, 32)

        items_flat = items.rearrange("p a b -> p (a b)")
        N_CONST_DMAS = 16 * 4


        @block.sync
        def _(e):

            def load_unit(u):
                slot = u % RING
                if u >= RING:
                    wait_split(e, u - RING)
                if u == 3:
                    e.dma_start(raw[:, slot, 0:KV_UNIT], w_kv).then_inc(raw_full[slot], 16)
                else:
                    e.dma_start(raw[:, slot, :], w_units[u - (u > 3)]).then_inc(raw_full[slot], 16)

            for t in range(T):
                if t >= XR:
                    e.wait_ge(x_nd, t - XR + 1)
                e.dma_start(x_in[:, t % XR, :], x[t * P:(t + 1) * P, :]).then_inc(xin[t % XR], 16)
                if t == 0:
                    e.dma_start(g_mix, rows[0]).then_inc(g_in, 16)
                    e.dma_start(cs_all, consts[:, 0:CONSTS["band"][0]]).then_inc(id_in, 16)
            load_unit(0)
            e.dma_start(pr, params).then_inc(c_in, 16)
            e.dma_start(band_f, consts[:, slice(*CONSTS["band"])]).then_inc(c_in, 16)
            e.dma_start(bv_sb, b_v).then_inc(c_in, 16)
            e.dma_start(br_sb, b_router).then_inc(c_in, 16)
            load_unit(1)
            load_unit(2)
            e.dma_start(table, table0).then_inc(init, 16)
            e.dma_start(h_rows[SEQ:SEQ + SPARE, :], zeros).then_inc(init, 16)
            e.dma_start(y_rows[SEQ:SEQ + SPARE, :], zeros).then_inc(init, 16)
            for u in range(3, 8):
                load_unit(u)
            e.wait_ge(ot_pe, 2 * T)
            e.dma_start(b_out, rows[1]).then_inc(rows_in, 16)
            e.dma_start(g_ffn, rows[2]).then_inc(rows_in, 16)

            def load_residual(t):
                if t >= XR:
                    e.wait_ge(acc_st[t % XR], 16 * (t // XR))
                e.dma_start(xr[:, t % XR, :], x[t * P:(t + 1) * P, :]).then_inc(xr_s[t % XR], 16)

            load_residual(0)
            load_residual(1)
            e.wait_ge(ms_pe, 4)
            e.dma_start(b2_sb[0:NE, :], b2).then_inc(r_in, 16)
            e.dma_start(wr, w_router).then_inc(r_in, 16)
            e.wait_ge(mhi_a, 4 * CT)
            e.wait_ge(mlo_p, 4 * CT)
            e.dma_start(b1_sb.rearrange("p a b -> p (a b)"), b1).then_inc(b1_in, 16)
            def first_item(v):
                if RAW_SLOT[v] < RING:
                    for s in (hi_done, lo_dve, lo_pool):
                        e.wait_ge(s, MIX_UNITS + v + 1 - RAW_BACK[v])
                e.dma_start(raw_slots[RAW_SLOT[v]], w_units[MIX_UNITS - 1 + v]).then_inc(raw_full[RAW_SLOT[v]], 16)

            for t in range(T + 3):
                if t + 2 < T:
                    load_residual(t + 2)
                if 1 <= t <= T:
                    e.wait_ge(hl_d, t)
                    e.dma_start(h_rows[(t - 1) * P:t * P, :], h_pair_f[:, (t - 1) % 2, :]).then_inc(h_st[(t - 1) % 2], 16)
                if t == T + 2:
                    e.wait_ge(scat, 16 * TOPK * T)
                    src = table.rearrange("(x s p) w -> p x s w", p=P, s=SEQ // P)
                    for blk in range(2):
                        e.dma_start(idx_all[:, 0:NE, blk, :], src[:, :, blk, :]).then_inc(idx_in, 16)
                    e.wait_ge(items_ready, 1)
                    last_item = e.value_load(items_flat[0:1, W_LAST:W_LAST + 1], min_val=NE - 1, max_val=ITEMS - 1)
                    with e.If(last_item > NE - 1):
                        for k in range(NE, ITEMS):
                            row = e.value_load(items_flat[0:1, ITEMS + k:ITEMS + k + 1], min_val=0, max_val=(NE - 1) * SEQ + 3 * ITEM_ROWS)
                            src = table[bass.ds(row, ITEM_ROWS), :].rearrange("(b p) w -> p b w", p=P)
                            e.dma_start(idx_all[:, k, :, :], src).then_inc(idx_in, 16)
                        e.wait_ge(idx_in, 32 + 16 * EXTRA)
                        e.sem_inc(lists_ready, 1)
                    with e.Else():
                        e.wait_ge(idx_in, 32)
                        e.sem_inc(lists_ready, 1)
                if t == T:
                    first_item(2)
                if t == T + 1:
                    for s in range(2, XR):
                        e.wait_ge(acc_st[s], 16)
                    first_item(3)
                if t >= 3:
                    e.wait_ge(acc_d, 2 * (t - 2))
                    e.dma_start(y_rows[(t - 3) * P:(t - 2) * P, :], xr[:, (t - 3) % XR, :]).then_inc(acc_st[(t - 3) % XR], 16)

            def item_weights(i, expert, first=0):
                for v in range(first, ITEM_UNITS):
                    for s in (hi_done, lo_dve, lo_pool):
                        e.wait_ge(s, i * ITEM_UNITS + (MIX_UNITS + v + 1 - RAW_BACK[v]))
                    src = w_units[bass.ds(expert * ITEM_UNITS + (MIX_UNITS - 1 + v), 1)].rearrange("a p n -> p (a n)")
                    e.dma_start(raw_slots[RAW_SLOT[v]], src).then_inc(raw_full[RAW_SLOT[v]], 16)

            e.wait_ge(gb_pe, 2 * T)
            e.wait_ge(hl_d, T)
            e.wait_ge(rt_pe, T)
            for blk in range(2):
                e.wait_ge(xg_in[blk], 16)
            first_item(4)
            first_item(5)
            with e.Fori(1, NE) as i:
                item_weights(i, i)
            e.wait_ge(items_ready, 1)
            last_item = e.value_load(items_flat[0:1, W_LAST:W_LAST + 1], min_val=NE - 1, max_val=ITEMS - 1)
            with e.If(last_item > NE - 1):
                with e.Fori(NE, last_item + 1) as i:
                    expert = e.value_load(items_flat[0:1, bass.ds(i, 1)], min_val=0, max_val=NE - 1)
                    item_weights(i, expert)
            e.nop()
            for s in (hi_done, lo_dve, lo_pool):
                e.wait_ge(s, last_item * ITEM_UNITS + (MIX_UNITS + ITEM_UNITS))
            e.dma_start(g_final, rows[3]).then_inc(gf_in, 16)
            e.wait_ge(ysc[0], last_item * 16 + 32)
            e.wait_ge(ysc[1], last_item * 16 + 32)
            for t in range(T):
                e.dma_start(fin[:, t, :], y_rows[t * P:(t + 1) * P, :]).then_inc(f_in[t], 16)
            for t in range(T):
                e.wait_ge(f_d, t + 1)
                e.dma_start(out[t * P:(t + 1) * P, :], fin[:, t, :]).then_inc(f_st, 16)
            e.wait_ge(f_st, 16 * T)

        @block.tensor
        def _(e):
            def product(out_ap, l_hi, l_lo, r_hi, r_lo, start, stop):
                e.matmul(out_ap, l_hi, r_hi, start=start, stop=False)
                e.matmul(out_ap, l_hi, r_lo, start=False, stop=False)
                return e.matmul(out_ap, l_lo, r_hi, start=False, stop=stop)

            e.wait_ge(id_in, 16)
            for t in range(T):
                e.wait_ge(x_nd, t + 1)
                if t >= 2:
                    e.wait_ge(u_ld, t - 1)
                for k in range(KC):
                    last = e.transpose(ps[:, 2 * (t % 2) + k // 4, (k % 4) * P:(k % 4 + 1) * P],
                                       xn[:, t % 2, k * P:(k + 1) * P], cs["ident"])
                last.then_inc(x_tr, 1)
            n = 0
            for u in range(4):
                slot = u % RING
                wait_split(e, u)
                for tile in range(4 if u < 3 else 1):
                    for half in range(2):
                        e.wait_ge(u_ld, 4 * (half + 1))
                        if n >= 4:
                            e.wait_ge(*proj_reader(n - 4))
                        wide = HALF if u < 3 else 256
                        for k in range(KC):
                            at = k * wide + tile * P
                            toks = slice(half * HALF, (half + 1) * HALF)
                            last = product(ps[:, 4 + n % 4, :], whi[:, slot, at:at + P], wlo[:, slot, at:at + P],
                                           u_hi[:, k, toks], u_lo[:, k, toks], k == 0, k == KC - 1)
                        last.then_inc(proj, 1)
                        n += 1
            for quad in range(2):
                e.wait_ge(*proj_reader(n - 4))
                for tt in range(4):
                    t = quad * 4 + tt
                    for k in range(KC):
                        at = k * 256 + P
                        toks = slice(t * P, (t + 1) * P)
                        last = product(ps[:, 4 + n % 4, tt * P:(tt + 1) * P], u_hi[:, k, toks], u_lo[:, k, toks],
                                       whi[:, 0, at:at + P], wlo[:, 0, at:at + P], k == 0, k == KC - 1)
                last.then_inc(proj, 1)
                n += 1

            def channel_mean(bank, src, done):
                for j in range(CT):
                    last = e.matmul(ps[:, bank, :], mean_w, src[:, j, :], start=(j == 0), stop=(j == CT - 1))
                last.then_inc(done, 1)

            def scores(n):
                b, g = n // KV, n % KV
                if n < 2:
                    e.wait_ge(ev_a, 18)
                else:
                    e.wait_ge(exp_a, 5 * (n - 1))
                lo = 0 if b else P
                part = slice(g * HD, (g + 1) * HD)
                for j in range(GROUP):
                    dst = ps[:, 2 * (n % 2) + j // 2, (j % 2) * 2 * P + lo:(j % 2 + 1) * 2 * P]
                    e.matmul(dst, q_t[part, j, b * P:(b + 1) * P], k_t[part, (b - 1) * P + lo:(b + 1) * P],
                             start=True, stop=False)
                    last = e.matmul(dst, ident_b, band_b[:, lo:2 * P], start=False, stop=True)
                last.then_inc(sc_pe, 1)

            def probs_t(n):
                b = n // KV
                e.wait_ge(pn_p, 4 * (n + 1))
                if n >= 1:
                    e.wait_ge(pta, n)
                    e.wait_ge(ptd, n)
                for kb in range(0 if b else 1, 2):
                    for j in range(GROUP):
                        last = e.transpose(ps[:, 4 + kb, j * P:(j + 1) * P],
                                           prob[:, n % 2, j, kb * P:(kb + 1) * P], cs["ident"])
                last.then_inc(pt_pe, 1)

            def heads_t(n):
                b, g = n // KV, n % KV
                e.wait_ge(pta, n + 1)
                e.wait_ge(ptd, n + 1)
                if n == 0:
                    e.wait_ge(ve_d, 2)
                else:
                    e.wait_ge(og_a, n)
                first = 0 if b else 1
                for kb in range(first, 2):
                    last = e.matmul(ps[g * HD:(g + 1) * HD, 6, :], v_sb[:, b - 1 + kb, g * HD:(g + 1) * HD],
                                    prob_t[:, kb, :], start=(kb == first), stop=(kb == 1))
                last.then_inc(ot_pe, 1)

            e.wait_ge(tap_d, CT * TAPS)
            e.wait_ge(tap_p, CT * TAPS)
            e.wait_ge(ev_d, 10)
            for h in range(2):
                channel_mean(7 - h, conv[:, :, h * HALF:(h + 1) * HALF], mean_pe)
            scores(0)
            scores(1)
            for h in range(2):
                e.wait_ge(vsq_a, CT * (h + 1))
                channel_mean(7 - h, sq, var_pe)

            def branch_meansq(i):
                e.wait_ge(csq_a, CT * (i + 1))
                e.wait_ge(*((ve_d, 1) if i == 0 else (mse_d, i)))
                channel_mean(7, sq, ms_pe)

            for n in range(2 * T):
                probs_t(n)
                if n + 2 < 2 * T:
                    scores(n + 2)
                heads_t(n)
                if n in (2, 5, 9):
                    branch_meansq((2, 5, 9).index(n))

            def out_half(t, half):
                slot = (4 + half) % RING
                if t == 0:
                    wait_split(e, 4 + half)
                    e.wait_ge(mlo_p, 3 * CT)
                    e.wait_ge(exp_a, 5 * 2 * T)
                if t == T // 2:
                    e.wait_ge(mlo_p, 4 * CT)
                if t >= 2 and half == 0:
                    e.wait_ge(x2_d, t - 1)
                toks = slice(t * P, (t + 1) * P)
                for c in range(2 * CT):
                    at = c * HALF
                    last = product(ps[:, 2 * (t % 2) + half, :], mix_hi[:, c, toks], mix_lo[:, c, toks],
                                   whi[:, slot, at:at + HALF], wlo[:, slot, at:at + HALF], c == 0, c == 2 * CT - 1)
                last.then_inc(out_pe, 1)

            def parts_t(row_pair, bank):
                for part in range(2):
                    to = ps[:, bank + part, :].bitcast(F16)
                    for k in range(KC):
                        last = e.transpose(to[:, k * P:(k + 1) * P], row_pair[:, part * D + k * P:part * D + (k + 1) * P], ident_h)
                return last

            def h_t(t):
                e.wait_ge(hl_d, t + 1)
                if t == 0:
                    e.wait_ge(pta, 2 * T)
                    e.wait_ge(ptd, 2 * T)
                else:
                    e.wait_ge(htl, t)
                    e.wait_ge(hth, t)
                last = parts_t(h_pair[:, t % 2, :], 4)
                last.then_inc(tr_pe, 1)

            def router(t):
                e.wait_ge(htl, t + 1)
                e.wait_ge(hth, t + 1)
                if t == 0:
                    e.wait_ge(og_a, 2 * T)
                    e.wait_ge(b1_t, 1)
                else:
                    e.wait_ge(rc, t)
                for k in range(KC):
                    last = product(ps[:, 6, 0:NE], ht_hi[:, k, :], ht_lo[:, k, :], wr_hi[:, k, :], wr_lo[:, k, :],
                                   k == 0, k == KC - 1)
                last.then_inc(rt_pe, 1)

            def positions(t):
                e.wait_ge(ra, 11 * (t + 1))
                for s in range(t):
                    e.matmul(ps[:, 6, NE:2 * NE], ones_b, mb[:, s, :], start=(s == 0), stop=False)
                e.matmul(ps[:, 6, NE:2 * NE], before_b, mb[:, t, :], start=(t == 0), stop=True)
                e.transpose(ps[0:NE, 6, P:2 * P], gates_g, cs["ident"]).then_inc(gt_pe, 1)

            def gate_bias(t, half):
                e.wait_ge(rc, t + 1)
                if t == 0 and half == 0:
                    e.wait_ge(mse_d, 4)
                elif half or t:
                    e.wait_ge(acc_d, 2 * t + half)
                if t == T - 1 and half == 0:
                    e.wait_ge(items_ready, 1)
                e.matmul(ps[:, 7, :], gt_sb[0:NE, :], b2_sb[0:NE, half * HALF:(half + 1) * HALF],
                         start=True, stop=True).then_inc(gb_pe, 1)

            def count_items():
                e.wait_ge(rc, T)
                e.wait_ge(acc_d, 2 * (T - 1))
                for t in range(T):
                    last = e.matmul(ps[0:NE, 6, 2 * P:2 * P + 1], mb[:, t, :], ones_b[:, 0:1], start=(t == 0), stop=(t == T - 1))
                last.then_inc(cnt_pe, 1)
                e.wait_ge(it_d, 4)
                e.matmul(ps[0:NE, 6, 2 * P + 2:2 * P + 3], cs["before"][0:NE, 0:NE], xe[0:NE, :], start=True, stop=True).then_inc(st_pe, 1)
                e.wait_ge(it_d, 18)
                e.matmul(ps[0:1, 7, 0:4 * ITEMS], cs["ones"][0:NE, 0:1], itm[0:NE, :, :].rearrange("p a b -> p (a b)"),
                         start=True, stop=True).then_inc(row_pe, 1)

            for t in range(T + 3):
                if t == T + 2:
                    count_items()
                if t < T:
                    out_half(t, 0)
                if t == 0:
                    branch_meansq(3)
                if t == 1:
                    e.wait_ge(r_in, 32)
                if 2 <= t <= T + 1:
                    positions(t - 2)
                if 3 <= t:
                    gate_bias(t - 3, 0)
                if 1 <= t <= T:
                    h_t(t - 1)
                if t < T:
                    out_half(t, 1)
                if 3 <= t:
                    gate_bias(t - 3, 1)
                if 1 <= t <= T:
                    router(t - 1)

            def rows_t(block, banks):
                return parts_t(xg_pair[:, block, :], banks)

            def transpose_rows(i, n):
                e.wait_ge(xg_in[0], i * 16 + 32)
                e.wait_ge(xg_in[1], i * 16 + 32)
                e.wait_ge(dch, i * 32 + (DCH0 + CLIPPED[2]))
                with e.If(n > P):
                    rows_t(1, 0)
                rows_t(0, 6).then_inc(t_done, 1)

            def up(u, width):
                slot, pair = u % RING, 2 * (u % 2)
                for tile in range(4):
                    for k in range(KC):
                        at = k * HALF + tile * P
                        last = product(ps[:, pair + tile // 2, (tile % 2) * ITEM_ROWS:(tile % 2) * ITEM_ROWS + width],
                                       whi[:, slot, at:at + P], wlo[:, slot, at:at + P],
                                       xt_hi[:, k, 0:width], xt_lo[:, k, 0:width], k == 0, k == KC - 1)
                last.then_inc(used, 1)

            def all_up(i, width):
                for u in range(W1_UNITS):
                    e.wait_ge(lo_dve, i * ITEM_UNITS + (MIX_UNITS + u + 1))
                    e.wait_ge(lo_pool, i * ITEM_UNITS + (MIX_UNITS + u + 1))
                    if u >= 2:
                        e.wait_ge(dch, i * 32 + (DCH0 + CLIPPED[u - 2]))
                    up(u, width)

            def by_width(n, widths, body):
                if len(widths) == 1:
                    body(widths[0])
                    return
                mid = len(widths) // 2
                with e.If(n <= widths[mid - 1]):
                    by_width(n, widths[:mid], body)
                    e.nop()
                with e.Else():
                    by_width(n, widths[mid:], body)
                    e.nop()

            def down(half, blk, first, last_k):
                slot = (W1_UNITS + half) % RING
                for k in range(first, last_k):
                    at = k * HALF
                    toks = slice(blk * P, (blk + 1) * P)
                    last = product(ps[:, 4 + 2 * half + blk, :], act_hi[:, k, toks], act_lo[:, k, toks],
                                   whi[:, slot, at:at + HALF], wlo[:, slot, at:at + HALF], k == 0, k == KC - 1)
                return last

            def item(i, n_last):
                n = e.value_load(items_flat[0:1, bass.ds(i + 2 * ITEMS, 1)], min_val=0, max_val=ITEM_ROWS)
                e.wait_ge(xt_ready, i + 1)
                by_width(n, WIDTHS, lambda w: all_up(i, w))
                if not n_last:
                    n_next = e.value_load(items_flat[0:1, bass.ds(i + (2 * ITEMS + 1), 1)], min_val=0, max_val=ITEM_ROWS)
                    transpose_rows(i, n_next)
                for half in range(W2_UNITS):
                    e.wait_ge(lo_dve, i * ITEM_UNITS + (MIX_UNITS + W1_UNITS + half + 1))
                    e.wait_ge(lo_pool, i * ITEM_UNITS + (MIX_UNITS + W1_UNITS + half + 1))
                    if half == 0:
                        e.wait_ge(dch, i * 32 + (DCH0 + SPLIT[2]))
                    elif not n_last:
                        e.wait_ge(xt_ready, i + 2)
                    with e.If(n > P):
                        down(half, 1, 0, KC - 2)
                    down(half, 0, 0, KC - 2)
                    if half == 0:
                        e.wait_ge(dch, i * 32 + (DCH0 + SPLIT[3]))
                    with e.If(n > P):
                        down(half, 1, KC - 2, KC)
                    down(half, 0, KC - 2, KC).then_inc(used, 1)

            e.wait_ge(items_ready, 1)
            last_item = e.value_load(items_flat[0:1, W_LAST:W_LAST + 1], min_val=NE - 1, max_val=ITEMS - 1)
            e.wait_ge(xg_in[0], 16)
            e.wait_ge(xg_in[1], 16)
            e.wait_ge(dch, DCH0)
            rows_t(1, 0)
            rows_t(0, 4).then_inc(t_done, 1)
            with e.Fori(0, last_item) as i:
                item(i, False)
            item(last_item, True)

        @block.scalar
        def _(e):
            act_engine[0] = e
            for t in range(T + 1):
                if t < T:
                    e.wait_ge(xin[t % XR], 16 * (t // XR + 1))
                    if t >= 4:
                        e.wait_ge(x_sq, t - 3)
                    e.activation(conv[:, t % 4, :], x_in[:, t % XR, :], ACT.Square,
                                 accum_out=ss1[:, t:t + 1]).then_inc(x_sq, 1)
                if t >= 1:
                    e.wait_ge(x_tr, t)
                    src = ps[:, 2 * ((t - 1) % 2):2 * ((t - 1) % 2) + 2, :].rearrange("p a (k c) -> p (a k) c", c=P)
                    e.activation(u_hi[:, :, (t - 1) * P:t * P], src, ACT.Copy).then_inc(u_hd, 1)
            for u in range(3):
                mixer_split(e, u)
            products = [(c, k) for c in range(CT) for k in range(1, TAPS)]

            def tap_products(ms):
                for m in ms:
                    c, k = products[m]
                    if k == 1:
                        e.wait_ge(ev_d, 2 * c + 2)
                    if m == 0:
                        e.wait_ge(setup, 5)
                    if m >= PARTS:
                        before = products[m - PARTS]
                        e.wait_ge(tap_p, before[0] * TAPS + before[1] + 1)
                    e.activation(tap_part[:, m % PARTS, :], cu[c][:, DVE_TOKENS + k:SEQ + k], ACT.Copy,
                                 scale=par["w_dw"][:, c * TAPS + k:c * TAPS + k + 1]).then_inc(tap_m, 1)

            for n in range(26):
                e.wait_ge(proj, n + 1)
                bank = ps[:, 4 + n % 4, :]
                half = n % 2
                if n < 16 and n % 4 < 2:
                    gi = n // 4 * 2 + half
                    if gi >= 2:
                        e.wait_ge(ev_d, gi - 1)
                    e.activation(sg[:, gi % 2, :], bank, ACT.Sigmoid, scale=1.0 / Z_SCALE,
                                 bias=par["b_gate"][:, n // 4:n // 4 + 1]).then_inc(ev_a, 1)
                elif n >= 16:
                    j = n // 2 - 8
                    if n < 24:
                        e.activation(q_t[:, j, half * HALF:(half + 1) * HALF], bank, ACT.Identity, scale=1.0 / Z_SCALE,
                                     bias=par["b_q"][:, j:j + 1]).then_inc(ev_a, 1)
                    else:
                        e.activation(k_t[:, half * HALF:(half + 1) * HALF], bank, ACT.Identity, scale=1.0 / Z_SCALE,
                                     bias=par["b_k"]).then_inc(ev_a, 1)
                if n in (8, 16, 24):
                    mixer_split(e, (8, 16, 24).index(n) + 3)
                if n >= 4:
                    each = -(-len(products) // 22)
                    tap_products(range((n - 4) * each, min((n - 3) * each, len(products))))
            mixer_split(e, 6)

            def centred_squares(h):
                for j in range(CT):
                    e.wait_ge(sub_d, CT * h + j + 1)
                    if j == 0:
                        e.wait_ge(*((ev_d, 10) if h == 0 else (var_pe, h)))
                    e.activation(sq[:, j, :], conv[:, j, h * HALF:(h + 1) * HALF], ACT.Square).then_inc(vsq_a, 1)

            def exps(n):
                b = n // KV
                lo = 0 if b else P
                e.wait_ge(nm_d, n + 1)
                if n >= 2:
                    e.wait_ge(pt_pe, n - 1)
                    e.wait_ge(den_d, n - 1)
                for j in range(GROUP):
                    src = ps[:, 2 * (n % 2) + j // 2, (j % 2) * 2 * P + lo:(j % 2 + 1) * 2 * P]
                    e.activation(prob[:, n % 2, j, lo:2 * P], src, ACT.Exp, scale=SCORE_SCALE,
                                 bias=nm[:, n % 2, j:j + 1], accum_out=rsum[:, n % 2, j:j + 1]).then_inc(exp_a, 1)
                e.wait_ge(dsk_d, n + 1)
                e.activation(esum[:, n % 2, :], dsk[:, n % 2, :], ACT.Exp).then_inc(exp_a, 1)

            def root(h, k):
                e.wait_ge(*((ve_d, k) if k <= 2 else (mse_d, k - 2)))
                e.activation(rs[:, h, :], rs[:, h, :], ACT.Sqrt).then_inc(root_a, 1)

            def swish_sigmoid(h):
                for j in range(CT):
                    e.wait_ge(y_d, CT * h + j + 1)
                    if j == 0:
                        e.wait_ge(*((var_pe, 2) if h == 0 else (ms_pe, 1)))
                    e.activation(sq[:, j, :], conv[:, j, h * HALF:(h + 1) * HALF], ACT.Sigmoid,
                                 scale=par["ln_g"][:, j:j + 1], bias=par["ln_b"][:, j:j + 1]).then_inc(sgm_a, 1)

            def swish_squares(h):
                for j in range(CT):
                    e.wait_ge(s_d, CT * h + j + 1)
                    e.activation(sq[:, j, :], conv[:, j, h * HALF:(h + 1) * HALF], ACT.Square).then_inc(csq_a, 1)

            def head_squares(h):
                e.wait_ge(og_a, 8 * (h + 1))
                e.wait_ge(ms_pe, 2 + h)
                for j in range(CT):
                    e.activation(sq[:, j, :], heads[h][:, j, :], ACT.Square).then_inc(csq_a, 1)

            def mixed_hi(i):
                h = i % 2
                for j in range(CT):
                    src = conv[:, j, h * HALF:(h + 1) * HALF] if i < 2 else heads[h][:, j, :]
                    e.wait_ge(m_d, CT * i + j + 1)
                    e.activation(mix_hi[:, j + (CT if i < 2 else 0), h * HALF:(h + 1) * HALF], src, ACT.Copy).then_inc(mhi_a, 1)

            centred_squares(0)
            exps(0)
            centred_squares(1)
            exps(1)
            root(0, 1)
            root(1, 2)
            for n in range(2 * T):
                b, g = n // KV, n % KV
                e.wait_ge(pt_pe, n + 1)
                if n:
                    e.wait_ge(ot_pe, n)
                e.activation(prob_t[:, 1, :], ps[:, 5, :], ACT.Copy).then_inc(pta, 1)
                if n + 2 < 2 * T:
                    exps(n + 2)
                e.wait_ge(ot_pe, n + 1)
                if n == 0:
                    e.wait_ge(tap_d, CT * TAPS)
                    e.wait_ge(tap_p, CT * TAPS)
                if n == 8:
                    e.wait_ge(mlo_p, 2 * CT)
                e.activation(heads[b // 4][g * HD:(g + 1) * HD, :, (b % 4) * P:(b % 4 + 1) * P],
                             ps[g * HD:(g + 1) * HD, 6, :].rearrange("p (j c) -> p j c", j=GROUP),
                             ACT.Copy).then_inc(og_a, 1)
                if n in (0, 3):
                    swish_sigmoid(n // 3)
                if n in (1, 4):
                    swish_squares(n // 3)
                if n in (2, 5, 9):
                    i = (2, 5, 9).index(n)
                    root(i % 2, 3 + i)
                if n in (3, 6, 10):
                    mixed_hi((3, 6, 10).index(n))
                if n == 8:
                    head_squares(0)
            head_squares(1)
            root(1, 6)
            mixed_hi(3)

            def h_hi(t):
                e.wait_ge(tr_pe, t + 1)
                if t:
                    e.wait_ge(rt_pe, t)
                e.activation(ht_hi, chunks_of(4), ACT.Copy).then_inc(hth, 1)

            for t in range(T + 1):
                if t >= 1:
                    h_hi(t - 1)
                if t < T:
                    e.wait_ge(x2_d, t + 1)
                    if t >= 1:
                        e.wait_ge(hl_d, t)
                    e.activation(h_sb, xr[:, t % XR, :], ACT.Square, accum_out=ss2[:, t:t + 1]).then_inc(x2sq, 1)
                if t >= 1:
                    e.wait_ge(ra, 11 * (t - 1) + 5)
                    e.activation(ex, mx8[:, 0:TOPK], ACT.Exp, bias=nm0, accum_out=se).then_inc(ea, 1)
                if t < T:
                    e.wait_ge(h_d, t + 1)
                    if t >= 2:
                        e.wait_ge(tr_pe, t - 1)
                        e.wait_ge(h_st[t % 2], 16 * (t // 2))
                    e.activation(h_pair[:, t % 2, 0:D], h_sb, ACT.Copy).then_inc(hh_a, 1)
            mixer_split(e, 7)
            mixer_split(e, 8)

            def rows_hi(i):
                e.wait_ge(t_done, i + 1)
                e.activation(xt_hi[:, :, 0:P], chunks_of(6), ACT.Copy).then_inc(xt_hd, 1)

            def sigmoid(i, u):
                e.wait_ge(dch, i * 32 + (DCH0 + CLIPPED[u]))
                e.activation(sig, glu, ACT.Sigmoid, scale=ALPHA / Z_SCALE).then_inc(sig_a, 1)

            def act_high(i, u):
                e.wait_ge(dch, i * 32 + (DCH0 + MADE[u]))
                e.activation(act_hi[:, 2 * u:2 * u + 2, :], act, ACT.Copy).then_inc(ahi_a, 1)

            def item(i, n_last):
                for u in range(3):
                    sigmoid(i, u)
                    item_hi(e, i, u + 3)
                    act_high(i, u)
                sigmoid(i, 3)
                act_high(i, 3)
                if not n_last:
                    rows_hi(i + 1)
                    for v in (6, 7, 8):
                        item_hi(e, i, v)

            e.wait_ge(items_ready, 1)
            last_item = e.value_load(items_flat[0:1, W_LAST:W_LAST + 1], min_val=NE - 1, max_val=ITEMS - 1)
            e.wait_ge(t_done, 1)
            e.activation(xt_hi[:, :, 0:P], chunks_of(4), ACT.Copy).then_inc(xt_hd, 1)
            with e.Fori(0, last_item) as i:
                item(i, False)
            item(last_item, True)

            for t in range(T):
                e.wait_ge(f_in[t], 16)
                if t >= 2:
                    e.wait_ge(f_sq, t - 1)
                e.activation(xg[:, t % 2, :], fin[:, t, :], ACT.Square, accum_out=ss3[:, t:t + 1]).then_inc(f_sq, 1)

        @block.vector
        def _(e):
            dve_engine[0] = e
            for c in (0, 1):
                e.memset(cu[c][:, 0:TAPS - 1], 0.0).then_inc(setup_d, 1)

            def u_lo_part(t):
                e.wait_ge(u_hd, t + 1)
                src = ps[:, 2 * (t % 2):2 * (t % 2) + 2, :].rearrange("p a (k c) -> p (a k) c", c=P)
                e.tensor_tensor(u_lo[:, :, t * P:(t + 1) * P], src, u_hi[:, :, t * P:(t + 1) * P], ALU.subtract).then_inc(u_ld, 1)

            for t in range(T + 1):
                if t < T:
                    e.wait_ge(x_rs, t + 1)
                    if t >= 2:
                        e.wait_ge(x_tr, t - 1)
                    if t == 0:
                        e.wait_ge(setup, 1)
                    e.scalar_tensor_tensor(out=xn[:, t % 2, :], in0=x_in[:, t % XR, :], scalar=rs1[:, t:t + 1], in1=g_mix,
                                           op0=ALU.mult, op1=ALU.mult).then_inc(x_nd, 1)
                if t >= 1:
                    u_lo_part(t - 1)
            for u in range(3):
                mixer_split(e, u)

            e.wait_ge(x_sq, T)
            e.wait_ge(setup, 5)
            e.wait_ge(id_in, 16)
            e.tensor_copy(ident_h, cs["ident"]).then_inc(setup_d, 1)
            e.wait_ge(x_tr, T)
            for c in (2, 3):
                e.memset(cu[c][:, 0:TAPS - 1], 0.0).then_inc(setup_d, 1)
            e.wait_ge(setup_d, 5)

            def glu_tile(c):
                for half in range(2):
                    e.wait_ge(proj, 4 * c + 3 + half)
                    e.wait_ge(ev_a, 2 * c + half + 1)
                    e.scalar_tensor_tensor(out=cu[c][:, TAPS - 1 + half * HALF:TAPS - 1 + (half + 1) * HALF],
                                           in0=ps[:, 4 + (4 * c + 2 + half) % 4, :], scalar=par["b_a"][:, c:c + 1],
                                           in1=sg[:, half, :], op0=ALU.add, op1=ALU.mult).then_inc(ev_d, 1)
                e.wait_ge(ev_d, 2 * c + 2)

            def tap(c, k):
                dst, w = conv[:, c, 0:DVE_TOKENS], par["w_dw"][:, c * TAPS + k:c * TAPS + k + 1]
                src = cu[c][:, k:k + DVE_TOKENS]
                if k == 0:
                    ins = e.tensor_scalar(dst, src, w, par["b_dw"][:, c:c + 1], ALU.mult, ALU.add)
                else:
                    e.wait_ge(tap_d, c * TAPS + k)
                    ins = e.scalar_tensor_tensor(out=dst, in0=src, scalar=w, in1=dst, op0=ALU.mult, op1=ALU.add)
                ins.then_inc(tap_d, 1)

            for s in range(CT * TAPS):
                if s % GLU_EVERY == 0 and s // GLU_EVERY < CT:
                    glu_tile(s // GLU_EVERY)
                if s in (2 * GLU_EVERY + 8, 4 * GLU_EVERY):
                    mixer_split(e, 3 if s < 3 * GLU_EVERY else 4)
                tap(s // TAPS, s % TAPS)
            for quad in range(2):
                e.wait_ge(proj, 27 + quad)
                e.scalar_tensor_tensor(out=v_sb[:, quad * 4:quad * 4 + 4, :],
                                       in0=ps[:, 6 + quad, :].rearrange("p (a b) -> p a b", a=4), scalar=1.0 / Z_SCALE,
                                       in1=bv_sb.unsqueeze(1).to_broadcast([P, 4, P]), op0=ALU.mult, op1=ALU.add).then_inc(ev_d, 1)
            mixer_split(e, 5)

            def centre(h):
                e.wait_ge(mean_pe, h + 1)
                for j in range(CT):
                    c = conv[:, j, h * HALF:(h + 1) * HALF]
                    e.tensor_tensor(c, c, ps[:, 7 - h, :], ALU.subtract).then_inc(sub_d, 1)

            def row_max(n):
                b, g = n // KV, n % KV
                lo = 0 if b else P
                e.wait_ge(sc_pe, n + 1)
                src = ps[:, 2 * (n % 2):2 * (n % 2) + 2, :].rearrange("p a (j c) -> p (a j) c", j=2)
                if n >= 2:
                    e.wait_ge(exp_a, 5 * (n - 1))
                e.tensor_reduce(mxs[:, n % 2, :], src[:, :, lo:2 * P], AXX, ALU.max).then_inc(mx_d, 1)
                e.wait_ge(mx_d, n + 1)
                e.scalar_tensor_tensor(out=nm[:, n % 2, :], in0=mxs[:, n % 2, :], scalar=-SCORE_SCALE,
                                       in1=neg_sinks[:, g * GROUP:(g + 1) * GROUP], op0=ALU.mult, op1=ALU.min).then_inc(nm_d, 1)
                e.wait_ge(nm_d, n + 1)
                e.tensor_tensor(dsk[:, n % 2, :], nm[:, n % 2, :], par["sinks"][:, g * GROUP:(g + 1) * GROUP], ALU.add).then_inc(dsk_d, 1)

            def plus_eps(src_done, k, bank, h, done):
                e.wait_ge(src_done, k)
                e.tensor_scalar(rs[:, h, :], ps[:, bank, :], EPS, None, ALU.add).then_inc(done, 1)

            def inverse(h, k):
                e.wait_ge(root_a, k)
                e.reciprocal(rs[:, h, :], rs[:, h, :]).then_inc(rstd_d, 1)
                e.wait_ge(rstd_d, k)

            def ln_scale(h):
                for j in range(CT):
                    c = conv[:, j, h * HALF:(h + 1) * HALF]
                    e.tensor_tensor(c, c, rs[:, h, :], ALU.mult).then_inc(y_d, 1)

            def swish_product(h):
                for j in range(CT):
                    c = conv[:, j, h * HALF:(h + 1) * HALF]
                    e.wait_ge(z_p, CT * h + j + 1)
                    e.tensor_tensor(c, c, sq[:, j, :], ALU.mult).then_inc(s_d, 1)

            def branch_eps(i):
                plus_eps(ms_pe, i + 1, 7, i % 2, mse_d)

            def branch_norm(i):
                h = i % 2
                inverse(h, 3 + i)
                name = "g_conv" if i < 2 else "g_attn"
                for j in range(CT):
                    c = conv[:, j, h * HALF:(h + 1) * HALF] if i < 2 else heads[h][:, j, :]
                    e.scalar_tensor_tensor(out=c, in0=c, scalar=par[name][:, j:j + 1], in1=rs[:, h, :],
                                           op0=ALU.mult, op1=ALU.mult).then_inc(m_d, 1)

            centre(0)
            row_max(0)
            centre(1)
            row_max(1)
            for h in range(2):
                plus_eps(var_pe, h + 1, 7 - h, h, ve_d)
            for h in range(2):
                inverse(h, h + 1)
            def denominators(n):
                e.wait_ge(exp_a, 5 * (n + 1))
                if n >= 2:
                    e.wait_ge(pn_p, 4 * (n - 1))
                e.tensor_tensor(rden[:, n % 2, :], rsum[:, n % 2, :], esum[:, n % 2, :], ALU.add).then_inc(den_d, 1)
                e.wait_ge(den_d, n + 1)
                e.reciprocal(rden[:, n % 2, :], rden[:, n % 2, :]).then_inc(rden_d, 1)

            denominators(0)
            for n in range(2 * T):
                if n + 1 < 2 * T:
                    denominators(n + 1)
                e.wait_ge(pt_pe, n + 1)
                if n >= 1:
                    e.wait_ge(ot_pe, n)
                if n < 2:
                    e.memset(prob_t[:, 0, 0:2], 0.0).then_inc(ptd, 1)
                    e.wait_ge(ptd, n + 1)
                else:
                    e.tensor_copy(prob_t[:, 0, :], ps[:, 4, :]).then_inc(ptd, 1)
                if n + 2 < 2 * T:
                    row_max(n + 2)
                if n in (0, 1):
                    ln_scale(n)
                if n in (1, 4):
                    swish_product(n // 3)
                if n in (2, 5, 9):
                    branch_eps((2, 5, 9).index(n))
                if n in (3, 6, 10):
                    branch_norm((3, 6, 10).index(n))
                if n == 12:
                    mixer_split(e, 6)
            branch_eps(3)
            branch_norm(3)

            def residual(t):
                e.wait_ge(out_pe, 2 * (t + 1))
                e.wait_ge(xb_p, t + 1)
                c = xr[:, t % XR, :]
                e.scalar_tensor_tensor(out=c, in0=ps[:, 2 * (t % 2):2 * (t % 2) + 2, :].rearrange("p a b -> p (a b)"),
                                       scalar=1.0 / Z_SCALE, in1=c, op0=ALU.mult, op1=ALU.add).then_inc(x2_d, 1)

            def normed(t):
                e.wait_ge(rs2_p, t + 1)
                e.scalar_tensor_tensor(out=h_sb, in0=xr[:, t % XR, :], scalar=rs2[:, t:t + 1], in1=g_ffn,
                                       op0=ALU.mult, op1=ALU.mult).then_inc(h_d, 1)

            def h_low(t):
                e.wait_ge(tr_pe, t + 1)
                if t:
                    e.wait_ge(rt_pe, t)
                e.tensor_copy(ht_lo, chunks_of(5)).then_inc(htl, 1)

            def h_parts_low(t):
                e.wait_ge(hh_a, t + 1)
                pair = h_pair[:, t % 2, :]
                e.tensor_tensor(pair[:, D:2 * D], h_sb, pair[:, 0:D], ALU.subtract).then_inc(hl_d, 1)

            def route(t):
                k = 11 * t

                def step(ins, n):
                    ins.then_inc(ra, 1)
                    e.wait_ge(ra, k + n)
                e.wait_ge(rt_pe, t + 1)
                step(e.scalar_tensor_tensor(out=lg, in0=ps[:, 6, 0:NE], scalar=1.0 / Z_SCALE, in1=br_sb, op0=ALU.mult, op1=ALU.add), 1)
                step(e.max(mx8, lg), 2)
                step(e.max_index(ix8, mx8, lg), 3)
                step(e.tensor_copy(ixf, ix8[:, 0:TOPK]), 4)
                step(e.tensor_scalar(nm0, mx8[:, 0:1], -1.0, None, ALU.mult), 5)
                step(e.tensor_tensor(oh[:, t % 2, :, :], cs["iota"].unsqueeze(1).to_broadcast([P, TOPK, NE]),
                                     ixf.unsqueeze(2).to_broadcast([P, TOPK, NE]), ALU.is_equal), 6)
                with nc.allow_low_precision(reason="zeros and ones"):
                    step(e.tensor_reduce(mb[:, t, :], oh[:, t % 2, :, :].rearrange("p k e -> p e k"), AXX, ALU.add), 7)

            def route_gates(t):
                k = 11 * t

                def step(ins, n):
                    ins.then_inc(ra, 1)
                    e.wait_ge(ra, k + n)
                e.wait_ge(ea, t + 1)
                step(e.reciprocal(rse, se), 8)
                gates = pay[:, t, :].rearrange("p (k w) -> p k w", w=2)[:, :, 1].bitcast(F32)
                step(e.tensor_scalar(gates, ex, rse, None, ALU.mult), 9)
                step(e.tensor_tensor(gk, oh[:, t % 2, :, :], gates.unsqueeze(2).to_broadcast([P, TOPK, NE]), ALU.mult), 10)
                if t:
                    e.wait_ge(gt_pe, t)
                step(e.tensor_reduce(gates_g, gk.rearrange("p k e -> p e k"), AXX, ALU.add), 11)

            def place(t):
                def step(ins, n):
                    ins.then_inc(rb, 1)
                    e.wait_ge(rb, 4 * t + n)
                e.wait_ge(gt_pe, t + 1)
                step(e.tensor_tensor(posb, ps[:, 6, NE:2 * NE], cs["base"], ALU.add), 1)
                step(e.tensor_tensor(gk, oh[:, t % 2, :, :], posb.unsqueeze(1).to_broadcast([P, TOPK, NE]), ALU.mult), 2)
                step(e.tensor_reduce(slf, gk, AXX, ALU.add), 3)
                step(e.tensor_copy(slots[:, t, :], slf), 4)
                if t:
                    e.wait_ge(gb_pe, 2 * t)
                e.tensor_copy(gt_sb[0:NE, :], ps[0:NE, 6, P:2 * P]).then_inc(rc, 1)

            def add_bias(t, half):
                e.wait_ge(gb_pe, 2 * t + half + 1)
                c = xr[:, t % XR, half * HALF:(half + 1) * HALF]
                e.tensor_tensor(c, c, ps[:, 7, :], ALU.add).then_inc(acc_d, 1)

            e.wait_ge(b1_t, 1)
            def make_items():
                def step(ins, n):
                    ins.then_inc(it_d, 1)
                    e.wait_ge(it_d, n)
                q = slice(0, NE)
                e.wait_ge(cnt_pe, 1)
                step(e.tensor_copy(cnt[q], ps[q, 6, 2 * P:2 * P + 1]), 1)
                step(e.tensor_scalar(xe[q], cnt[q], float(ITEM_ROWS), None, ALU.is_gt), 2)
                step(e.scalar_tensor_tensor(out=xe[q], in0=cnt[q], scalar=2.0 * ITEM_ROWS, in1=xe[q], op0=ALU.is_gt, op1=ALU.add), 3)
                step(e.scalar_tensor_tensor(out=xe[q], in0=cnt[q], scalar=3.0 * ITEM_ROWS, in1=xe[q], op0=ALU.is_gt, op1=ALU.add), 4)
                e.wait_ge(st_pe, 1)
                step(e.tensor_copy(st[q], ps[q, 6, 2 * P + 2:2 * P + 3]), 5)
                step(e.tensor_tensor(en[q], st[q], xe[q], ALU.add), 6)
                step(e.tensor_scalar(mt[q], cs["extra"][q], st[q], None, ALU.is_ge), 7)
                step(e.scalar_tensor_tensor(out=mt[q], in0=cs["extra"][q], scalar=en[q], in1=mt[q], op0=ALU.is_lt, op1=ALU.mult), 8)
                step(e.tensor_scalar(rr[q], cs["extra"][q], st[q], 1.0, ALU.subtract, ALU.add), 9)
                step(e.tensor_scalar(itm[q, 0, NE:ITEMS], mt[q], cs["e"][q], None, ALU.mult), 10)
                step(e.tensor_copy(itm[q, 0, 0:NE], cs["item_e"][q, 0:NE]), 11)
                step(e.tensor_scalar(t1[q], rr[q], float(ITEM_ROWS), cs["e_row"][q], ALU.mult, ALU.add), 12)
                step(e.tensor_tensor(itm[q, 1, NE:ITEMS], t1[q], mt[q], ALU.mult), 13)
                step(e.tensor_copy(itm[q, 1, 0:NE], cs["item_row"][q, 0:NE]), 14)
                step(e.tensor_scalar(t1[q], rr[q], -float(ITEM_ROWS), cnt[q], ALU.mult, ALU.add), 15)
                step(e.tensor_tensor(itm[q, 2, NE:ITEMS], t1[q], mt[q], ALU.mult), 16)
                step(e.tensor_scalar(itm[q, 2, 0:NE], cs["eye"][q], cnt[q], None, ALU.mult), 17)
                step(e.tensor_scalar(itm[q, 3, :], cs["item_e"][q], 0.0, xe[q], ALU.mult, ALU.add), 18)
                e.wait_ge(row_pe, 1)
                row = ps[0:1, 7, 0:4 * ITEMS]
                step(e.tensor_copy(items_flat[0:1, 0:2 * ITEMS], row[:, 0:2 * ITEMS]), 19)
                step(e.tensor_scalar(items_flat[0:1, 2 * ITEMS:3 * ITEMS], row[:, 2 * ITEMS:3 * ITEMS], float(ITEM_ROWS), None, ALU.min), 20)
                e.tensor_scalar(items_flat[0:1, 3 * ITEMS:4 * ITEMS], row[:, 3 * ITEMS:4 * ITEMS], float(NE - 1), None, ALU.add).then_inc(items_ready, 1)

            for t in range(T + 3):
                if t == T + 2:
                    make_items()
                    e.wait_ge(tr_pe, T)
                    all_stored(e, h_st)
                    for a in (act_lo, y_sb, glu, lin, act):
                        e.memset(a, 0.0).then_inc(dch, 1)
                if 3 <= t:
                    add_bias(t - 3, 0)
                if 1 <= t <= T:
                    h_low(t - 1)
                if 2 <= t <= T + 1:
                    place(t - 2)
                if 3 <= t:
                    add_bias(t - 3, 1)
                if t < T:
                    residual(t)
                if 1 <= t <= T:
                    route(t - 1)
                if t < T:
                    normed(t)
                if 1 <= t <= T:
                    route_gates(t - 1)
                if t < T:
                    h_parts_low(t)
                if t == T:
                    for a in (xt_hi, xt_lo, act_hi):
                        e.memset(a, 0.0).then_inc(dch, 1)

            mixer_split(e, 7)

            e.wait_ge(dch, DCH0)

            def rows_low(i, n, first=False):
                e.wait_ge(t_done, i + 1)
                if first:
                    e.tensor_copy(xt_hi[:, :, P:2 * P], chunks_of(0))
                    e.tensor_copy(xt_lo[:, :, P:2 * P], chunks_of(1))
                else:
                    after_waits(e)
                    with e.If(n > P):
                        e.tensor_copy(xt_hi[:, :, P:2 * P], chunks_of(0))
                        e.tensor_copy(xt_lo[:, :, P:2 * P], chunks_of(1))
                e.wait_ge(xt_hd, i + 1)
                e.tensor_copy(xt_lo[:, :, 0:P], chunks_of(5 if first else 7)).then_inc(xt_ready, 1)

            def clip(i, u, expert, w):
                e.wait_ge(used, i * ITEM_UNITS + (u + 1))
                e.wait_ge(dch, i * 32 + (DCH0 + (MADE[u - 1] if u else 0)))
                for p in range(2):
                    bank, j = 2 * (u % 2) + p, 2 * u + p
                    e.tensor_scalar(glu[:, p, 0:w], ps[:, bank, 0:w], g_top[:, j, bass.ds(expert, 1)],
                                    g_add[:, j, bass.ds(expert, 1)], ALU.min, ALU.add).then_inc(dch, 1)
                    e.tensor_scalar(lin[:, p, 0:w], ps[:, bank, ITEM_ROWS:ITEM_ROWS + w], l_top[:, j, bass.ds(expert, 1)],
                                    l_low[:, j, bass.ds(expert, 1)], ALU.min, ALU.max).then_inc(dch, 1)

            def make(i, u, expert, w):
                e.wait_ge(sig_a, i * 4 + (u + 1))
                e.scalar_tensor_tensor(out=gs[:, :, 0:w], in0=glu[:, :, 0:w], scalar=X_SCALE / Z_SCALE ** 2, in1=sig[:, :, 0:w],
                                       op0=ALU.mult, op1=ALU.mult).then_inc(dch, 1)
                e.wait_ge(dch, i * 32 + (DCH0 + MADE[u] - 2))
                for p in range(2):
                    e.scalar_tensor_tensor(out=act[:, p, 0:w], in0=lin[:, p, 0:w], scalar=l_add[:, 2 * u + p, bass.ds(expert, 1)],
                                           in1=gs[:, p, 0:w], op0=ALU.add, op1=ALU.mult).then_inc(dch, 1)

            def act_low(i, u, w):
                e.wait_ge(ahi_a, i * 4 + (u + 1))
                e.tensor_tensor(act_lo[:, 2 * u:2 * u + 2, 0:w], act[:, :, 0:w], act_hi[:, 2 * u:2 * u + 2, 0:w],
                                ALU.subtract).then_inc(dch, 1)

            def output(i, half, w):
                e.wait_ge(used, i * ITEM_UNITS + (W1_UNITS + half + 1))
                if half == 0:
                    e.wait_ge(ysc[0], i * 16 + 16)
                    e.wait_ge(ysc[1], i * 16 + 16)
                gate = [idx_all[:, bass.ds(i, 1), blk, 1].bitcast(F32) for blk in range(2)]
                for blk in reversed(range(w // P)):
                    last = e.tensor_scalar(y_sb[:, blk, half * HALF:(half + 1) * HALF], ps[:, 4 + 2 * half + blk, :], gate[blk],
                                           1.0 / Z_SCALE, ALU.mult, ALU.mult)
                last.then_inc(yd, 1)

            def item_of_width(i, expert, w, n_next):
                clip(i, 0, expert, w)
                item_lo_dve(e, i, 2)
                make(i, 0, expert, w)
                for u in (1, 2):
                    clip(i, u, expert, w)
                    act_low(i, u - 1, w)
                    item_lo_dve(e, i, u + 2)
                    make(i, u, expert, w)
                clip(i, 3, expert, w)
                act_low(i, 2, w)
                make(i, 3, expert, w)
                act_low(i, 3, w)
                if n_next is not None:
                    rows_low(i + 1, n_next)
                item_lo_dve(e, i, 5)
                for half in range(W2_UNITS):
                    output(i, half, w)
                    if n_next is not None:
                        item_lo_dve(e, i, 6 + half)

            def item(i, n_last):
                n = e.value_load(items_flat[0:1, bass.ds(i + 2 * ITEMS, 1)], min_val=0, max_val=ITEM_ROWS)
                expert = e.value_load(items_flat[0:1, bass.ds(i, 1)], min_val=0, max_val=NE - 1)
                n_next = None
                if not n_last:
                    n_next = e.value_load(items_flat[0:1, bass.ds(i + (2 * ITEMS + 1), 1)], min_val=0, max_val=ITEM_ROWS)
                with e.If(n > P):
                    item_of_width(i, expert, ITEM_ROWS, n_next)
                with e.Else():
                    item_of_width(i, expert, P, n_next)

            e.wait_ge(items_ready, 1)
            last_item = e.value_load(items_flat[0:1, W_LAST:W_LAST + 1], min_val=NE - 1, max_val=ITEMS - 1)
            rows_low(0, None, first=True)
            e.wait_ge(lists_ready, 1)
            with e.Fori(0, last_item) as i:
                item(i, False)
            item(last_item, True)

            e.wait_ge(gf_in, 16)
            for t in range(T):
                e.wait_ge(f_rs, t + 2)
                e.scalar_tensor_tensor(out=fin[:, t, :], in0=fin[:, t, :], scalar=rs3[:, t:t + 1], in1=g_final,
                                       op0=ALU.mult, op1=ALU.mult).then_inc(f_d, 1)

        @block.gpsimd
        def _(e):
            pool_engine[0] = e
            e.wait_ge(g_in, 16)
            e.tensor_scalar(g_mix, g_mix, OUT_SCALE, 0.0, ALU.mult, ALU.add).then_inc(setup, 1)
            e.wait_ge(id_in, 16)

            def rstd(dst, src, k):
                e.tensor_scalar(dst, src, D * EPS, 0.0, ALU.add, ALU.add).then_inc(eps_p, 1)
                e.wait_ge(eps_p, k)
                return e.tensor_tensor(dst, dst, cs["power"], ALU.pow)

            for t in range(T):
                e.wait_ge(x_sq, t + 1)
                if t == 0:
                    e.wait_ge(setup, 1)
                rstd(rs1[:, t:t + 1], ss1[:, t:t + 1], t + 1).then_inc(x_rs, 1)
            for u in range(3):
                mixer_split(e, u)
            e.wait_ge(c_in, N_CONST_DMAS)
            e.tensor_scalar(par["b_a"], par["b_a"], Z_SCALE, 0.0, ALU.mult, ALU.add).then_inc(setup, 1)
            e.tensor_scalar(par["w_dw"], par["w_dw"], 1.0 / Z_SCALE, 0.0, ALU.mult, ALU.add).then_inc(setup, 1)
            gains = pr[:, PARAMS["g_attn"][0]:PARAMS["g_conv"][1]]
            e.tensor_scalar(gains, gains, X_SCALE, 0.0, ALU.mult, ALU.add).then_inc(setup, 1)
            e.tensor_scalar(neg_sinks, par["sinks"], -1.0, 0.0, ALU.mult, ALU.add).then_inc(setup, 1)
            e.tensor_copy(ident_b, cs["ident"]).then_inc(setup, 1)
            e.tensor_copy(before_b, cs["before"]).then_inc(setup, 1)
            e.tensor_copy(ones_b, cs["ones"]).then_inc(setup, 1)
            e.tensor_copy(band_b, band_f).then_inc(setup, 1)
            e.tensor_scalar(mean_w, cs["ones"], 1.0 / CW, 0.0, ALU.mult, ALU.add).then_inc(setup, 1)
            tap_sums = conv[:, :, DVE_TOKENS:SEQ]
            for c in range(CT):
                e.wait_ge(ev_d, 2 * c + 2)
                if c == 0:
                    e.wait_ge(x_sq, T)
                    e.wait_ge(setup, 5)
                for k in range(TAPS):
                    src, w = cu[c][:, DVE_TOKENS + k:SEQ + k], par["w_dw"][:, c * TAPS + k:c * TAPS + k + 1]
                    if k == 0:
                        e.tensor_scalar(tap_sums[:, c, :], src, w, par["b_dw"][:, c:c + 1], ALU.mult, ALU.add).then_inc(tap_p, 1)
                        continue
                    m = c * (TAPS - 1) + k - 1
                    e.wait_ge(tap_m, m + 1)
                    e.wait_ge(tap_p, c * TAPS + k)
                    e.tensor_tensor(tap_sums[:, c, :], tap_sums[:, c, :], tap_part[:, m % PARTS, :], ALU.add).then_inc(tap_p, 1)
                if c in (1, 2):
                    mixer_split(e, 2 + c)
            mixer_split(e, 5)

            def affine(h):
                for j in range(CT):
                    c = conv[:, j, h * HALF:(h + 1) * HALF]
                    e.wait_ge(sgm_a, CT * h + j + 1)
                    e.tensor_scalar(c, c, par["ln_g"][:, j:j + 1], par["ln_b"][:, j:j + 1], ALU.mult, ALU.add).then_inc(z_p, 1)

            def mixed_lo(i):
                h = i % 2
                for j in range(CT):
                    src = conv[:, j, h * HALF:(h + 1) * HALF] if i < 2 else heads[h][:, j, :]
                    at = j + (CT if i < 2 else 0)
                    e.wait_ge(mhi_a, CT * i + j + 1)
                    e.tensor_tensor(mix_lo[:, at, h * HALF:(h + 1) * HALF], src, mix_hi[:, at, h * HALF:(h + 1) * HALF],
                                    ALU.subtract).then_inc(mlo_p, 1)

            for n in range(2 * T):
                lo = 0 if n // KV else P
                e.wait_ge(rden_d, n + 1)
                for j in range(GROUP):
                    pj = prob[:, n % 2, j, lo:2 * P]
                    e.tensor_scalar(pj, pj, rden[:, n % 2, j:j + 1], 0.0, ALU.mult, ALU.add).then_inc(pn_p, 1)
                if n in (1, 3):
                    affine(n // 2)
                if n in (4, 7, 11):
                    mixed_lo((4, 7, 11).index(n))
                if n == 13:
                    mixer_split(e, 6)

            def residual_bias(t):
                e.wait_ge(xr_s[t % XR], 16 * (t // XR + 1))
                c = xr[:, t % XR, :]
                e.tensor_tensor(c, c, b_out, ALU.add).then_inc(xb_p, 1)

            e.wait_ge(rows_in, 32)
            e.tensor_scalar(g_ffn, g_ffn, OUT_SCALE, 0.0, ALU.mult, ALU.add).then_inc(setup, 1)
            residual_bias(0)
            mixed_lo(3)
            e.wait_ge(r_in, 32)
            e.tensor_scalar(wr_hi.rearrange("p a b -> p (a b)"), wr, W_SCALE, 0.0, ALU.mult, ALU.add).then_inc(setup, 1)
            e.wait_ge(setup, 12)
            token = pay.rearrange("p t (k w) -> p t k w", w=2)
            e.tensor_copy(token[:, :, :, 0], cs["token"].unsqueeze(2).to_broadcast([P, T, TOPK])).then_inc(setup, 1)
            e.tensor_scalar(wr, wr, W_SCALE, 0.0, ALU.mult, ALU.add).then_inc(setup, 1)
            e.wait_ge(setup, 14)
            e.tensor_tensor(wr_lo.rearrange("p a b -> p (a b)"), wr, wr_hi.rearrange("p a b -> p (a b)"), ALU.subtract).then_inc(b1_t, 1)

            def store_slots(t):
                e.wait_ge(rb, 4 * (t + 1))
                if t == 0:
                    e.wait_ge(init, 48)
                for k in range(TOPK):
                    e.indirect_dma_start(table, bass.IndirectOffsetOnAxis(ap=slots[:, t, k:k + 1], axis=0),
                                         pay[:, t, 2 * k:2 * k + 2], None).then_inc(scat, 16)

            for t in range(T + 2):
                if t < T:
                    e.wait_ge(x2sq, t + 1)
                    rstd(rs2[:, t:t + 1], ss2[:, t:t + 1], T + t + 1).then_inc(rs2_p, 1)
                if t + 1 < T:
                    residual_bias(t + 1)
                if t == 1:
                    e.wait_ge(b1_in, 16)
                    bg, bl = b1_sb[:, 0:KC, :], b1_sb[:, KC:2 * KC, :]
                    e.tensor_scalar(g_top, bg, -Z_SCALE, LIMIT * Z_SCALE, ALU.mult, ALU.add).then_inc(b1_t, 1)
                    e.tensor_scalar(g_add, bg, Z_SCALE, 0.0, ALU.mult, ALU.add).then_inc(b1_t, 1)
                    e.tensor_scalar(l_top, bl, -Z_SCALE, LIMIT * Z_SCALE, ALU.mult, ALU.add).then_inc(b1_t, 1)
                    e.tensor_scalar(l_low, bl, -Z_SCALE, -LIMIT * Z_SCALE, ALU.mult, ALU.add).then_inc(b1_t, 1)
                    e.tensor_scalar(l_add, bl, Z_SCALE, Z_SCALE, ALU.mult, ALU.add).then_inc(b1_t, 1)
                if t >= 2:
                    store_slots(t - 2)

            mixer_split(e, 7)
            e.wait_ge(items_ready, 1)
            last_item = e.value_load(items_flat[0:1, W_LAST:W_LAST + 1], min_val=NE - 1, max_val=ITEMS - 1)
            e.wait_ge(lists_ready, 1)

            def gather(blk, rows=P):
                e.indirect_dma_start(xg[0:rows, blk, :], None, h_rows, bass.IndirectOffsetOnAxis(ap=idx_g[0:rows, blk, 0:1], axis=0)).then_inc(xg_in[blk], 16)

            def scatter(blk, rows=P):
                e.indirect_dma_start(y_rows, bass.IndirectOffsetOnAxis(ap=idx_s[0:rows, blk, 0:1], axis=0), y_sb[0:rows, blk, :], None,
                                     compute_op=ALU.add).then_inc(ysc[blk], 16)

            def fetch_rows(k, n=None):
                e.tensor_copy(idx_g.rearrange("p a b -> p (a b)"), idx_all[:, bass.ds(k, 1), :, :].rearrange("p a b w -> p (a b w)")).then_inc(ig, 1)
                e.wait_ge(ig, k + 1)
                after_waits(e)
                gather(0)
                if n is None:
                    gather(1)
                else:
                    with e.If(n > P):
                        gather(1)
                    with e.Else():
                        gather(1, FEW)

            def scatter_rows(i, n, k):
                e.wait_ge(ysc[0], k)
                e.wait_ge(ysc[1], k)
                after_waits(e)
                e.tensor_copy(idx_s.rearrange("p a b -> p (a b)"), idx_all[:, bass.ds(i, 1), :, :].rearrange("p a b w -> p (a b w)")).then_inc(is_, 1)
                e.wait_ge(is_, i + 2)
                e.wait_ge(yd, i * 2 + 2)
                after_waits(e)
                scatter(0)
                with e.If(n > P):
                    scatter(1)
                with e.Else():
                    scatter(1, FEW)

            def item(i, n_last):
                n = e.value_load(items_flat[0:1, bass.ds(i + 2 * ITEMS, 1)], min_val=0, max_val=ITEM_ROWS)
                if not n_last:
                    n_next = e.value_load(items_flat[0:1, bass.ds(i + (2 * ITEMS + 1), 1)], min_val=0, max_val=ITEM_ROWS)
                    e.wait_ge(t_done, i + 1)
                    after_waits(e)
                    fetch_rows(i + 1, n_next)
                for v in range(2, 6 if n_last else 8):
                    item_lo_pool(e, i, v)
                scatter_rows(i, n, i * 16 + 16)

            all_stored(e, h_st)
            e.wait_ge(out_pe, 2 * T)
            fetch_rows(0)
            all_stored(e, acc_st)
            e.tensor_copy(idx_s.rearrange("p a b -> p (a b)"), idx_all[:, 0, :, :].rearrange("p b w -> p (b w)")).then_inc(is_, 1)
            e.wait_ge(is_, 1)
            e.wait_ge(dch, DCH0)
            scatter(0, FEW)
            scatter(1, FEW)
            with e.Fori(0, last_item) as i:
                item(i, False)
            item(last_item, True)

            e.wait_ge(gf_in, 16)
            e.tensor_scalar(g_final, g_final, D ** 0.5, 0.0, ALU.mult, ALU.add).then_inc(f_rs, 1)
            for t in range(T):
                e.wait_ge(f_sq, t + 1)
                rstd(rs3[:, t:t + 1], ss3[:, t:t + 1], 2 * T + t + 1).then_inc(f_rs, 1)


def _constants(np):
    c = np.zeros((P, N_CONSTS), np.float32)

    def put(name, a):
        lo, hi = CONSTS[name]
        c[:a.shape[0], lo:hi] = a
    r = np.arange(P)
    put("ident", np.eye(P))
    put("before", r[:, None] < r[None, :])
    put("ones", np.ones((P, P)))
    ahead = np.arange(2 * P)[None, :] - r[:, None]
    put("band", np.where((ahead >= 1) & (ahead <= P), 0.0, -1e30))
    put("iota", np.tile(np.arange(NE), (P, 1)))
    put("base", np.tile(np.arange(NE) * SEQ, (P, 1)))
    put("token", r[:, None] + P * np.arange(T)[None, :])
    ne = np.arange(NE)
    e_of = np.zeros((NE, ITEMS))
    e_of[ne, ne] = ne
    put("item_e", e_of)
    put("item_row", e_of * SEQ)
    put("eye", np.eye(NE))
    put("extra", np.tile(np.arange(EXTRA), (P, 1)))
    put("power", np.full((P, 1), -0.5))
    put("e", ne[:, None])
    put("e_row", ne[:, None] * SEQ)
    slot = np.arange(NE * SEQ)
    table = np.stack([SEQ + slot % SPARE, 0 * slot], axis=1).astype(np.uint32)
    return c, table


def kernel(**inputs):
    import numpy as np
    import concourse.bacc as bacc
    from concourse.bass_utils import run_bass_kernel_spmd as run

    a = {k: np.asarray(v) for k, v in inputs.items()}
    w_in, w_out, w1, w2 = a["w_in"][0], a["w_out"][0], a["w1"][0], a["w2"][0]
    att, kvw = HEADS * HD, KV * HD

    def chunks(w):
        return w.reshape(w.shape[0] // P, P, w.shape[1]).transpose(1, 0, 2)

    order = np.arange(att).reshape(KV, GROUP, HD).transpose(1, 0, 2).reshape(-1)
    conv_a, gate = w_in[:, att + 2 * kvw:att + 2 * kvw + CW], w_in[:, att + 2 * kvw + CW:]
    glu_cols = [np.concatenate([m[:, c * P:(c + 1) * P] for c in (2 * i, 2 * i + 1) for m in (gate, conv_a)], axis=1) for i in range(2)]
    q_cols = w_in[:, :att][:, order]
    wo = np.concatenate([w_out[:att][order], w_out[att:]], axis=0)
    units = [chunks(m) for m in (glu_cols[0], glu_cols[1], q_cols, wo[:, :HALF], wo[:, HALF:])]
    up = w1.reshape(NE, KC, P, W1_UNITS, 2, P, 2).transpose(0, 3, 2, 1, 4, 6, 5).reshape(NE, W1_UNITS, P, UNIT)
    down = w2.reshape(NE, KC, P, W2_UNITS, HALF).transpose(0, 3, 2, 1, 4).reshape(NE, W2_UNITS, P, UNIT)
    experts = np.concatenate([up, down], axis=1).reshape(NE * ITEM_UNITS, P, UNIT)
    w_units = np.concatenate([np.stack([u.reshape(P, UNIT) for u in units]), experts], axis=0)
    w_kv = np.ascontiguousarray(chunks(w_in[:, att:att + 2 * kvw]).reshape(P, KV_UNIT))

    def cols(v):
        return v.reshape(-1, P).T
    b_in = a["b_in"][0]
    b_conv, b_gate = b_in[att + 2 * kvw:att + 2 * kvw + CW], b_in[att + 2 * kvw + CW:]
    params = np.concatenate([
        cols(b_gate), cols(b_conv), cols(b_in[:att][order]), cols(b_in[att:att + kvw]),
        a["w_dw"][0].reshape(TAPS, CT, P).transpose(2, 1, 0).reshape(P, CT * TAPS), cols(a["b_dw"][0]),
        cols(a["ln_g"][0]), cols(a["ln_b"][0]), cols(a["g_attn_out"][0][order]), cols(a["g_conv_out"][0]),
        np.broadcast_to(a["sinks"][0], (P, HEADS))], axis=1)
    rows = np.stack([np.broadcast_to(v, (P, D)) for v in (a["g_mix"][0], a["b_out"][0], a["g_ffn"][0], a["g_final"])])
    b1 = a["b1"][0].reshape(NE, KC, P, 2).transpose(2, 3, 1, 0).reshape(P, 2 * KC * NE)
    w_router = chunks(a["w_router"][0]).reshape(P, KC * NE)
    consts, table0 = _constants(np)
    arrays = {
        "x": a["x"][0], "w_units": w_units, "w_kv": w_kv, "params": params, "rows": rows,
        "b_v": np.broadcast_to(b_in[att + kvw:att + 2 * kvw], (P, P)), "b_router": np.broadcast_to(a["b_router"][0], (P, NE)),
        "w_router": w_router, "b1": b1, "b2": a["b2"][0], "consts": consts, "table0": table0,
        "zeros": np.zeros((SPARE, D), np.float32),
    }
    arrays = {f"in_{k}": np.ascontiguousarray(v) for k, v in arrays.items()}
    nc = bacc.Bacc("TRN2", target_bir_lowering=False, num_devices=1)
    args = [nc.dram_tensor(k, v.shape, mybir.dt.from_np(v.dtype), kind="ExternalInput").ap() for k, v in arrays.items()]
    out = nc.dram_tensor("out", (SEQ, D), F32, kind="ExternalOutput").ap()
    hymba_layer_kernel(nc, *args, out)
    r = run(nc, [arrays], core_ids=[0])
    return r.results[0]["out"].reshape(1, SEQ, D)
```
